# Optimizing a Trainium2 kernel written in Bass

```python
import math
import jax
import jax.numpy as jnp
from jax import lax
import numpy as np

D_MODEL = 1024
BATCH = 1
SEQ = 256
DEPTH = 1

GRID_W = 64
CTX_LEN = 256
S5_WIDTH = 512
S5_GROUP = 16
S5_GROUPS = S5_WIDTH // S5_GROUP
S5_STATE = 64
SGU_WIDTH = 512
SGU_GROUPS = 8
SGU_GROUP_DIM = SGU_WIDTH // SGU_GROUPS
CHUNK = 128
FFN_HIDDEN = 2816
CONV_K = 3
N_BRANCH = 2
IN_WIDTH = S5_WIDTH + 2 * SGU_WIDTH + N_BRANCH * D_MODEL
N_MOD = 6
EPS = 1e-6
DT_MIN = 1e-3
DT_MAX = 1e-1

kernel_name = 'hybrid_s5_sgu_convffn_block'

def rms_norm(x, g):
    x32 = x.astype(jnp.float32)
    y = x32 * lax.rsqrt(jnp.mean(x32 * x32, axis=-1, keepdims=True) + EPS)
    return y.astype(x.dtype) * g

def layer_norm(x, g, b):
    x32 = x.astype(jnp.float32)
    xc = x32 - jnp.mean(x32, axis=-1, keepdims=True)
    y = xc * lax.rsqrt(jnp.mean(xc * xc, axis=-1, keepdims=True) + EPS)
    return y.astype(x.dtype) * g + b

def modulate(x, g, shift, scale):
    return rms_norm(x, g) * (1 + scale) + shift

def s5_discretize(a_re, a_im, log_step, b_re, b_im):
    f32 = jnp.float32
    a_re = a_re.astype(f32)
    a_im = a_im.astype(f32)
    dt = jnp.exp(log_step.astype(f32))[:, None]
    mag = jnp.exp(a_re * dt)
    ab_re = mag * jnp.cos(a_im * dt)
    ab_im = mag * jnp.sin(a_im * dt)
    p = ab_re - 1.0
    q = ab_im
    den = a_re * a_re + a_im * a_im
    k_re = ((p * a_re + q * a_im) / den)[..., None]
    k_im = ((q * a_re - p * a_im) / den)[..., None]
    b_re = b_re.astype(f32)
    b_im = b_im.astype(f32)
    bb_re = k_re * b_re - k_im * b_im
    bb_im = k_re * b_im + k_im * b_re
    return ab_re, ab_im, bb_re, bb_im

def _linear_recurrence_combine(e1, e2):
    a1r, a1i, b1r, b1i = e1
    a2r, a2i, b2r, b2i = e2
    return (a2r * a1r - a2i * a1i,
            a2r * a1i + a2i * a1r,
            a2r * b1r - a2i * b1i + b2r,
            a2r * b1i + a2i * b1r + b2i)

def s5_scan(u, ab_re, ab_im, bb_re, bb_im, s0=None):
    bsz, length, _ = u.shape
    ug = u.astype(jnp.float32).reshape(bsz, length, S5_GROUPS, S5_GROUP)
    bu_re = jnp.einsum('blgh,gnh->blgn', ug, bb_re)
    bu_im = jnp.einsum('blgh,gnh->blgn', ug, bb_im)
    if s0 is not None:
        s0_re, s0_im = s0
        bu_re = bu_re.at[:, 0].add(ab_re * s0_re - ab_im * s0_im)
        bu_im = bu_im.at[:, 0].add(ab_re * s0_im + ab_im * s0_re)
    a_re = jnp.broadcast_to(ab_re, (1, length) + ab_re.shape)
    a_im = jnp.broadcast_to(ab_im, (1, length) + ab_im.shape)
    _, _, h_re, h_im = lax.associative_scan(
        _linear_recurrence_combine, (a_re, a_im, bu_re, bu_im), axis=1)
    return h_re, h_im

def s5_readout(h_re, h_im, c_re, c_im):
    y = (jnp.einsum('blgn,ghn->blgh', h_re, c_re.astype(jnp.float32))
         - jnp.einsum('blgn,ghn->blgh', h_im, c_im.astype(jnp.float32)))
    return y.reshape(y.shape[0], y.shape[1], S5_WIDTH)

def s5_glu(y, w, b):
    y = jax.nn.gelu(y)
    return y * jax.nn.sigmoid(y @ w + b)

def s5_mixer(u, u_ctx, a_re, a_im, log_step, b_re, b_im, c_re, c_im, d_skip, w_glu, b_glu, with_ctx_out):
    f32 = jnp.float32
    y = u.astype(f32) * d_skip.astype(f32)
    y_ctx = u_ctx.astype(f32) * d_skip.astype(f32) if with_ctx_out else None
    for direction in range(2):
        ab_re, ab_im, bb_re, bb_im = s5_discretize(
            a_re[direction], a_im[direction], log_step[direction], b_re[direction], b_im[direction])
        orient = (lambda t: jnp.flip(t, axis=1)) if direction == 1 else (lambda t: t)
        hc_re, hc_im = s5_scan(orient(u_ctx), ab_re, ab_im, bb_re, bb_im)
        h_re, h_im = s5_scan(orient(u), ab_re, ab_im, bb_re, bb_im,
                             s0=(hc_re[:, -1], hc_im[:, -1]))
        y = y + orient(s5_readout(h_re, h_im, c_re[direction], c_im[direction]))
        if with_ctx_out:
            y_ctx = y_ctx + orient(s5_readout(hc_re, hc_im, c_re[direction], c_im[direction]))
    y = s5_glu(y.astype(u.dtype), w_glu, b_glu)
    if with_ctx_out:
        y_ctx = s5_glu(y_ctx.astype(u.dtype), w_glu, b_glu)
    return y, y_ctx

def sgu_mixer(z, ln_g, ln_b, w_sp, b_sp):
    u, v = jnp.split(z, 2, axis=-1)
    v = layer_norm(v, ln_g, ln_b)
    bsz, length, _ = v.shape
    v = v.reshape(bsz, length // CHUNK, CHUNK, SGU_GROUPS, SGU_GROUP_DIM)
    s = jnp.einsum('bcpgd,gqp->bcqgd', v, w_sp) + jnp.transpose(b_sp)[None, None, :, :, None]
    return u * s.reshape(bsz, length, SGU_WIDTH)

def merge_branches(y_a, y_b, gate_logits, w_proj_a, w_proj_b, b_gate, w_out):
    g_a, g_b = jnp.split(jax.nn.sigmoid(gate_logits + b_gate), N_BRANCH, axis=-1)
    return (g_a * (y_a @ w_proj_a) + g_b * (y_b @ w_proj_b)) @ w_out

def depthwise_conv_grid(u, w, b, rows, cols):
    bsz, _, ch = u.shape
    y = lax.conv_general_dilated(
        u.reshape(bsz, rows, cols, ch), w[:, :, None, :], (1, 1), 'SAME',
        dimension_numbers=('NHWC', 'HWIO', 'NHWC'), feature_group_count=ch)
    return y.reshape(bsz, rows * cols, ch) + b

def conv_ffn(h, w_up, conv_w, conv_b, w_down, rows, cols):
    up = depthwise_conv_grid(h @ w_up, conv_w, conv_b, rows, cols)
    gate, val = jnp.split(up, 2, axis=-1)
    return (jax.nn.silu(gate) * val) @ w_down

def trunk_layer(x, xc, c_silu, cc_silu, rows, w_ada, b_ada, g_mix, w_in,
                s5_a_re, s5_a_im, s5_log_step, s5_b_re, s5_b_im, s5_c_re, s5_c_im,
                s5_d, s5_w_glu, s5_b_glu, sgu_ln_g, sgu_ln_b, sgu_w, sgu_b,
                w_proj_a, w_proj_b, b_gate, w_out, g_ffn, w_up, conv_w, conv_b, w_down,
                update_ctx):
    mod = c_silu @ w_ada + b_ada
    sh1, sc1, ga1, sh2, sc2, ga2 = jnp.split(mod[:, None, :], N_MOD, axis=-1)
    mod_c = cc_silu @ w_ada + b_ada
    sh1c, sc1c, ga1c, sh2c, sc2c, ga2c = jnp.split(mod_c, N_MOD, axis=-1)

    h = modulate(x, g_mix, sh1, sc1)
    hc = modulate(xc, g_mix, sh1c, sc1c)
    proj = h @ w_in
    u_a = proj[..., :S5_WIDTH]
    z_b = jax.nn.gelu(proj[..., S5_WIDTH:S5_WIDTH + 2 * SGU_WIDTH])
    gate_logits = proj[..., S5_WIDTH + 2 * SGU_WIDTH:]
    proj_c = hc @ (w_in if update_ctx else w_in[:, :S5_WIDTH])
    u_ac = proj_c[..., :S5_WIDTH]
    y_a, y_ac = s5_mixer(u_a, u_ac, s5_a_re, s5_a_im, s5_log_step, s5_b_re, s5_b_im,
                         s5_c_re, s5_c_im, s5_d, s5_w_glu, s5_b_glu, update_ctx)
    y_b = sgu_mixer(z_b, sgu_ln_g, sgu_ln_b, sgu_w, sgu_b)
    x = x + ga1 * merge_branches(y_a, y_b, gate_logits, w_proj_a, w_proj_b, b_gate, w_out)

    h2 = modulate(x, g_ffn, sh2, sc2)
    x = x + ga2 * conv_ffn(h2, w_up, conv_w, conv_b, w_down, rows, GRID_W)

    if update_ctx:
        z_bc = jax.nn.gelu(proj_c[..., S5_WIDTH:S5_WIDTH + 2 * SGU_WIDTH])
        gate_c = proj_c[..., S5_WIDTH + 2 * SGU_WIDTH:]
        y_bc = sgu_mixer(z_bc, sgu_ln_g, sgu_ln_b, sgu_w, sgu_b)
        xc = xc + ga1c * merge_branches(y_ac, y_bc, gate_c, w_proj_a, w_proj_b, b_gate, w_out)
        h2c = modulate(xc, g_ffn, sh2c, sc2c)
        mid = CONV_K // 2
        xc = xc + ga2c * conv_ffn(h2c, w_up, conv_w[mid:mid + 1], conv_b, w_down, 1, xc.shape[1])
    else:
        xc = None
    return x, xc

def setup_inputs(seed: int = 0) -> dict:
    key = jax.random.key(seed)
    ks = jax.random.split(key, 40)
    f32 = jnp.float32
    D, L = D_MODEL, DEPTH
    G, N, H = S5_GROUPS, S5_STATE, S5_GROUP
    F2 = 2 * FFN_HIDDEN

    def nrm(k, shape, scale):
        return jax.random.normal(k, shape, f32) * scale

    n_idx = jnp.arange(N, dtype=f32)
    return {
        'x': nrm(ks[0], (BATCH, SEQ, D), 1.0),
        'c': nrm(ks[1], (BATCH, D), 1.0),
        'ctx': nrm(ks[2], (BATCH, CTX_LEN, D), 1.0),
        'c_ctx': nrm(ks[3], (D,), 1.0),
        'w_ada': nrm(ks[4], (L, D, N_MOD * D), 0.5 * D ** -0.5),
        'b_ada': nrm(ks[5], (L, N_MOD * D), 0.02),
        'g_mix': 1.0 + nrm(ks[6], (L, D), 0.02),
        'w_in': nrm(ks[7], (L, D, IN_WIDTH), D ** -0.5),
        's5_a_re': -0.5 + nrm(ks[8], (L, 2, G, N), 0.01),
        's5_a_im': math.pi * n_idx + nrm(ks[9], (L, 2, G, N), 0.01),
        's5_log_step': jax.random.uniform(ks[10], (L, 2, G), f32, math.log(DT_MIN), math.log(DT_MAX)),
        's5_b_re': nrm(ks[11], (L, 2, G, N, H), (2 * H) ** -0.5),
        's5_b_im': nrm(ks[12], (L, 2, G, N, H), (2 * H) ** -0.5),
        's5_c_re': nrm(ks[13], (L, 2, G, H, N), N ** -0.5),
        's5_c_im': nrm(ks[14], (L, 2, G, H, N), N ** -0.5),
        's5_d': nrm(ks[15], (L, S5_WIDTH), 1.0),
        's5_w_glu': nrm(ks[16], (L, S5_WIDTH, S5_WIDTH), S5_WIDTH ** -0.5),
        's5_b_glu': nrm(ks[17], (L, S5_WIDTH), 0.02),
        'sgu_ln_g': 1.0 + nrm(ks[18], (L, SGU_WIDTH), 0.02),
        'sgu_ln_b': nrm(ks[19], (L, SGU_WIDTH), 0.02),
        'sgu_w': nrm(ks[20], (L, SGU_GROUPS, CHUNK, CHUNK), CHUNK ** -0.5),
        'sgu_b': 1.0 + nrm(ks[21], (L, SGU_GROUPS, CHUNK), 0.1),
        'w_proj_a': nrm(ks[22], (L, S5_WIDTH, D), S5_WIDTH ** -0.5),
        'w_proj_b': nrm(ks[23], (L, SGU_WIDTH, D), SGU_WIDTH ** -0.5),
        'b_gate': nrm(ks[24], (L, N_BRANCH * D), 0.02),
        'w_out': nrm(ks[25], (L, D, D), D ** -0.5),
        'g_ffn': 1.0 + nrm(ks[26], (L, D), 0.02),
        'w_up': nrm(ks[27], (L, D, F2), D ** -0.5),
        'conv_w': nrm(ks[28], (L, CONV_K, CONV_K, F2), 1.0 / CONV_K),
        'conv_b': nrm(ks[29], (L, F2), 0.02),
        'w_down': nrm(ks[30], (L, FFN_HIDDEN, D), FFN_HIDDEN ** -0.5),
        'g_final': 1.0 + nrm(ks[31], (D,), 0.02),
    }

def reference(x, c, ctx, c_ctx, w_ada, b_ada, g_mix, w_in, s5_a_re, s5_a_im, s5_log_step,
              s5_b_re, s5_b_im, s5_c_re, s5_c_im, s5_d, s5_w_glu, s5_b_glu,
              sgu_ln_g, sgu_ln_b, sgu_w, sgu_b, w_proj_a, w_proj_b, b_gate, w_out,
              g_ffn, w_up, conv_w, conv_b, w_down, g_final):
    rows = x.shape[1] // GRID_W
    c_silu = jax.nn.silu(c)
    cc_silu = jax.nn.silu(c_ctx)
    xc = ctx
    for i in range(DEPTH):
        x, xc = trunk_layer(
            x, xc, c_silu, cc_silu, rows, w_ada[i], b_ada[i], g_mix[i], w_in[i],
            s5_a_re[i], s5_a_im[i], s5_log_step[i], s5_b_re[i], s5_b_im[i], s5_c_re[i], s5_c_im[i],
            s5_d[i], s5_w_glu[i], s5_b_glu[i], sgu_ln_g[i], sgu_ln_b[i], sgu_w[i], sgu_b[i],
            w_proj_a[i], w_proj_b[i], b_gate[i], w_out[i], g_ffn[i], w_up[i], conv_w[i], conv_b[i],
            w_down[i], i + 1 < DEPTH)
    return rms_norm(x, g_final)


_drawn_inputs = setup_inputs


def setup_inputs(seed=0):
    import zlib

    import numpy as np

    out = dict(_drawn_inputs(seed))
    spreads = {}
    factors = {'ctx': 64.0,
     'c_ctx': 64.0,
     'b_ada': 2.931,
     'g_mix': 8.0,
     's5_a_re': 64.0,
     's5_a_im': 47.552,
     's5_log_step': 54.464,
     's5_b_re': 64.0,
     's5_b_im': 64.0,
     's5_c_re': 60.824,
     's5_c_im': 64.0,
     's5_b_glu': 200.0,
     'sgu_ln_g': 22.538,
     'sgu_ln_b': 21.338,
     'sgu_b': 4.536,
     'b_gate': 8.0,
     'g_ffn': 21.345,
     'conv_b': 41.518,
     'g_final': 23.603}
    for name, (base, spread) in spreads.items():
        noise = np.random.default_rng([zlib.crc32(name.encode()), seed]).standard_normal(out[name].shape)
        drawn = base * np.exp(spread * noise) if base else spread * noise
        out[name] = jnp.asarray(drawn.astype(out[name].dtype))
    for name, factor in factors.items():
        out[name] = (out[name] * factor).astype(out[name].dtype)
    return out
```

```python
from contextlib import ExitStack

import numpy as np

import concourse.bass as bass
from concourse import mybir

F32 = mybir.dt.float32
ALU = mybir.AluOpType
ACT = mybir.ActivationFunctionType

P = 128
D = 1024
KD = D // P
TOK = 256
GRID_W = 64
GRID_H = TOK // GRID_W
S5W = 512
KS = S5W // P
G, H, N = 32, 16, 64
PAIRS = G // 2
T = 8
CH = TOK // T
LAGS = 2 * T - 1
FFN = 2816
KF = FFN // P
NMOD = 6
EPS = 1e-6
TWO_PI = 2.0 * np.pi
ROUND_MAGIC = 12582912.0

RING = 3
UNIT = 2048
U_ADA1, U_INU, U_ZU, U_V, U_LOOP = 0, 8, 10, 12, 14
LOOPS = 8
U_GLU = U_LOOP + 3 * LOOPS
U_PROJ = U_GLU + 1
U_OUT = U_PROJ + 4
UNITS = U_OUT + 4
USLOTS = 11
UP_ROUNDS = KF // USLOTS

_PK = {}
_at = 0
for _name, _w in [("c", KD), ("c_ctx", KD), ("b_ada", NMOD * KD), ("g_mix", KD), ("g_ffn", KD), ("g_final", KD),
                  ("b_gate", 2 * KD), ("b_glu", KS), ("s5_d", KS), ("conv_b", 2 * KF), ("conv_w", 2 * KF * 9)]:
    _PK[_name] = (_at, _at + _w)
    _at += _w
PKW = _at
DP = 2 * PAIRS
S5RAW = DP * 2 + DP * H * 4


def build(nc, x_t, ctx_t, pk, s5raw, log_step, ring_w, up_w, ln, sgu_w, sgu_b, out):
    with ExitStack() as ctx:
        def sb(name, n):
            return ctx.enter_context(nc.sbuf_tensor(name, [P, n], F32))

        def sem(name):
            return ctx.enter_context(nc.semaphore(name))

        bank = [ctx.enter_context(nc.psum_tensor(f"bank{i}", [P, 512], F32)) for i in range(8)]

        s5_region = sb("s5_region", 8192 + 9216 + 4096 + 4096)
        w_in_s5 = s5_region[:, 0:8192].rearrange("p (d r q m) -> p d r q m", d=2, r=2, q=PAIRS)
        ca_region = s5_region[:, 8192:8192 + 9216]
        w_src = ca_region[:, 0:8192].rearrange("p (d r q t h) -> p d r q t h", d=2, r=2, q=PAIRS, t=T)
        ca = ca_region.rearrange("p (r c e h) -> p r c e h", r=2, c=DP, e=T + 1)
        m_region = s5_region[:, 17408:17408 + 4096]
        scratch = m_region[:, 0:2304]
        b_raw = m_region[:, 2304:2304 + 1024].rearrange("p (r c h) -> p r c h", r=2, c=DP)
        m_toep = m_region.rearrange("p (g m) -> p g m", g=G)
        e_region = s5_region[:, 21504:21504 + 4096]
        c_raw = e_region[:, 0:1024].rearrange("p (r c h) -> p r c h", r=2, c=DP)
        b_bar = e_region[:, 1024:2048].rearrange("p (r c h) -> p r c h", r=2, c=DP)
        b_pad = e_region[:, 2048:4096].rearrange("p (r c g h) -> p r c g h", r=2, c=DP, g=2)
        e_chunk = e_region.rearrange("p (s c) -> p s c", s=2 * CH)
        up_ring = s5_region[:, 0:USLOTS * UNIT].rearrange("p (s n) -> p s n", s=USLOTS)

        x_region = sb("x_region", KD * TOK)
        x_sb = x_region[:, :].rearrange("p (k t) -> p k t", k=KD)
        carry = x_region[:, :].rearrange("p (c s) -> p c s", c=2 * DP)
        ctx_region = sb("ctx_region", KD * TOK)
        ctx_sb = ctx_region[:, :].rearrange("p (k t) -> p k t", k=KD)
        u_chunk = ctx_region[:, :].rearrange("p (g c) -> p g c", g=G)
        y_chunk = ctx_region[:, 0:1024]
        y_feat = ctx_region[:, 1024:2048].rearrange("p (m t c) -> p m t c", m=KS, t=T)
        glu_gate = ctx_region[:, 0:1024].rearrange("p (m t) -> p m t", m=KS)
        up_sb = ctx_region[:, 0:1024].rearrange("p (b n) -> p b n", b=2)
        conv = ctx_region[:, 1024:2048].rearrange("p (b n) -> p b n", b=2)
        hx_region = sb("hx_region", KD * TOK)
        h_x = hx_region[:, :].rearrange("p (k t) -> p k t", k=KD)
        merged = h_x
        hc_region = sb("hc_region", KD * TOK)
        h_c = hc_region[:, :].rearrange("p (k t) -> p k t", k=KD)
        ln_sb = hc_region[:, 0:1024].rearrange("p (a n) -> p a n", a=2)
        sgu_w_sb = hc_region[:, 1024:2048].rearrange("p (g q) -> p g q", g=8)
        h2 = h_c
        uf_region = sb("uf_region", 2048)
        u_feat = uf_region[:, :].rearrange("p (m t c) -> p m t c", m=KS, t=T)
        y_gelu = uf_region[:, 0:1024].rearrange("p (m t) -> p m t", m=KS)
        y_a = uf_region[:, 1024:2048].rearrange("p (m t) -> p m t", m=KS)
        ring_region = sb("ring_region", RING * UNIT)
        ring = ring_region[:, :].rearrange("p (s n) -> p s n", s=RING)
        ffn_act = ring_region[:, 0:KF * TOK].rearrange("p (j t) -> p j t", j=KF)
        gates = sb("gates", 2 * KD * TOK)[:, :].rearrange("p (m t) -> p m t", m=2 * KD)
        silu_sb = gates[:, 0:2, :]
        merge_tmp = sb("merge_tmp", 2 * TOK)[:, :].rearrange("p (b t) -> p b t", b=2)
        z_region = sb("z_region", 2048)
        z_u = z_region[:, 0:1024].rearrange("p (m t) -> p m t", m=KS)
        v_tok = z_region[:, 1024:2048].rearrange("p (c n) -> p c n", c=2)
        squares = z_region[:, 1024:2048].rearrange("p (b n) -> p b n", b=2)
        y_b = z_u
        sgu_b_sb = sb("sgu_b_sb", 512)[:, :].rearrange("p (j q) -> p j q", j=4)
        rstd = sb("rstd", 512)
        pk_sb = sb("pk_sb", PKW)
        c_silu = sb("c_silu", 2 * KD)[:, :].rearrange("p (k v) -> p k v", k=KD)
        mod1 = sb("mod1", 4 * KD)[:, :].rearrange("p (m v) -> p m v", v=2)
        scale1 = sb("scale1", 2 * KD)[:, :].rearrange("p (k v) -> p k v", v=2)
        mod2 = sb("mod2", 4 * KD)
        scale2 = sb("scale2", KD)
        ones = sb("ones", P)
        ident = sb("ident", P)
        power = sb("power", 2 * (T + 1) * DP)[:, :].rearrange("p (r e c) -> p r e c", r=2, e=T + 1)
        a_raw = sb("a_raw", 3 * DP)
        small = sb("small", 20 * DP)
        ptmp = sb("ptmp", 4 * DP)
        stepper = sb("stepper", 2 * 2 * DP)
        a_same, a_cross = stepper[:, 0:2 * DP], stepper[:, 2 * DP:4 * DP]
        state = sb("state", 2 * DP)
        scan_t = sb("scan_t", 2 * 2 * DP)
        scan_same, scan_cross = scan_t[:, 0:2 * DP], scan_t[:, 2 * DP:4 * DP]
        bn = sb("bn", 2 * 6 + 2 * 2 + 4)
        k_sb = m_region[:, 0:KS * LAGS * H]

        def par(name):
            a, b = _PK[name]
            return pk_sb[:, a:b]

        u_dram = nc.dram_tensor("u_scratch", [KS, P, T, 2 * CH], F32)
        k_dram = nc.dram_tensor("k_scratch", [KS, P, LAGS * H], F32)
        y_dram = nc.dram_tensor("y_scratch", [KS, P, T, CH], F32)

        s_pk, s_raw, s_x, s_ctx = sem("pk_loaded"), sem("s5_raw_loaded"), sem("x_loaded"), sem("ctx_loaded")
        s_ls = sem("log_step_loaded")
        s_ring = [sem(f"ring_loaded{i}") for i in range(RING)]
        s_unit = sem("unit_multiplied")
        s_up = [sem(f"up_loaded{i}") for i in range(USLOTS)]
        s_up_used = sem("up_used")
        s_const, s_pad = sem("constants_set"), sem("pad_zeroed")
        s_sq, s_sq_used = sem("squares_ready"), sem("squares_used")
        s_stat, s_std, s_rstd = sem("stat_summed"), sem("std_ready"), sem("rstd_ready")
        s_csilu = sem("c_silu_ready")
        s_mod1, s_scale1 = sem("mod1_ready"), sem("scale1_ready")
        s_norm, s_h = sem("normed_ready"), sem("h_ready")
        s_trig_in, s_trig = sem("trig_args_ready"), sem("act_exp_sin_done")
        s_wsrc, s_tr, s_win = sem("w_src_ready"), sem("transposed"), sem("w_in_evacuated")
        s_bpad, s_ca = sem("b_pad_ready"), sem("ca_ready")
        s_u_ps, s_uf, s_u_out, s_uchunk = sem("u_in_psum"), sem("u_feat_ready"), sem("u_stored"), sem("u_chunk_loaded")
        s_z = sem("z_ready")
        s_v_ps, s_v, s_vn = sem("v_in_psum"), sem("v_gelu_ready"), sem("v_normed")
        s_ln = sem("gating_params_loaded")
        s_sgu_ps, s_yb = sem("sgu_in_psum"), sem("y_b_ready")
        s_k_ps, s_k, s_k_out, s_m = sem("k_in_psum"), sem("k_evacuated"), sem("k_stored"), sem("m_loaded")
        s_e_ps, s_e, s_scan = sem("e_in_psum"), sem("e_evacuated"), sem("scan_step")
        s_gate = sem("gate_ready")
        s_mod2, s_scale2 = sem("mod2_ready"), sem("scale2_ready")
        s_y8_ps, s_y8, s_y_out, s_yf = sem("y_chunk_in_psum"), sem("y_chunk_ready"), sem("y_stored"), sem("y_feat_loaded")
        s_y, s_ygelu = sem("y_with_skip_ready"), sem("y_gelu_ready")
        s_glu_ps, s_glu, s_ya = sem("glu_in_psum"), sem("glu_gate_ready"), sem("y_a_ready")
        s_pr_ps, s_mg = sem("proj_in_psum"), sem("merged_ready")
        s_xr = sem("x_reloaded")
        s_x1 = sem("x1_ready")
        s_norm2, s_h2 = sem("normed2_ready"), sem("h2_ready")
        s_up_ps, s_upsb, s_conv = sem("up_in_psum"), sem("up_evacuated"), sem("conv_tap")
        s_silu, s_act = sem("silu_ready"), sem("ffn_act_ready")
        s_dn_ps, s_x2, s_fin, s_stored = sem("down_in_psum"), sem("x2_ready"), sem("final_ready"), sem("out_stored")
        s_dve = sem("dve_chain")
        s_pool = sem("pool_chain")
        s_lnvar, s_lnstd = sem("ln_variance_ready"), sem("ln_deviation_ready")

        CONV_OPS = 18
        SCAN_OPS = 4
        block = ctx.enter_context(nc.Block())

        def ring_ready(pe, u):
            pe.wait_ge(s_ring[u % RING], 16 * (u // RING + 1))

        @block.sync
        def _(sp):
            sp.dma_start(x_region[:, :], x_t).then_inc(s_x, 16)
            sp.dma_start(ctx_region[:, :], ctx_t).then_inc(s_ctx, 16)
            for s in range(RING):
                sp.dma_start(ring[:, s, :], ring_w[s]).then_inc(s_ring[s], 16)
            full = UNITS // RING
            with sp.Fori(1, full) as i:
                for s in range(RING):
                    sp.wait_ge(s_unit, i * RING + (s - RING + 1))
                    sp.dma_start(ring[:, s, :], ring_w[bass.ds(i * RING + s, 1)].rearrange("a p n -> p (a n)")).then_inc(s_ring[s], 16)
            for u in range(full * RING, UNITS):
                sp.wait_ge(s_unit, u - RING + 1)
                sp.dma_start(ring[:, u % RING, :], ring_w[u]).then_inc(s_ring[u % RING], 16)
            sp.wait_ge(s_y8_ps, 2)
            for s in range(USLOTS):
                sp.dma_start(up_ring[:, s, :], up_w[s]).then_inc(s_up[s], 16)
            with sp.Fori(1, UP_ROUNDS + 1) as r:
                for s in range(USLOTS):
                    sp.wait_ge(s_up_used, r * USLOTS + (s - USLOTS + 1))
                    sp.dma_start(up_ring[:, s, :], up_w[bass.ds(r * USLOTS + s, 1)].rearrange("a p n -> p (a n)")).then_inc(s_up[s], 16)
            for m in range(KD):
                sp.wait_ge(s_fin, m + 1)
                sp.dma_start(out[:, m, :], x_sb[:, m, :]).then_inc(s_stored, 16)
            sp.wait_ge(s_stored, 16 * KD)

        @block.gpsimd
        def _(pool):
            pool.memset(ones[:, :], 1.0).then_inc(s_const, 1)
            pool.memset(ident[:, :], 0.0).then_inc(s_pool, 1)
            pool.wait_ge(s_pool, 1)
            pool.affine_select(out=ident[:, :], in_=ident[:, :], compare_op=ALU.not_equal, fill=1.0, base=0,
                               pattern=[[-1, P]], channel_multiplier=1).then_inc(s_const, 1)
            pool.memset(b_pad, 0.0).then_inc(s_pad, 1)
            pool.dma_start(sgu_b_sb[0:64, :, :], sgu_b[0:1].partition_broadcast(64)).then_inc(s_ln, 16)
            pool.dma_start(sgu_b_sb[64:128, :, :], sgu_b[1:2].partition_broadcast(64)).then_inc(s_ln, 16)
            pool.wait_ge(s_unit, U_ZU)
            pool.dma_start(ln_sb, ln.partition_broadcast(P)).then_inc(s_ln, 16)
            pool.dma_start(sgu_w_sb, sgu_w).then_inc(s_ln, 16)
            pool.wait_ge(s_y8_ps, 2)
            pool.dma_start(x_region[:, :], x_t).then_inc(s_xr, 16)
            pool.sem_inc(s_act, 2)
            with pool.Fori(0, KF // 2) as i:
                for b in range(2):
                    pool.wait_ge(s_silu, i * 2 + (b + 1))
                    pool.tensor_tensor(ffn_act[:, bass.ds(i * 2 + b, 1), :].rearrange("p a t -> p (a t)"), silu_sb[:, b, :],
                                       conv[:, b, TOK:2 * TOK], ALU.mult).then_inc(s_act, 1)

        @block.tensor
        def _(pe):
            pe.wait_ge(s_const, 1)
            for k in range(KD):
                pe.wait_ge(s_sq, k + 1)
                pe.matmul(bank[7][:, :], ones[:, :], squares[:, k % 2, :], start=(k == 0),
                          stop=(k == KD - 1)).then_inc(s_sq_used, 1)

            pe.wait_ge(s_csilu, 1)
            for u in range(U_ADA1, U_INU):
                ring_ready(pe, u)
                for mm in range(2):
                    m = 2 * u + mm
                    for k in range(KD):
                        mx = pe.matmul(bank[6][:, 2 * m:2 * m + 2], ring[:, u % RING, (mm * KD + k) * P:(mm * KD + k + 1) * P],
                                       c_silu[:, k, :], start=(k == 0), stop=(k == KD - 1))
                mx.then_inc(s_unit, 1)

            pe.wait_ge(s_const, 2)
            job = 0
            for d in range(2):
                for r in range(2):
                    pe.wait_ge(s_wsrc, 2 * d + r + 1)
                    for q0 in range(0, PAIRS, 4):
                        if job >= 4:
                            pe.wait_ge(s_win, job - 3)
                        for q in range(4):
                            mx = pe.transpose(bank[job % 4][:, q * P:(q + 1) * P],
                                              w_src[:, d, r, q0 + q].rearrange("p t h -> p (t h)"), ident[:, :])
                        mx.then_inc(s_tr, 1)
                        job += 1
            n_tr = job

            for m in range(KS):
                u = U_INU + m // 2
                if m % 2 == 0:
                    ring_ready(pe, u)
                pe.wait_ge(s_win, n_tr - 3 + m)
                for src, h, off in ((0, h_c, 0), (1, h_x, TOK)):
                    if m == 0:
                        pe.wait_ge(s_h, (1 + src) * KD)
                    for k in range(KD):
                        mx = pe.matmul(bank[m][:, off:off + TOK], ring[:, u % RING, ((m % 2) * KD + k) * P:((m % 2) * KD + k + 1) * P],
                                       h[:, k, :], start=(k == 0), stop=(k == KD - 1))
                mx.then_inc(s_unit if m % 2 else s_u_ps, 1)

            for i in range(2):
                u = U_ZU + i
                ring_ready(pe, u)
                for mm in range(2):
                    for k in range(KD):
                        mx = pe.matmul(bank[4 + i][:, mm * TOK:(mm + 1) * TOK], ring[:, u % RING, (mm * KD + k) * P:(mm * KD + k + 1) * P],
                                       h_x[:, k, :], start=(k == 0), stop=(k == KD - 1))
                mx.then_inc(s_unit, 1)

            pe.wait_ge(s_mod1, 1)
            pe.wait_ge(s_std, 1)
            for half in range(2):
                u = U_V + half
                ring_ready(pe, u)
                for c in range(2):
                    for kk in range(KD // 2):
                        k = half * (KD // 2) + kk
                        mx = pe.matmul(bank[6 + c][:, :], h_x[:, k, c * P:(c + 1) * P], ring[:, u % RING, kk * 512:(kk + 1) * 512],
                                       start=(k == 0), stop=(k == KD - 1))
                    if half == 1 and c == 0:
                        mx.then_inc(s_v_ps, 1)
                mx.then_inc(s_unit, 1)

            pe.wait_ge(s_bpad, 1)
            pe.wait_ge(s_ca, 2)
            pe.wait_ge(s_v, 2)
            for q in range(PAIRS):
                m, row = q // 4, 32 * (q % 4)
                base = (m % 2) * LAGS * H
                for d, e0, j0 in ((1, 1, 0), (0, 0, T - 1)):
                    for r in range(2):
                        mx = pe.matmul(bank[6 + m // 2][row:row + 32, base + j0 * H:base + (j0 + T) * H],
                                       b_pad[:, r, d * PAIRS + q].rearrange("p g h -> p (g h)"),
                                       ca[:, r, d * PAIRS + q, e0:e0 + T, :].rearrange("p e h -> p (e h)"),
                                       start=(d == 1 and r == 0), stop=(d == 0 and r == 1), skip_group_check=True)
                if q % 8 == 7:
                    mx.then_inc(s_k_ps, 1)

            pe.wait_ge(s_uchunk, 16 * T)
            for job in range(8):
                d, r, q0 = job // 4, (job // 2) % 2, 8 * (job % 2)
                if job < 4:
                    pe.wait_ge(s_uf, KS)
                else:
                    pe.wait_ge(s_e, job - 3)
                for q in range(q0, q0 + 8):
                    for g2 in range(2):
                        rhs = u_chunk[:, 2 * q + g2, :].rearrange("p (a c) -> p a c", a=2)
                        if d == 1:
                            rhs = rhs[:, :, ::-1]
                        mx = pe.matmul(bank[job % 4][g2 * N:(g2 + 1) * N, (q - q0) * 2 * CH:(q - q0 + 1) * 2 * CH],
                                       w_in_s5[:, d, r, q, g2 * N:(g2 + 1) * N], rhs, start=True, stop=True)
                mx.then_inc(s_e_ps, 1)

            pe.wait_ge(s_vn, 2)
            pe.wait_ge(s_ln, 64)
            pe.wait_ge(s_z, 2)
            for j in range(4):
                for g2 in range(2):
                    for c in range(2):
                        mx = pe.matmul(bank[4 + j // 2][g2 * 64:(g2 + 1) * 64, (j % 2) * TOK + c * P:(j % 2) * TOK + (c + 1) * P],
                                       v_tok[:, c, (2 * j + g2) * 64:(2 * j + g2 + 1) * 64], sgu_w_sb[:, 2 * j + g2, :],
                                       start=True, stop=True)
                if j % 2 == 1:
                    mx.then_inc(s_sgu_ps, 1)

            def gates_and_modulation(i):
                for s in range(3):
                    slot = (U_LOOP + s) % RING
                    pe.wait_ge(s_ring[slot], (i + ((U_LOOP + s) // RING + 1)) * 16)
                    if s == 0:
                        pe.wait_ge(s_gate, i * 2 + 1)
                        for mm in range(2):
                            for k in range(KD):
                                mx = pe.matmul(bank[6][:, mm * TOK:(mm + 1) * TOK], ring[:, slot, (mm * KD + k) * P:(mm * KD + k + 1) * P],
                                               h_x[:, k, :], start=(k == 0), stop=(k == KD - 1))
                        mx.then_inc(s_unit, 1)
                    else:
                        for mm in range(2):
                            for k in range(KD):
                                mx = pe.matmul(bank[7][:, bass.ds(i * 4 + (2 * (s - 1) + mm), 1)],
                                               ring[:, slot, (mm * KD + k) * P:(mm * KD + k + 1) * P],
                                               c_silu[:, k, 0:1], start=(k == 0), stop=(k == KD - 1))
                        mx.then_inc(s_unit, 1)

            pe.wait_ge(s_k, 2)
            with pe.Fori(0, LOOPS // 2) as i:
                gates_and_modulation(i)

            pe.wait_ge(s_m, 16 * T)
            pe.wait_ge(s_scan, SCAN_OPS * (2 * CH - 1) + 2)
            pe.wait_ge(s_e, 8)
            for g2 in range(2):
                for q in range(PAIRS):
                    dst = bank[g2][:, q * CH:(q + 1) * CH]
                    pe.matmul(dst, m_toep[:, 2 * q + g2, :], u_chunk[:, 2 * q + g2, CH:2 * CH], start=True, stop=False)
                    for d, e0 in ((0, 1), (1, 0)):
                        for r in range(2):
                            rhs = carry[g2 * N:(g2 + 1) * N, (r * 2 + d) * PAIRS + q, :]
                            if d == 1:
                                rhs = rhs[:, ::-1]
                            mx = pe.matmul(dst, ca[g2 * N:(g2 + 1) * N, r, d * PAIRS + q, e0:e0 + T, :].rearrange("p e h -> p (e h)"),
                                           rhs, start=False, stop=(d == 1 and r == 1))
                mx.then_inc(s_y8_ps, 1)

            with pe.Fori(LOOPS // 2, LOOPS) as i:
                gates_and_modulation(i)

            ring_ready(pe, U_GLU)
            pe.wait_ge(s_ygelu, 1)
            for m in range(KS):
                for k in range(KS):
                    mx = pe.matmul(bank[2 + m // 2][:, (m % 2) * TOK:(m % 2 + 1) * TOK],
                                   ring[:, U_GLU % RING, (m * KS + k) * P:(m * KS + k + 1) * P], y_gelu[:, k, :],
                                   start=(k == 0), stop=(k == KS - 1))
                if m == 1:
                    mx.then_inc(s_glu_ps, 1)
            mx.then_inc(s_unit, 1)

            pe.wait_ge(s_yb, 4)
            for m in range(KD):
                ub, ua = U_PROJ + 2 * (m // 4), U_PROJ + 2 * (m // 4) + 1
                dst = bank[(4, 6, 7, 5)[m % 4]]
                if m >= 4:
                    pe.wait_ge(s_mg, m - 3)
                elif m == 1:
                    pe.wait_ge(s_gate, 2 * LOOPS + 1)
                elif m == 2:
                    pe.wait_ge(s_mod2, 1)
                if m % 4 == 0:
                    ring_ready(pe, ub)
                    ring_ready(pe, ua)
                for half, (u, src) in enumerate(((ub, y_b), (ua, y_a))):
                    if m == 0 and half == 1:
                        pe.wait_ge(s_ya, KS)
                    for k in range(KS):
                        mx = pe.matmul(dst[:, (1 - half) * TOK:(2 - half) * TOK], ring[:, u % RING, ((m % 4) * KS + k) * P:((m % 4) * KS + k + 1) * P],
                                       src[:, k, :], start=(k == 0), stop=(k == KS - 1))
                    if m % 4 == 3 and half == 0:
                        mx.then_inc(s_unit, 1)
                mx.then_inc(s_unit if m % 4 == 3 else s_pr_ps, 1)

            for i in range(4):
                u = U_OUT + i
                ring_ready(pe, u)
                if i == 0:
                    pe.wait_ge(s_mg, KD)
                    pe.wait_ge(s_y8, 2)
                if i == 2:
                    pe.wait_ge(s_glu, KS)
                for mm in range(2):
                    for k in range(KD):
                        mx = pe.matmul(bank[i][:, mm * TOK:(mm + 1) * TOK], ring[:, u % RING, (mm * KD + k) * P:(mm * KD + k + 1) * P],
                                       merged[:, k, :], start=(k == 0), stop=(k == KD - 1))
                mx.then_inc(s_unit, 1)

            for k in range(KD):
                pe.wait_ge(s_sq, KD + k + 1)
                pe.matmul(bank[4][:, 0:TOK], ones[:, :], squares[:, k % 2, 0:TOK], start=(k == 0),
                          stop=(k == KD - 1)).then_inc(s_sq_used, 1)

            pe.wait_ge(s_h2, KD)
            with pe.Fori(0, UP_ROUNDS) as r:
                for s in range(USLOTS):
                    pe.wait_ge(s_up[s], r * 16 + 16)
                    pe.wait_ge(s_upsb, r * USLOTS + max(1, s - 1))
                    for half in range(2):
                        for k in range(KD):
                            mx = pe.matmul(bank[s % 3][:, half * TOK:(half + 1) * TOK], up_ring[:, s, (half * KD + k) * P:(half * KD + k + 1) * P],
                                           h2[:, k, :], start=(k == 0), stop=(k == KD - 1))
                    mx.then_inc(s_up_used, 1)

            pe.wait_ge(s_h2, KD)
            for k in range(KF):
                s = k // 2
                if k % 2 == 0:
                    pe.wait_ge(s_up[s], 16 * (UP_ROUNDS + 1))
                pe.wait_ge(s_act, k + 3)
                for m in range(KD):
                    mx = pe.matmul(bank[4 + m // 2][:, (m % 2) * TOK:(m % 2 + 1) * TOK],
                                   up_ring[:, s, (k % 2) * D + m * P:(k % 2) * D + (m + 1) * P], ffn_act[:, k, :],
                                   start=(k == 0 and m % 2 == 0), stop=(k == KF - 1), skip_group_check=True)
                    if k == KF - 1 and m % 2 == 1:
                        mx.then_inc(s_dn_ps, 1)

            for k in range(KD):
                pe.wait_ge(s_sq, 2 * KD + k + 1)
                pe.matmul(bank[3][:, 0:TOK], ones[:, :], squares[:, k % 2, 0:TOK], start=(k == 0),
                          stop=(k == KD - 1)).then_inc(s_sq_used, 1)

        @block.scalar
        def _(act):
            act.sem_inc(s_gate, 1)
            act.sem_inc(s_upsb, 1)
            act.dma_start(a_raw[:, 0:2 * DP], s5raw[:, 0:2 * DP]).then_inc(s_raw, 16)
            for g2 in range(2):
                act.dma_start(a_raw[g2 * N:(g2 + 1) * N, 2 * DP:3 * DP], log_step[g2:g2 + 1].partition_broadcast(N)).then_inc(s_ls, 16)
            act.dma_start(pk_sb[:, :], pk).then_inc(s_pk, 16)
            act.dma_start(m_region[:, 2304:2304 + 1024], s5raw[:, 2 * DP:2 * DP + 1024]).then_inc(s_raw, 16)
            act.dma_start(e_region[:, 0:1024], s5raw[:, 2 * DP + 1024:2 * DP + 2048]).then_inc(s_raw, 16)

            act.wait_ge(s_ls, 32)
            act.activation(small[:, 0:DP], a_raw[:, 2 * DP:3 * DP], ACT.Exp).then_inc(s_trig, 1)
            act.wait_ge(s_trig_in, 1)
            act.activation(small[:, 2 * DP:3 * DP], small[:, DP:2 * DP], ACT.Exp).then_inc(s_trig, 1)
            act.wait_ge(s_trig_in, 2)
            act.activation(small[:, 5 * DP:6 * DP], small[:, 4 * DP:5 * DP], ACT.Sin).then_inc(s_trig, 1)
            act.activation(small[:, 6 * DP:7 * DP], small[:, 4 * DP:5 * DP], ACT.Sin, scale=0.5).then_inc(s_trig, 1)

            act.wait_ge(s_pk, 16)
            act.activation(c_silu.rearrange("p k v -> p v k"), pk_sb[:, 0:2 * KD].rearrange("p (v k) -> p v k", v=2),
                           ACT.Silu).then_inc(s_csilu, 1)

            act.wait_ge(s_ctx, 16)
            act.wait_ge(s_x, 16)
            for k in range(KD):
                if k >= 2:
                    act.wait_ge(s_sq_used, k - 1)
                act.activation(squares[:, k % 2, 0:TOK], ctx_sb[:, k, :], ACT.Square)
                act.activation(squares[:, k % 2, TOK:2 * TOK], x_sb[:, k, :], ACT.Square).then_inc(s_sq, 1)
            act.wait_ge(s_sq_used, KD)
            act.activation(rstd[:, :], bank[7][:, :], ACT.Sqrt, scale=1.0 / D, bias=EPS).then_inc(s_std, 1)

            job = 0
            for d in range(2):
                for r in range(2):
                    for q0 in range(0, PAIRS, 4):
                        act.wait_ge(s_tr, job + 1)
                        act.activation(w_in_s5[:, d, r, q0:q0 + 4, :].rearrange("p q m -> p (q m)"), bank[job % 4][:, :],
                                       ACT.Copy).then_inc(s_win, 1)
                        job += 1

            act.wait_ge(s_scale1, 1)
            for v, h in ((1, h_c), (0, h_x)):
                for k in range(KD):
                    act.wait_ge(s_norm, (1 - v) * KD + k + 1)
                    act.activation(h[:, k, :], h[:, k, :], ACT.Identity, scale=scale1[:, k, v:v + 1],
                                   bias=mod1[:, k, v:v + 1]).then_inc(s_h, 1)

            for m in range(KS):
                act.wait_ge(*((s_unit, U_INU + m // 2 + 1) if m % 2 else (s_u_ps, m // 2 + 1)))
                act.activation(u_feat[:, m, :, :], bank[m][:, :].rearrange("p (c t) -> p t c", t=T), ACT.Copy).then_inc(s_uf, 1)
                act.wait_ge(s_uf, m + 1)
                act.dma_start(u_dram[m].rearrange("p t c -> p (t c)"), u_feat[:, m, :, :].rearrange("p t c -> p (t c)")).then_inc(s_u_out, 16)
            act.wait_ge(s_u_out, 16 * KS)
            for tau in range(T):
                act.dma_start(u_chunk[tau * H:(tau + 1) * H, :, :],
                              u_dram[:, :, tau, :].rearrange("m (g h) c -> h (m g) c", h=H)).then_inc(s_uchunk, 16)

            for i in range(2):
                act.wait_ge(s_unit, U_ZU + i + 1)
                act.activation(z_u[:, 2 * i:2 * i + 2, :].rearrange("p m t -> p (m t)"), bank[4 + i][:, :], ACT.Gelu_apprx_tanh).then_inc(s_z, 1)
            for c in range(2):
                act.wait_ge(*((s_unit, U_LOOP) if c else (s_v_ps, 1)))
                act.activation(v_tok[:, c, :], bank[6 + c][:, :], ACT.Gelu_apprx_tanh).then_inc(s_v, 1)

            for b in range(2):
                act.wait_ge(s_k_ps, b + 1)
                act.activation(k_sb[:, 2 * b * LAGS * H:(2 * b + 2) * LAGS * H], bank[6 + b][:, 0:2 * LAGS * H], ACT.Copy).then_inc(s_k, 1)
            act.wait_ge(s_k, 2)
            act.dma_start(k_dram[:].rearrange("m p n -> p m n"), k_sb[:, :].rearrange("p (m n) -> p m n", m=KS)).then_inc(s_k_out, 16)
            for c in range(2):
                act.wait_ge(s_lnvar, c + 1)
                act.activation(bn[:, 18 + c:19 + c], bn[:, 16 + c:17 + c], ACT.Sqrt).then_inc(s_lnstd, 1)
            for job in range(8):
                d, r, q0 = job // 4, (job // 2) % 2, 8 * (job % 2)
                act.wait_ge(s_e_ps, job + 1)
                col = (r * 2 + d) * PAIRS + q0
                act.activation(e_chunk[:, :, col:col + 8].rearrange("p s c -> p c s"), bank[job % 4][:, :].rearrange("p (c s) -> p c s", c=8),
                               ACT.Copy).then_inc(s_e, 1)
            act.wait_ge(s_k_out, 16)
            for tau in range(T):
                act.dma_start(m_toep[tau * H:(tau + 1) * H, :, :],
                              k_dram[:, :, (T - 1 - tau) * H:(2 * T - 1 - tau) * H].rearrange("m (g h) n -> h (m g) n", h=H)).then_inc(s_m, 16)

            def gate_sigmoids(i):
                act.wait_ge(s_unit, i * 3 + (U_LOOP + 1))
                for mm in range(2):
                    act.activation(gates[:, bass.ds(i * 2 + mm, 1), :].rearrange("p a t -> p (a t)"), bank[6][:, mm * TOK:(mm + 1) * TOK],
                                   ACT.Sigmoid, bias=par("b_gate")[:, bass.ds(i * 2 + mm, 1)]).then_inc(s_gate, 1)

            with act.Fori(0, LOOPS // 2) as i:
                gate_sigmoids(i)

            act.wait_ge(s_y8_ps, 2)
            for b in range(2):
                act.activation(y_chunk.rearrange("p (q g c) -> p g q c", g=2, c=CH)[:, b], bank[b][:, :].rearrange("p (q c) -> p q c", c=CH),
                               ACT.Copy).then_inc(s_y8, 1)
            act.wait_ge(s_y8, 2)
            for tau in range(T):
                act.dma_start(y_dram[:, :, tau, :].rearrange("m (g h) c -> h (m g) c", h=H),
                              y_chunk[tau * H:(tau + 1) * H, :].rearrange("p (g c) -> p g c", g=G)).then_inc(s_y_out, 16)
            act.wait_ge(s_y_out, 16 * T)
            act.dma_start(y_feat.rearrange("p m t c -> p m (t c)"), y_dram[:].rearrange("m p t c -> p m (t c)")).then_inc(s_yf, 16)

            with act.Fori(LOOPS // 2, LOOPS) as i:
                gate_sigmoids(i)

            act.wait_ge(s_y, KS)
            act.activation(y_gelu.rearrange("p m (c t) -> p m t c", t=T), y_feat, ACT.Gelu_apprx_tanh).then_inc(s_ygelu, 1)
            for m in range(KS):
                act.wait_ge(*((s_unit, U_GLU + 1) if m // 2 else (s_glu_ps, 1)))
                act.activation(glu_gate[:, m, :], bank[2 + m // 2][:, (m % 2) * TOK:(m % 2 + 1) * TOK], ACT.Sigmoid,
                               bias=par("b_glu")[:, m:m + 1]).then_inc(s_glu, 1)

            for k in range(KD):
                act.wait_ge(s_x1, k + 1)
                if k >= 2:
                    act.wait_ge(s_sq_used, KD + k - 1)
                act.activation(squares[:, k % 2, 0:TOK], x_sb[:, k, :], ACT.Square).then_inc(s_sq, 1)
            act.wait_ge(s_sq_used, 2 * KD)
            act.activation(rstd[:, 0:TOK], bank[4][:, 0:TOK], ACT.Sqrt, scale=1.0 / D, bias=EPS).then_inc(s_std, 1)
            act.wait_ge(s_scale2, 1)
            for k in range(KD):
                act.wait_ge(s_norm2, k + 1)
                act.activation(h2[:, k, :], h2[:, k, :], ACT.Identity, scale=scale2[:, k:k + 1],
                               bias=mod2[:, KD + k:KD + k + 1]).then_inc(s_h2, 1)

            for j in range(KF + 1):
                if j < KF:
                    if j >= 2:
                        act.wait_ge(s_conv, CONV_OPS * (j - 1))
                    act.wait_ge(s_up_used, j + 1)
                    act.activation(up_sb[:, j % 2, :], bank[(j % USLOTS) % 3][:, :], ACT.Copy).then_inc(s_upsb, 1)
                if j >= 1:
                    act.wait_ge(s_conv, CONV_OPS * j)
                    if j >= 3:
                        act.wait_ge(s_act, j)
                    act.activation(silu_sb[:, (j - 1) % 2, :], conv[:, (j - 1) % 2, 0:TOK], ACT.Silu).then_inc(s_silu, 1)

            for k in range(KD):
                act.wait_ge(s_x2, k + 1)
                if k >= 2:
                    act.wait_ge(s_sq_used, 2 * KD + k - 1)
                act.activation(squares[:, k % 2, 0:TOK], x_sb[:, k, :], ACT.Square).then_inc(s_sq, 1)
            act.wait_ge(s_sq_used, 3 * KD)
            act.activation(rstd[:, 0:TOK], bank[3][:, 0:TOK], ACT.Sqrt, scale=1.0 / D, bias=EPS).then_inc(s_std, 1)

        @block.vector
        def _(dve):
            count = [0]

            def mark(ins):
                count[0] += 1
                ins.then_inc(s_dve, 1)

            def settle():
                dve.wait_ge(s_dve, count[0])

            def tt(o, a, b, op):
                mark(dve.tensor_tensor(o, a, b, op))

            def ts(o, a, s1, s2, op0, op1=None):
                mark(dve.tensor_scalar(o, a, s1, s2, op0, op1) if op1 is not None else dve.tensor_scalar(o, a, s1, None, op0))

            def col(i):
                return small[:, i * DP:(i + 1) * DP]

            are, aim = a_raw[:, 0:DP], a_raw[:, DP:2 * DP]
            dt, re_dt, mag, phase, red, sin, sinh = (col(i) for i in range(7))
            t0, t1, t2, t3, k_re, k_im, den, turns = (col(i) for i in range(7, 15))

            dve.wait_ge(s_raw, 48)
            dve.wait_ge(s_trig, 1)
            dve.tensor_tensor(re_dt, are, dt, ALU.mult).then_inc(s_trig_in, 1)
            tt(phase, aim, dt, ALU.mult)
            settle()
            ts(turns, phase, 1.0 / TWO_PI, None, ALU.mult)
            settle()
            ts(t0, turns, ROUND_MAGIC, ROUND_MAGIC, ALU.add, ALU.subtract)
            rest, parts = TWO_PI, []
            for _ in range(3):
                e = np.floor(np.log2(rest))
                part = np.floor(rest / 2.0 ** (e - 7)) * 2.0 ** (e - 7)
                parts.append(float(part))
                rest -= part
            parts.append(float(rest))
            cur = phase
            for i, part in enumerate(parts):
                settle()
                nxt = (t1, t2, t1, t2)[i]
                mark(dve.scalar_tensor_tensor(out=nxt, in0=t0, scalar=-part, in1=cur, op0=ALU.mult, op1=ALU.add))
                cur = nxt
            settle()
            dve.tensor_scalar(red, cur, float(np.float32(3.1415925)), float(np.float32(-3.1415925)), ALU.min, ALU.max).then_inc(s_trig_in, 1)
            dve.wait_ge(s_trig, 4)
            tt(t0, sinh, sinh, ALU.mult)
            settle()
            ts(t1, t0, -2.0, 1.0, ALU.mult, ALU.add)
            mark(dve.memset(power[:, 0, 0, :], 1.0))
            mark(dve.memset(power[:, 1, 0, :], 0.0))
            settle()
            p_re, p_im = power[:, 0], power[:, 1]
            tt(p_re[:, 1, :], mag, t1, ALU.mult)
            tt(p_im[:, 1, :], mag, sin, ALU.mult)
            tt(t2, are, are, ALU.mult)
            tt(t3, aim, aim, ALU.mult)
            settle()
            tt(den, t2, t3, ALU.add)
            ts(t0, p_re[:, 1, :], -1.0, None, ALU.add)
            settle()
            mark(dve.reciprocal(turns, den))
            tt(t1, t0, are, ALU.mult)
            tt(t2, p_im[:, 1, :], aim, ALU.mult)
            tt(t3, p_im[:, 1, :], are, ALU.mult)
            tt(phase, t0, aim, ALU.mult)
            settle()
            tt(t1, t1, t2, ALU.add)
            tt(t3, t3, phase, ALU.subtract)
            settle()
            tt(k_re, t1, turns, ALU.mult)
            tt(k_im, t3, turns, ALU.mult)
            settle()

            def cmul(o_re, o_im, a_re, a_im, b_re, b_im, s_a, s_b):
                tt(s_a, a_re, b_re, ALU.mult)
                tt(s_b, a_im, b_im, ALU.mult)
                settle()
                tt(o_re, s_a, s_b, ALU.subtract)
                settle()
                tt(s_a, a_re, b_im, ALU.mult)
                tt(s_b, a_im, b_re, ALU.mult)
                settle()
                tt(o_im, s_a, s_b, ALU.add)
                settle()

            sa = scratch[:, 0:DP * H].rearrange("p (c h) -> p c h", h=H)
            sb_ = scratch[:, DP * H:2 * DP * H].rearrange("p (c h) -> p c h", h=H)

            def over_h(a):
                return a.unsqueeze(2).broadcast_to([P, DP, H])

            cmul(b_bar[:, 0], b_bar[:, 1], over_h(k_re), over_h(k_im), b_raw[:, 0], b_raw[:, 1], sa, sb_)
            for lo, n in ((1, 1), (2, 2), (4, 4)):
                def lead(r):
                    return power[:, r, lo, :].unsqueeze(1).broadcast_to([P, n, DP])
                def rest_(r):
                    return power[:, r, 1:1 + n, :]
                q_a = scratch[:, 0:n * DP].rearrange("p (e c) -> p e c", e=n)
                q_b = scratch[:, 512:512 + n * DP].rearrange("p (e c) -> p e c", e=n)
                cmul(power[:, 0, lo + 1:lo + 1 + n, :], power[:, 1, lo + 1:lo + 1 + n, :], lead(0), lead(1), rest_(0), rest_(1), q_a, q_b)
            a8_re, a8_im = power[:, 0, T, :], power[:, 1, T, :]
            mark(dve.tensor_copy(a_same[:, 0:DP], a8_re))
            mark(dve.tensor_copy(a_same[:, DP:2 * DP], a8_re))
            mark(dve.tensor_copy(a_cross[:, 0:DP], a8_im))
            ts(a_cross[:, DP:2 * DP], a8_im, -1.0, None, ALU.mult)

            def over_q_h(r, d):
                pw = power[:, r, 0:T, d * PAIRS:(d + 1) * PAIRS]
                if d == 0:
                    pw = pw[:, ::-1, :]
                return pw.rearrange("p e c -> p c e").unsqueeze(3)

            s_big = scratch[:, 0:PAIRS * T * H].rearrange("p (q t h) -> p q t h", q=PAIRS, t=T)
            for d in range(2):
                def pw(r):
                    return over_q_h(r, d).broadcast_to([P, PAIRS, T, H])

                def bb(r):
                    return b_bar[:, r, d * PAIRS:(d + 1) * PAIRS, :].unsqueeze(2).broadcast_to([P, PAIRS, T, H])

                tt(w_src[:, d, 0], bb(0), pw(0), ALU.mult)
                tt(s_big, bb(1), pw(1), ALU.mult)
                settle()
                dve.tensor_tensor(w_src[:, d, 0], w_src[:, d, 0], s_big, ALU.subtract).then_inc(s_wsrc, 1)
                dve.wait_ge(s_wsrc, 2 * d + 1)
                tt(w_src[:, d, 1], bb(0), pw(1), ALU.mult)
                tt(s_big, bb(1), pw(0), ALU.mult)
                settle()
                dve.tensor_tensor(w_src[:, d, 1], w_src[:, d, 1], s_big, ALU.add).then_inc(s_wsrc, 1)
                dve.wait_ge(s_wsrc, 2 * d + 2)
            dve.wait_ge(s_pad, 1)
            for g2 in range(2):
                rows = slice(g2 * N, (g2 + 1) * N)
                for r in range(2):
                    ins = dve.tensor_copy(b_pad[rows, r, :, g2, :], b_bar[rows, r])
                    if (g2, r) == (1, 1):
                        ins.then_inc(s_bpad, 1)
                    else:
                        mark(ins)

            dve.wait_ge(s_unit, U_INU)
            dve.wait_ge(s_pk, 16)
            dve.tensor_tensor(mod1, bank[6][:, 0:4 * KD].rearrange("p (m v) -> p m v", v=2),
                              par("b_ada")[:, 0:2 * KD].unsqueeze(2).broadcast_to([P, 2 * KD, 2]), ALU.add).then_inc(s_mod1, 1)
            dve.wait_ge(s_std, 1)
            mark(dve.reciprocal(rstd[:, :], rstd[:, :]))
            dve.wait_ge(s_mod1, 1)
            dve.scalar_tensor_tensor(out=scale1, in0=mod1[:, KD:2 * KD, :], scalar=1.0,
                                     in1=par("g_mix").unsqueeze(2).broadcast_to([P, KD, 2]), op0=ALU.add, op1=ALU.mult).then_inc(s_scale1, 1)
            settle()
            for src, h, off in ((ctx_sb, h_c, 0), (x_sb, h_x, TOK)):
                for k in range(KD):
                    dve.tensor_tensor(h[:, k, :], src[:, k, :], rstd[:, off:off + TOK], ALU.mult).then_inc(s_norm, 1)

            dve.wait_ge(s_tr, 16)
            E1 = T + 1
            c_big = scratch[:, 0:PAIRS * E1 * H].rearrange("p (q t h) -> p q t h", q=PAIRS, t=E1)
            for d in range(2):
                def pe_(r):
                    pw_ = power[:, r, :, d * PAIRS:(d + 1) * PAIRS]
                    if d == 1:
                        pw_ = pw_[:, ::-1, :]
                    return pw_.rearrange("p e c -> p c e").unsqueeze(3).broadcast_to([P, PAIRS, E1, H])

                def cc(r):
                    return c_raw[:, r, d * PAIRS:(d + 1) * PAIRS, :].unsqueeze(2).broadcast_to([P, PAIRS, E1, H])

                o_re, o_im = (ca[:, r, d * PAIRS:(d + 1) * PAIRS] for r in range(2))
                tt(o_re, cc(0), pe_(0), ALU.mult)
                tt(c_big, cc(1), pe_(1), ALU.mult)
                settle()
                tt(o_re, o_re, c_big, ALU.subtract)
                settle()
                tt(o_im, cc(0), pe_(1), ALU.mult)
                tt(c_big, cc(1), pe_(0), ALU.mult)
                settle()
                dve.scalar_tensor_tensor(out=o_im.rearrange("p q e h -> p (q e h)"), in0=o_im.rearrange("p q e h -> p (q e h)"), scalar=-1.0,
                                         in1=c_big.rearrange("p q e h -> p (q e h)"), op0=ALU.mult, op1=ALU.subtract).then_inc(s_ca, 1)
                dve.wait_ge(s_ca, d + 1)

            for c in range(2):
                dve.wait_ge(s_v, c + 1)
                stats, mean_var = bn[:, 6 * c:6 * c + 6], bn[:, 12 + 2 * c:14 + 2 * c]
                mark(dve.bn_stats(stats, v_tok[:, c, :]))
                settle()
                mark(dve.bn_aggr(mean_var, stats))
                settle()
                dve.tensor_scalar(bn[:, 16 + c:17 + c], mean_var[:, 1:2], EPS, None, ALU.add).then_inc(s_lnvar, 1)
            dve.wait_ge(s_lnstd, 2)
            mark(dve.reciprocal(bn[:, 18:20], bn[:, 18:20]))
            dve.wait_ge(s_ln, 64)
            for c in range(2):
                v = v_tok[:, c, :]
                settle()
                ts(v, v, bn[:, 12 + 2 * c:13 + 2 * c], bn[:, 18 + c:19 + c], ALU.subtract, ALU.mult)
                settle()
                tt(v, v, ln_sb[:, 0, :], ALU.mult)
                settle()
                dve.tensor_tensor(v, v, ln_sb[:, 1, :], ALU.add).then_inc(s_vn, 1)

            dve.wait_ge(s_e, 8)
            dve.memset(state[:, :], 0.0).then_inc(s_scan, 1)

            def crossed(h):
                return h.rearrange("p (r c) -> p r c", r=2)[:, ::-1, :]

            def carry_step(h, dst, e, base):
                dve.wait_ge(s_scan, base)
                dve.tensor_tensor(scan_same, a_same, h, ALU.mult).then_inc(s_scan, 1)
                dve.tensor_tensor(crossed(scan_cross), a_cross.rearrange("p (r c) -> p r c", r=2), h.rearrange("p (r c) -> p r c", r=2), ALU.mult).then_inc(s_scan, 1)
                dve.wait_ge(s_scan, base + 1)
                dve.tensor_tensor(scan_same, scan_same, e, ALU.add).then_inc(s_scan, 1)
                dve.wait_ge(s_scan, base + 3)
                dve.tensor_tensor(dst, scan_same, scan_cross, ALU.add).then_inc(s_scan, 1)

            with dve.Fori(0, CH) as s:
                carry_step(state[:, :], state[:, :], e_chunk[:, bass.ds(s, 1), :].rearrange("p a c -> p (a c)"), s * SCAN_OPS + 1)
            dve.wait_ge(s_scan, SCAN_OPS * CH + 1)
            dve.tensor_copy(carry[:, :, 0], state[:, :]).then_inc(s_scan, 1)
            with dve.Fori(0, CH - 1) as s:
                carry_step(carry[:, :, bass.ds(s, 1)].rearrange("p c a -> p (c a)"), carry[:, :, bass.ds(s + 1, 1)].rearrange("p c a -> p (c a)"),
                           e_chunk[:, bass.ds(s + CH, 1), :].rearrange("p a c -> p (a c)"), s * SCAN_OPS + (SCAN_OPS * CH + 2))

            for j in range(4):
                dve.wait_ge(s_sgu_ps, j // 2 + 1)
                if j == 0:
                    dve.wait_ge(s_z, 2)
                t = merge_tmp[:, j % 2, :]
                tt(t.rearrange("p (c q) -> p c q", c=2), bank[4 + j // 2][:, (j % 2) * TOK:(j % 2 + 1) * TOK].rearrange("p (c q) -> p c q", c=2),
                   sgu_b_sb[:, j, :].unsqueeze(1).broadcast_to([P, 2, P]), ALU.add)
                settle()
                dve.tensor_tensor(y_b[:, j, :], z_u[:, j, :], t, ALU.mult).then_inc(s_yb, 1)
            dve.wait_ge(s_yb, 4)

            dve.wait_ge(s_yf, 16)
            for m in range(KS):
                dve.scalar_tensor_tensor(out=y_feat[:, m], in0=u_feat[:, m, :, CH:2 * CH], scalar=par("s5_d")[:, m:m + 1], in1=y_feat[:, m],
                                         op0=ALU.mult, op1=ALU.add).then_inc(s_y, 1)

            dve.wait_ge(s_unit, U_GLU)
            dve.tensor_tensor(mod2[:, :], bank[7][:, 0:4 * KD], par("b_ada")[:, 2 * KD:6 * KD], ALU.add).then_inc(s_mod2, 1)
            dve.wait_ge(s_mod2, 1)
            dve.scalar_tensor_tensor(out=scale2[:, :], in0=mod2[:, 2 * KD:3 * KD], scalar=1.0, in1=par("g_ffn"), op0=ALU.add,
                                     op1=ALU.mult).then_inc(s_scale2, 1)

            for m in range(KS):
                dve.wait_ge(s_glu, m + 1)
                dve.tensor_tensor(y_a[:, m, :], y_gelu[:, m, :], glu_gate[:, m, :], ALU.mult).then_inc(s_ya, 1)

            dve.wait_ge(s_gate, 2 * LOOPS + 1)
            for m in range(KD):
                dve.wait_ge(*((s_unit, U_PROJ + 2 * (m // 4 + 1)) if m % 4 == 3 else (s_pr_ps, m - m // 4 + 1)))
                src = bank[(4, 6, 7, 5)[m % 4]]
                t = merge_tmp[:, 0, :], merge_tmp[:, 1, :]
                tt(t[0], src[:, 0:TOK], gates[:, m, :], ALU.mult)
                tt(t[1], src[:, TOK:2 * TOK], gates[:, KD + m, :], ALU.mult)
                settle()
                dve.tensor_tensor(merged[:, m, :], t[0], t[1], ALU.add).then_inc(s_mg, 1)
                dve.wait_ge(s_mg, m + 1)

            dve.wait_ge(s_xr, 16)
            for m in range(KD):
                dve.wait_ge(s_unit, U_OUT + m // 2 + 1)
                dve.scalar_tensor_tensor(out=x_sb[:, m, :], in0=bank[m // 2][:, (m % 2) * TOK:(m % 2 + 1) * TOK], scalar=mod2[:, m:m + 1],
                                         in1=x_sb[:, m, :], op0=ALU.mult, op1=ALU.add).then_inc(s_x1, 1)
            dve.wait_ge(s_x1, KD)
            dve.wait_ge(s_std, 2)
            mark(dve.reciprocal(rstd[:, 0:TOK], rstd[:, 0:TOK]))
            settle()
            for k in range(KD):
                dve.tensor_tensor(h2[:, k, :], x_sb[:, k, :], rstd[:, 0:TOK], ALU.mult).then_inc(s_norm2, 1)

            taps = [(dy, dx) for dy in (-1, 0, 1) for dx in (-1, 0, 1) if (dy, dx) != (0, 0)]
            cw = par("conv_w").rearrange("p (m k) -> p m k", k=9)
            with dve.Fori(0, KF // 2) as i:
                for b in range(2):
                    base = i * (2 * CONV_OPS) + b * CONV_OPS
                    dve.wait_ge(s_upsb, i * 2 + (b + 2))
                    dve.wait_ge(s_act, i * 2 + (b + 1))
                    src = [up_sb[:, b, half * TOK:(half + 1) * TOK] for half in range(2)]
                    dst = [conv[:, b, half * TOK:(half + 1) * TOK] for half in range(2)]
                    tile = [bass.ds(i * 2 + (b + KF * half), 1) for half in range(2)]
                    for half in range(2):
                        dve.tensor_scalar(dst[half], src[half], cw[:, tile[half], 4], par("conv_b")[:, tile[half]],
                                          ALU.mult, ALU.add).then_inc(s_conv, 1)
                    done = 2
                    for dy, dx in taps:
                        r0, r1 = max(0, -dy), GRID_H - max(0, dy)
                        c0, c1 = max(0, -dx), GRID_W - max(0, dx)
                        for half in range(2):
                            o = dst[half].rearrange("p (r c) -> p r c", c=GRID_W)[:, r0:r1, c0:c1]
                            a = src[half].rearrange("p (r c) -> p r c", c=GRID_W)[:, r0 + dy:r1 + dy, c0 + dx:c1 + dx]
                            dve.wait_ge(s_conv, base + (done - 1))
                            dve.scalar_tensor_tensor(out=o, in0=a, scalar=cw[:, tile[half], (dy + 1) * 3 + dx + 1], in1=o, op0=ALU.mult,
                                                     op1=ALU.add).then_inc(s_conv, 1)
                            done += 1

            for m in range(KD):
                dve.wait_ge(s_dn_ps, m // 2 + 1)
                dve.scalar_tensor_tensor(out=x_sb[:, m, :], in0=bank[4 + m // 2][:, (m % 2) * TOK:(m % 2 + 1) * TOK],
                                         scalar=mod2[:, 3 * KD + m:3 * KD + m + 1], in1=x_sb[:, m, :], op0=ALU.mult, op1=ALU.add).then_inc(s_x2, 1)
            dve.wait_ge(s_x2, KD)
            dve.wait_ge(s_std, 3)
            mark(dve.reciprocal(rstd[:, 0:TOK], rstd[:, 0:TOK]))
            settle()
            for k in range(KD):
                dve.scalar_tensor_tensor(out=x_sb[:, k, :], in0=x_sb[:, k, :], scalar=par("g_final")[:, k:k + 1], in1=rstd[:, 0:TOK],
                                         op0=ALU.mult, op1=ALU.mult).then_inc(s_fin, 1)


_INS = [("x_t", [P, KD * TOK]), ("ctx_t", [P, KD * TOK]), ("pk", [P, PKW]), ("s5raw", [P, S5RAW]), ("log_step", [2, DP]),
        ("ring_w", [UNITS, P, UNIT]), ("up_w", [3 * USLOTS, P, UNIT]), ("ln", [1, 2, S5W]), ("sgu_w", [P, 8, P]), ("sgu_b", [2, 4, P])]


def _tiles(w, m_per_unit):
    k, m = w.shape
    w = w.reshape(k // P, P, m // P // m_per_unit, m_per_unit, P)
    return w.transpose(2, 1, 3, 0, 4).reshape(m // P // m_per_unit, P, -1)


def _features(*vs):
    return [np.asarray(v).reshape(-1, P).T for v in vs]


def kernel(**inputs):
    import concourse.bacc as bacc
    from concourse.bass_utils import run_bass_kernel_spmd

    a = {k: np.asarray(v) for k, v in inputs.items()}
    w_in, w_ada, w_up = a["w_in"][0], a["w_ada"][0], a["w_up"][0]
    ada = _tiles(w_ada, 2)
    w_u, w_zu, w_v, w_gate = w_in[:, :512], w_in[:, 512:1024], w_in[:, 1024:1536], w_in[:, 1536:]
    gate = _tiles(w_gate, 2)
    v_units = w_v.reshape(2, 4, P, 512).transpose(0, 2, 1, 3).reshape(2, P, UNIT)
    loop = np.concatenate([gate[:, None], ada[8:].reshape(LOOPS, 2, P, UNIT)], axis=1).reshape(3 * LOOPS, P, UNIT)
    pa, pb = _tiles(a["w_proj_a"][0], 4), _tiles(a["w_proj_b"][0], 4)
    ring_w = np.concatenate([ada[:8], _tiles(w_u, 2), _tiles(w_zu, 2), v_units, loop, _tiles(a["s5_w_glu"][0], 4),
                             pb[0:1], pa[0:1], pb[1:2], pa[1:2], _tiles(a["w_out"][0], 2)], axis=0)
    up = w_up.reshape(KD, P, 2, KF, P).transpose(3, 1, 2, 0, 4).reshape(KF, P, UNIT)
    down = a["w_down"][0].reshape(KF // 2, 2, P, D).transpose(0, 2, 1, 3).reshape(KF // 2, P, UNIT)
    conv_w = a["conv_w"][0].reshape(9, 2 * KF, P).transpose(2, 1, 0).reshape(P, -1)
    pk = np.concatenate(_features(a["c"][0], a["c_ctx"], a["b_ada"][0], a["g_mix"][0], a["g_ffn"][0], a["g_final"], a["b_gate"][0],
                                  a["s5_b_glu"][0], a["s5_d"][0], a["conv_b"][0]) + [conv_w], axis=1)

    def per_state(v):
        v = v.reshape(2, PAIRS, 2, N, -1)
        return v.transpose(2, 3, 0, 1, 4).reshape(P, -1)

    c_re, c_im = (a[n][0].transpose(0, 1, 3, 2) for n in ("s5_c_re", "s5_c_im"))
    s5raw = np.concatenate([per_state(v) for v in (a["s5_a_re"][0], a["s5_a_im"][0], a["s5_b_re"][0], a["s5_b_im"][0], c_re, c_im)], axis=1)
    log_step = a["s5_log_step"][0].reshape(2, PAIRS, 2).transpose(2, 0, 1).reshape(2, DP)

    def tokens_t(v):
        return v.reshape(TOK, KD, P).transpose(2, 1, 0).reshape(P, -1)

    arrays = {
        "x_t": tokens_t(a["x"][0]), "ctx_t": tokens_t(a["ctx"][0]), "pk": pk, "s5raw": s5raw, "log_step": log_step,
        "ring_w": ring_w, "up_w": np.concatenate([up, down], axis=0),
        "ln": np.stack([a["sgu_ln_g"][0], a["sgu_ln_b"][0]])[None], "sgu_w": a["sgu_w"][0].transpose(2, 0, 1),
        "sgu_b": a["sgu_b"][0].reshape(4, 2, P).transpose(1, 0, 2),
    }
    arrays = {k: np.ascontiguousarray(v) for k, v in arrays.items()}
    nc = bacc.Bacc("TRN2", target_bir_lowering=False, num_devices=1)
    aps = [nc.dram_tensor(name, shape, F32, kind="ExternalInput").ap() for name, shape in _INS]
    out = nc.dram_tensor("out", [P, KD, TOK], F32, kind="ExternalOutput").ap()
    build(nc, *aps, out)
    r = run_bass_kernel_spmd(nc, [arrays], core_ids=[0])
    y = np.asarray(r.results[0]["out"])
    return np.ascontiguousarray(y.transpose(2, 1, 0).reshape(1, TOK, D))
```

```python
from contextlib import ExitStack

import numpy as np

import concourse.bass as bass
from concourse import mybir

F32 = mybir.dt.float32
ALU = mybir.AluOpType
ACT = mybir.ActivationFunctionType

P = 128
D = 1024
KD = D // P
TOK = 256
GRID_W = 64
GRID_H = TOK // GRID_W
S5W = 512
KS = S5W // P
G, H, N = 32, 16, 64
PAIRS = G // 2
CT = 32
NCT = P // CT
T = 8
CH = TOK // T
LAGS = 2 * T - 1
FFN = 2816
KF = FFN // P
NMOD = 6
EPS = 1e-6
TWO_PI = 2.0 * np.pi
ROUND_MAGIC = 12582912.0

RING = 4
UNIT = 2048
U_INU, U_ADA1, U_V, U_ZU, U_LOOP = 0, 2, 4, 6, 8
LOOPS = 4
PART1, PART2 = 2, 1
U_GLU = U_LOOP + 4 * LOOPS
U_PROJ = U_GLU + 1
U_OUT = U_PROJ + 8
UNITS = U_OUT + 8
BLK = 8
USLOTS = 11
UP_ROUNDS = KF // USLOTS

_PK = {}
_at = 0
for _name, _w in [("c", KD), ("c_ctx", KD), ("b_ada", NMOD * KD), ("g_mix", KD), ("g_ffn", KD), ("g_final", KD),
                  ("b_gate", 2 * KD), ("b_glu", KS), ("s5_d", KS), ("conv_b", 2 * KF), ("pick", 2), ("conv_w", 2 * KF * 9)]:
    _PK[_name] = (_at, _at + _w)
    _at += _w
PKW = _at
DP = 2 * PAIRS
S5RAW = DP * 2 + DP * H * 4


def build(nc, x_t, ctx_t, pk, s5raw, log_step, early_w, ring_w, up_w, ln, sgu_w, sgu_b, out):
    with ExitStack() as ctx:
        def sb(name, n):
            return ctx.enter_context(nc.sbuf_tensor(name, [P, n], F32))

        def sem(name):
            return ctx.enter_context(nc.semaphore(name))

        bank = [ctx.enter_context(nc.psum_tensor(f"bank{i}", [P, 512], F32)) for i in range(8)]

        s5_region = sb("s5_region", 8192 + 9216 + 4096 + 4096)
        w_in_s5 = s5_region[:, 0:8192].rearrange("p (d r q m) -> p d r q m", d=2, r=2, q=PAIRS)
        ca_region = s5_region[:, 8192:8192 + 9216]
        w_src = ca_region[:, 0:8192].rearrange("p (d r q t h) -> p d r q t h", d=2, r=2, q=PAIRS, t=T)
        ca = ca_region.rearrange("p (r c e h) -> p r c e h", r=2, c=DP, e=T + 1)
        m_region = s5_region[:, 17408:17408 + 4096]
        scratch = m_region[:, 0:2304]
        b_raw = m_region[:, 2304:2304 + 1024].rearrange("p (r c h) -> p r c h", r=2, c=DP)
        m_toep = m_region.rearrange("p (g m) -> p g m", g=G)
        e_region = s5_region[:, 21504:21504 + 4096]
        c_raw = e_region[:, 0:1024].rearrange("p (r c h) -> p r c h", r=2, c=DP)
        b_bar = e_region[:, 1024:2048].rearrange("p (r c h) -> p r c h", r=2, c=DP)
        b_pad = e_region[:, 2048:4096].rearrange("p (r c g h) -> p r c g h", r=2, c=DP, g=2)
        e_chunk = e_region.rearrange("p (s c) -> p s c", s=2 * CH)
        up_ring = s5_region[:, 0:USLOTS * UNIT].rearrange("p (s n) -> p s n", s=USLOTS)

        x_region = sb("x_region", KD * TOK)
        x_sb = x_region[:, :].rearrange("p (k t) -> p k t", k=KD)
        carry = x_region[:, :].rearrange("p (c s) -> p c s", c=2 * DP)
        ctx_region = sb("ctx_region", KD * TOK)
        ctx_sb = ctx_region[:, :].rearrange("p (k t) -> p k t", k=KD)
        u_chunk = ctx_region[:, :].rearrange("p (g c) -> p g c", g=G)
        y_tok = ctx_region[:, 0:1024]
        y_feat = ctx_region[:, 1024:2048].rearrange("p (m t c) -> p m t c", m=KS, t=T)
        glu_gate = ctx_region[:, 0:1024].rearrange("p (m t) -> p m t", m=KS)
        up_sb = ctx_region[:, 0:1024].rearrange("p (b n) -> p b n", b=2)
        conv = ctx_region[:, 1024:2048].rearrange("p (b n) -> p b n", b=2)
        h_all = sb("h_all", KD * 2 * TOK)[:, :].rearrange("p (k t) -> p k t", k=KD)
        h_x = h_all[:, :, TOK:2 * TOK]
        merged = h_x
        h2 = h_all[:, :, 0:TOK]
        ln_sb = h_all[:, 0:4, 0:TOK]
        sgu_w_sb = h_all[:, 4:8, 0:TOK]
        u_x = sb("u_x", 1024)
        y_gelu = u_x[:, :].rearrange("p (m t) -> p m t", m=KS)
        ring_region = sb("ring_region", RING * UNIT)
        ring = ring_region[:, :].rearrange("p (s n) -> p s n", s=RING)
        ffn_act = ring_region[:, 0:KF * TOK].rearrange("p (j t) -> p j t", j=KF)
        gate_region = sb("gates", 2 * KD * TOK)
        gates = gate_region[:, :].rearrange("p (m t) -> p m t", m=2 * KD)
        u_feat = gate_region[:, 0:2048].rearrange("p (m t c) -> p m t c", m=KS, t=T)
        silu_sb = gates[:, 0:2, :]
        merge_tmp = sb("merge_tmp", 2 * TOK)[:, :].rearrange("p (b t) -> p b t", b=2)
        z_region = sb("z_region", 2048)
        z_u = z_region[:, 0:1024].rearrange("p (m t) -> p m t", m=KS)
        v_tok = z_region[:, 1024:2048].rearrange("p (c n) -> p c n", c=2)
        squares = z_region[:, 1024:2048].rearrange("p (b n) -> p b n", b=2)
        y_b = z_u
        wide_same, wide_cross = z_region[:, 1024:1536], z_region[:, 1536:2048]
        y_a = z_region[:, 1024:2048].rearrange("p (m t) -> p m t", m=KS)
        entering = merge_tmp.rearrange("p b t -> p (b t)")[:, 0:(BLK - 1) * 2 * DP].rearrange("p (b c) -> p b c", c=2 * DP)
        sgu_b_sb = sb("sgu_b_sb", 512)[:, :].rearrange("p (j q) -> p j q", j=4)
        rstd = sb("rstd", 512)
        pk_sb = sb("pk_sb", PKW)
        c_pad = sb("c_pad", KD * CT)[:, :].rearrange("p (k v) -> p k v", k=KD)
        c_silu = c_pad[:, :, 0:2]
        rows1 = merge_tmp
        rows2 = rstd[:, :].rearrange("p (b t) -> p b t", b=2)
        mod1 = sb("mod1", 4 * KD)[:, :].rearrange("p (k a v) -> p k a v", a=2, v=2)
        scale1 = sb("scale1", 2 * KD)[:, :].rearrange("p (k v) -> p k v", v=2)
        mod2 = sb("mod2", 4 * KD)
        scale2 = sb("scale2", KD)
        ones = sb("ones", P)
        ident = sb("ident", P)
        power = sb("power", 2 * (T + 1) * DP)[:, :].rearrange("p (r e c) -> p r e c", r=2, e=T + 1)
        a_raw = sb("a_raw", 3 * DP)
        small = sb("small", 16 * DP)
        cross = small[:, :].rearrange("p (j r c) -> p j r c", j=BLK, r=2)
        bn = sb("bn", 2 * 6 + 2 * 2 + 4)
        k_sb = m_region[:, 0:KS * LAGS * H]

        def par(name):
            a, b = _PK[name]
            return pk_sb[:, a:b]

        early = [gate_region[:, k * UNIT:(k + 1) * UNIT] for k in range(2)] + \
                [s5_region[:, k * UNIT:(k + 1) * UNIT] for k in range(4)] + [ring[:, 2, :], ring[:, 3, :]]

        u_dram = nc.dram_tensor("u_scratch", [KS, P, T, 2 * CH], F32)
        k_dram = nc.dram_tensor("k_scratch", [KS, P, LAGS * H], F32)

        s_pk, s_raw, s_x, s_ctx = sem("pk_loaded"), sem("s5_raw_loaded"), sem("x_loaded"), sem("ctx_loaded")
        s_ls = sem("log_step_loaded")
        s_ring = [sem(f"ring_loaded{i}") for i in range(RING)]
        s_unit = sem("unit_multiplied")
        s_up = [sem(f"up_loaded{i}") for i in range(USLOTS)]
        s_up_used = sem("up_used")
        s_const, s_pad = sem("constants_set"), sem("pad_zeroed")
        s_sq, s_sq_used = sem("squares_ready"), sem("squares_used")
        s_stat, s_std, s_rstd = sem("stat_summed"), sem("std_ready"), sem("rstd_ready")
        s_csilu = sem("c_silu_ready")
        s_early = [sem(f"early_unit_loaded{k}") for k in range(6)]
        s_cpad = sem("c_pad_zeroed")
        s_sqx = sem("squares_of_x_ready")
        s_rows, s_pick = sem("modulation_rows_ready"), sem("modulation_in_psum")
        s_ada_ps, s_mod1, s_scale1 = sem("ada_in_psum"), sem("mod1_ready"), sem("scale1_ready")
        s_norm, s_h = sem("normed_ready"), sem("h_ready")
        s_trig_in, s_trig = sem("trig_args_ready"), sem("act_exp_sin_done")
        s_wsrc, s_tr, s_win = sem("w_src_ready"), sem("transposed"), sem("w_in_evacuated")
        s_ux = sem("u_x_copied")
        s_bpad, s_ca = sem("b_pad_ready"), sem("ca_ready")
        s_u_ps, s_uf, s_u_out, s_uchunk = sem("u_in_psum"), sem("u_feat_ready"), sem("u_stored"), sem("u_chunk_loaded")
        s_z = sem("z_ready")
        s_v_ps, s_v, s_vn = sem("v_in_psum"), sem("v_gelu_ready"), sem("v_normed")
        s_ln = sem("gating_params_loaded")
        s_sgu_ps, s_yb = sem("sgu_in_psum"), sem("y_b_ready")
        s_k_ps, s_k, s_k_out, s_m = sem("k_in_psum"), sem("k_evacuated"), sem("k_stored"), sem("m_loaded")
        s_e_ps, s_e, s_scan = sem("e_in_psum"), sem("e_evacuated"), sem("scan_step")
        s_gate = sem("gate_ready")
        s_mod2, s_scale2 = sem("mod2_ready"), sem("scale2_ready")
        s_y8_ps, s_y8, s_y_tr = sem("y_by_chunk_in_psum"), sem("y_by_chunk_ready"), sem("y_transposed")
        s_y, s_ygelu = sem("y_with_skip_ready"), sem("y_gelu_ready")
        s_glu_ps, s_glu, s_ya = sem("glu_in_psum"), sem("glu_gate_ready"), sem("y_a_ready")
        s_pr_ps, s_mg = sem("proj_in_psum"), sem("merged_ready")
        s_xr = sem("x_reloaded")
        s_x1 = sem("x1_ready")
        s_norm2, s_h2 = sem("normed2_ready"), sem("h2_ready")
        s_up_ps, s_upsb, s_conv = sem("up_in_psum"), sem("up_evacuated"), sem("conv_tap")
        s_silu, s_act = sem("silu_ready"), sem("ffn_act_ready")
        s_dn_ps, s_x2, s_fin, s_stored = sem("down_in_psum"), sem("x2_ready"), sem("final_ready"), sem("out_stored")
        s_dve = sem("dve_chain")
        s_pool = sem("pool_chain")
        s_lnvar, s_lnstd = sem("ln_variance_ready"), sem("ln_deviation_ready")

        PROJ_BANK = (4, 5, 7, 0)
        OUT_BANK = (1, 2, 4, 5)
        CONV_OPS = 18
        block = ctx.enter_context(nc.Block())

        def ring_ready(pe, u):
            pe.wait_ge(s_ring[u % RING], 16 * (u // RING + 1))

        @block.sync
        def _(sp):
            sp.dma_start(x_region[:, :], x_t).then_inc(s_x, 16)
            sp.dma_start(ctx_region[:, :], ctx_t).then_inc(s_ctx, 16)
            for u in range(2):
                sp.dma_start(ring[:, u, :], ring_w[u]).then_inc(s_ring[u], 16)
            for k in range(6):
                sp.dma_start(early[k], early_w[k]).then_inc(s_early[k], 16)
            for u in range(2, RING):
                sp.dma_start(ring[:, u, :], ring_w[u]).then_inc(s_ring[u], 16)
            sp.wait_ge(s_unit, RING)
            for u in range(RING, 2 * RING):
                sp.dma_start(ring[:, u % RING, :], ring_w[u]).then_inc(s_ring[u % RING], 16)
            full = UNITS // RING
            with sp.Fori(2, full) as i:
                for s in range(RING):
                    sp.wait_ge(s_unit, i * RING + (s - RING + 1))
                    sp.dma_start(ring[:, s, :], ring_w[bass.ds(i * RING + s, 1)].rearrange("a p n -> p (a n)")).then_inc(s_ring[s], 16)
            for u in range(full * RING, UNITS):
                sp.wait_ge(s_unit, u - RING + 1)
                sp.dma_start(ring[:, u % RING, :], ring_w[u]).then_inc(s_ring[u % RING], 16)
            sp.wait_ge(s_y8_ps, 2)
            for s in range(USLOTS):
                sp.dma_start(up_ring[:, s, :], up_w[s]).then_inc(s_up[s], 16)
            with sp.Fori(1, UP_ROUNDS + 1) as r:
                for s in range(USLOTS):
                    sp.wait_ge(s_up_used, r * USLOTS + (s - USLOTS + 1))
                    sp.dma_start(up_ring[:, s, :], up_w[bass.ds(r * USLOTS + s, 1)].rearrange("a p n -> p (a n)")).then_inc(s_up[s], 16)
            for m in range(KD):
                sp.wait_ge(s_fin, m + 1)
                sp.dma_start(out[:, m, :], x_sb[:, m, :]).then_inc(s_stored, 16)
            sp.wait_ge(s_stored, 16 * KD)

        @block.gpsimd
        def _(pool):
            pool.memset(ones[:, :], 1.0).then_inc(s_const, 1)
            pool.memset(c_pad, 0.0).then_inc(s_cpad, 1)
            pool.memset(ident[:, :], 0.0).then_inc(s_pool, 1)
            pool.wait_ge(s_pool, 1)
            pool.affine_select(out=ident[:, :], in_=ident[:, :], compare_op=ALU.not_equal, fill=1.0, base=0,
                               pattern=[[-1, P]], channel_multiplier=1).then_inc(s_const, 1)
            pool.memset(b_pad, 0.0).then_inc(s_pad, 1)
            pool.dma_start(sgu_b_sb[0:64, :, :], sgu_b[0:1].partition_broadcast(64)).then_inc(s_ln, 16)
            pool.dma_start(sgu_b_sb[64:128, :, :], sgu_b[1:2].partition_broadcast(64)).then_inc(s_ln, 16)
            pool.wait_ge(s_unit, U_V)
            pool.dma_start(ln_sb, ln.partition_broadcast(P)).then_inc(s_ln, 16)
            pool.dma_start(sgu_w_sb, sgu_w).then_inc(s_ln, 16)
            pool.wait_ge(s_y8_ps, 2)
            pool.dma_start(x_region[:, :], x_t).then_inc(s_xr, 16)
            pool.sem_inc(s_act, 2)
            with pool.Fori(0, KF // 2) as i:
                for b in range(2):
                    pool.wait_ge(s_silu, i * 2 + (b + 1))
                    pool.tensor_tensor(ffn_act[:, bass.ds(i * 2 + b, 1), :].rearrange("p a t -> p (a t)"), silu_sb[:, b, :],
                                       conv[:, b, TOK:2 * TOK], ALU.mult).then_inc(s_act, 1)

        @block.tensor
        def _(pe):
            pe.wait_ge(s_const, 1)
            for k in range(KD):
                pe.wait_ge(s_sq, k + 1)
                pe.wait_ge(s_sqx, k + 1)
                pe.matmul(bank[7][:, :], ones[:, :], squares[:, k % 2, :], start=(k == 0),
                          stop=(k == KD - 1)).then_inc(s_sq_used, 1)

            pe.wait_ge(s_csilu, 1)

            def modulation_rows(dst, unit, count):
                u3 = unit.rearrange("p (a k n) -> p k a n", a=2, k=KD)
                for k in range(KD):
                    c = k % NCT
                    mx = pe.matmul(dst[c * CT:(c + 1) * CT, :].rearrange("p (a n) -> p a n", a=2), c_pad[:, k, :], u3[:, k],
                                   start=(k < NCT), stop=(k >= KD - NCT), skip_group_check=True)
                mx.then_inc(count, 1)

            def first_rows(k):
                if k < 6:
                    pe.wait_ge(s_early[k], 16)
                else:
                    ring_ready(pe, U_ADA1 + k - 6)
                if k == 3:
                    pe.wait_ge(s_std, 1)
                elif k >= 4:
                    pe.wait_ge(s_mod1, k - 3)
                modulation_rows(bank[4 + k % 4][:, 0:2 * P], early[k], s_ada_ps)

            def first_pick(k):
                pe.wait_ge(s_rows, k + 1)
                for a in range(2):
                    mx = pe.matmul(bank[4 + k % 4][:, 2 * P + 2 * a:2 * P + 2 * a + 2], rows1[:, k % 2, a * P:(a + 1) * P], par("pick"),
                                   start=True, stop=True)
                mx.then_inc(s_pick, 1)

            def u_of_tile(k):
                pe.wait_ge(s_h, 2 * (k + 1))
                for m in range(KS):
                    if k == 0 and m % 2 == 0:
                        ring_ready(pe, U_INU + m // 2)
                    mx = pe.matmul(bank[m][:, :], ring[:, U_INU + m // 2, ((m % 2) * KD + k) * P:((m % 2) * KD + k + 1) * P],
                                   h_all[:, k, :], start=(k == 0), stop=(k == KD - 1))
                    if k == KD - 1:
                        mx.then_inc(s_unit, 1)

            first_rows(0)
            first_rows(1)
            first_pick(0)
            for k in range(KD):
                if k + 2 < KD:
                    first_rows(k + 2)
                if k + 1 < KD:
                    first_pick(k + 1)
                u_of_tile(k)

            pe.wait_ge(s_const, 2)
            job = 0
            for d in range(2):
                for r in range(2):
                    pe.wait_ge(s_wsrc, 2 * d + r + 1)
                    for q0 in range(0, PAIRS, 4):
                        if job >= 2:
                            pe.wait_ge(s_win, job - 1)
                        for q in range(4):
                            mx = pe.transpose(bank[4 + job % 2][:, q * P:(q + 1) * P],
                                              w_src[:, d, r, q0 + q].rearrange("p t h -> p (t h)"), ident[:, :])
                        mx.then_inc(s_tr, 1)
                        job += 1
            n_tr = job

            pe.wait_ge(s_mod1, KD)
            for half in range(2):
                u = U_V + half
                ring_ready(pe, u)
                for c in range(2):
                    for kk in range(KD // 2):
                        k = half * (KD // 2) + kk
                        mx = pe.matmul(bank[6 + c][:, :], h_x[:, k, c * P:(c + 1) * P], ring[:, u % RING, kk * 512:(kk + 1) * 512],
                                       start=(k == 0), stop=(k == KD - 1))
                    if half == 1 and c == 0:
                        mx.then_inc(s_v_ps, 1)
                mx.then_inc(s_unit, 1)

            pe.wait_ge(s_win, n_tr)
            for i in range(2):
                u = U_ZU + i
                ring_ready(pe, u)
                for mm in range(2):
                    for k in range(KD):
                        mx = pe.matmul(bank[4 + i][:, mm * TOK:(mm + 1) * TOK], ring[:, u % RING, (mm * KD + k) * P:(mm * KD + k + 1) * P],
                                       h_x[:, k, :], start=(k == 0), stop=(k == KD - 1))
                mx.then_inc(s_unit, 1)

            pe.wait_ge(s_bpad, 1)
            pe.wait_ge(s_ca, 2)
            pe.wait_ge(s_v, 2)
            for q in range(PAIRS):
                m, row = q // 4, 32 * (q % 4)
                base = (m % 2) * LAGS * H
                for d, e0, j0 in ((1, 1, 0), (0, 0, T - 1)):
                    for r in range(2):
                        mx = pe.matmul(bank[6 + m // 2][row:row + 32, base + j0 * H:base + (j0 + T) * H],
                                       b_pad[:, r, d * PAIRS + q].rearrange("p g h -> p (g h)"),
                                       ca[:, r, d * PAIRS + q, e0:e0 + T, :].rearrange("p e h -> p (e h)"),
                                       start=(d == 1 and r == 0), stop=(d == 0 and r == 1), skip_group_check=True)
                if q % 8 == 7:
                    mx.then_inc(s_k_ps, 1)

            pe.wait_ge(s_uchunk, 16 * T)
            for job in range(8):
                d, r, q0 = job // 4, (job // 2) % 2, 8 * (job % 2)
                if job < 4:
                    pe.wait_ge(s_uf, KS)
                else:
                    pe.wait_ge(s_e, job - 3)
                for q in range(q0, q0 + 8):
                    for g2 in range(2):
                        rhs = u_chunk[:, 2 * q + g2, :].rearrange("p (a c) -> p a c", a=2)
                        if d == 1:
                            rhs = rhs[:, :, ::-1]
                        mx = pe.matmul(bank[job % 4][g2 * N:(g2 + 1) * N, (q - q0) * 2 * CH:(q - q0 + 1) * 2 * CH],
                                       w_in_s5[:, d, r, q, g2 * N:(g2 + 1) * N], rhs, start=True, stop=True)
                mx.then_inc(s_e_ps, 1)

            pe.wait_ge(s_vn, 2)
            pe.wait_ge(s_ln, 64)
            pe.wait_ge(s_k, 2)
            for j in range(4):
                for g2 in range(2):
                    for c in range(2):
                        mx = pe.matmul(bank[6 + j // 2][g2 * 64:(g2 + 1) * 64, (j % 2) * TOK + c * P:(j % 2) * TOK + (c + 1) * P],
                                       v_tok[:, c, (2 * j + g2) * 64:(2 * j + g2 + 1) * 64], sgu_w_sb[:, j, g2 * P:(g2 + 1) * P],
                                       start=True, stop=True)
                if j % 2 == 1:
                    mx.then_inc(s_sgu_ps, 1)

            mod_rows = bank[3][:, 2 * P:4 * P]

            def gates_and_modulation(i):
                for b in range(2):
                    slot = (U_LOOP + 2 * b) % RING
                    pe.wait_ge(s_ring[slot], (i + (U_LOOP // RING + 1)) * 16)
                    modulation_rows(mod_rows, ring[:, slot, :], s_unit)
                    slot = (U_LOOP + 2 * b + 1) % RING
                    pe.wait_ge(s_ring[slot], (i + (U_LOOP // RING + 1)) * 16)
                    pe.wait_ge(s_gate, i * 4 + (2 * b + 1))
                    for mm in range(2):
                        for k in range(KD):
                            mx = pe.matmul(bank[4 + b][:, mm * TOK:(mm + 1) * TOK], ring[:, slot, (mm * KD + k) * P:(mm * KD + k + 1) * P],
                                           h_x[:, k, :], start=(k == 0), stop=(k == KD - 1))
                    mx.then_inc(s_unit, 1)
                    pe.wait_ge(s_rows, i * 2 + (KD + b + 1))
                    for mm in range(2):
                        mx = pe.matmul(bank[3][:, bass.ds(i * 4 + (2 * b + mm), 1)], rows2[:, b, mm * P:(mm + 1) * P], par("pick")[:, 0:1],
                                       start=True, stop=True)
                    mx.then_inc(s_pick, 1)

            def later_rows(u):
                ring_ready(pe, u)
                modulation_rows(mod_rows, ring[:, u % RING, :], s_unit)

            def later_pick(n):
                pe.wait_ge(s_rows, KD + n + 1)
                for mm in range(2):
                    mx = pe.matmul(bank[3][:, 2 * n + mm:2 * n + mm + 1], rows2[:, n % 2, mm * P:(mm + 1) * P], par("pick")[:, 0:1],
                                   start=True, stop=True)
                mx.then_inc(s_pick, 1)

            pe.wait_ge(s_z, 2)
            pe.wait_ge(s_e, 8)
            with pe.Fori(0, PART1) as i:
                gates_and_modulation(i)

            pe.wait_ge(s_m, 16 * T)
            pe.wait_ge(s_scan, 1)
            for g2 in range(2):
                half = slice(g2 * N, (g2 + 1) * N)
                for part in (None, (0, 0, 1), (0, 1, 1), (1, 0, 0), (1, 1, 0)):
                    for j in range(P // H // 2):
                        for m in range(KS):
                            q = m * (P // H // 2) + j
                            dst = bank[g2][m * CH:(m + 1) * CH, j * P:(j + 1) * P]
                            if part is None:
                                pe.matmul(dst, u_chunk[:, 2 * q + g2, CH:2 * CH], m_toep[:, 2 * q + g2, :], start=(j == 0), stop=False,
                                          skip_group_check=True)
                                continue
                            d, r, e0 = part
                            mx = pe.matmul(dst, carry[half, (r * 2 + d) * PAIRS + q, :],
                                           ca[half, r, d * PAIRS + q, e0:e0 + T, :].rearrange("p e h -> p (e h)"),
                                           start=False, stop=(d == 1 and r == 1), skip_group_check=True)
                mx.then_inc(s_y8_ps, 1)

            with pe.Fori(PART1, PART1 + PART2) as i:
                gates_and_modulation(i)

            pe.wait_ge(s_y8, 2)
            for tau in range(T):
                mx = pe.transpose(bank[tau // 4][:, (tau % 4) * P:(tau % 4 + 1) * P], y_tok[:, tau * P:(tau + 1) * P], ident[:, :])
                if tau % 4 == 3:
                    mx.then_inc(s_y_tr, 1)

            with pe.Fori(PART1 + PART2, LOOPS) as i:
                gates_and_modulation(i)

            ring_ready(pe, U_GLU)
            pe.wait_ge(s_ygelu, 1)
            pe.wait_ge(s_yb, 4)
            for m in range(KS):
                for k in range(KS):
                    mx = pe.matmul(bank[(2, 6)[m // 2]][:, (m % 2) * TOK:(m % 2 + 1) * TOK],
                                   ring[:, U_GLU % RING, (m * KS + k) * P:(m * KS + k + 1) * P], y_gelu[:, k, :],
                                   start=(k == 0), stop=(k == KS - 1))
                if m == 1:
                    mx.then_inc(s_glu_ps, 1)
            mx.then_inc(s_unit, 1)

            pe.wait_ge(s_mod2, 1)
            for m in range(KD):
                um = U_PROJ + 4 * (m // 4)
                ub, ua = um + 2, um + 3
                if m % 2 == 0:
                    later_rows(um + (m % 4) // 2)
                dst = bank[PROJ_BANK[m % 4]]
                if m >= 4:
                    pe.wait_ge(s_mg, m - 3)
                elif m == 0:
                    pe.wait_ge(s_gate, 4 * LOOPS + 1)
                elif m == 3:
                    pe.wait_ge(s_y, 2 * KS)
                if m % 4 == 0:
                    ring_ready(pe, ub)
                    ring_ready(pe, ua)
                for half, (u, src) in enumerate(((ub, y_b), (ua, y_a))):
                    if m == 0 and half == 1:
                        pe.wait_ge(s_ya, KS)
                    for k in range(KS):
                        mx = pe.matmul(dst[:, (1 - half) * TOK:(2 - half) * TOK], ring[:, u % RING, ((m % 4) * KS + k) * P:((m % 4) * KS + k + 1) * P],
                                       src[:, k, :], start=(k == 0), stop=(k == KS - 1))
                    if m % 4 == 3 and half == 0:
                        mx.then_inc(s_unit, 1)
                mx.then_inc(s_unit if m % 4 == 3 else s_pr_ps, 1)
                if m % 2 == 1:
                    later_pick(2 * LOOPS + m // 2)

            for i in range(4):
                later_rows(U_OUT + 2 * i)
                u = U_OUT + 2 * i + 1
                ring_ready(pe, u)
                if i == 0:
                    pe.wait_ge(s_mg, KD)
                for mm in range(2):
                    for k in range(KD):
                        mx = pe.matmul(bank[OUT_BANK[i]][:, mm * TOK:(mm + 1) * TOK], ring[:, u % RING, (mm * KD + k) * P:(mm * KD + k + 1) * P],
                                       merged[:, k, :], start=(k == 0), stop=(k == KD - 1))
                mx.then_inc(s_unit, 1)
                later_pick(2 * LOOPS + 4 + i)

            for k in range(KD):
                pe.wait_ge(s_sq, KD + k + 1)
                pe.matmul(bank[6][:, 0:TOK], ones[:, :], squares[:, k % 2, 0:TOK], start=(k == 0),
                          stop=(k == KD - 1)).then_inc(s_sq_used, 1)

            pe.wait_ge(s_h2, KD)
            with pe.Fori(0, UP_ROUNDS) as r:
                for s in range(USLOTS):
                    pe.wait_ge(s_up[s], r * 16 + 16)
                    pe.wait_ge(s_upsb, r * USLOTS + max(1, s - 1))
                    for half in range(2):
                        for k in range(KD):
                            mx = pe.matmul(bank[s % 3][:, half * TOK:(half + 1) * TOK], up_ring[:, s, (half * KD + k) * P:(half * KD + k + 1) * P],
                                           h2[:, k, :], start=(k == 0), stop=(k == KD - 1))
                    mx.then_inc(s_up_used, 1)

            pe.wait_ge(s_h2, KD)
            for k in range(KF):
                s = k // 2
                if k % 2 == 0:
                    pe.wait_ge(s_up[s], 16 * (UP_ROUNDS + 1))
                pe.wait_ge(s_act, k + 3)
                for m in range(KD):
                    mx = pe.matmul(bank[4 + m // 2][:, (m % 2) * TOK:(m % 2 + 1) * TOK],
                                   up_ring[:, s, (k % 2) * D + m * P:(k % 2) * D + (m + 1) * P], ffn_act[:, k, :],
                                   start=(k == 0 and m % 2 == 0), stop=(k == KF - 1), skip_group_check=True)
                    if k == KF - 1 and m % 2 == 1:
                        mx.then_inc(s_dn_ps, 1)

            for k in range(KD):
                pe.wait_ge(s_sq, 2 * KD + k + 1)
                pe.matmul(bank[3][:, 0:TOK], ones[:, :], squares[:, k % 2, 0:TOK], start=(k == 0),
                          stop=(k == KD - 1)).then_inc(s_sq_used, 1)

        @block.scalar
        def _(act):
            act.sem_inc(s_gate, 1)
            act.sem_inc(s_upsb, 1)
            act.dma_start(pk_sb[:, :], pk).then_inc(s_pk, 16)
            act.dma_start(a_raw[:, 0:2 * DP], s5raw[:, 0:2 * DP]).then_inc(s_raw, 16)
            for g2 in range(2):
                act.dma_start(a_raw[g2 * N:(g2 + 1) * N, 2 * DP:3 * DP], log_step[g2:g2 + 1].partition_broadcast(N)).then_inc(s_ls, 16)
            act.dma_start(m_region[:, 2304:2304 + 1024], s5raw[:, 2 * DP:2 * DP + 1024]).then_inc(s_raw, 16)
            act.dma_start(e_region[:, 0:1024], s5raw[:, 2 * DP + 1024:2 * DP + 2048]).then_inc(s_raw, 16)

            act.wait_ge(s_ctx, 16)
            for k in range(KD):
                if k >= 2:
                    act.wait_ge(s_sq_used, k - 1)
                act.activation(squares[:, k % 2, 0:TOK], ctx_sb[:, k, :], ACT.Square).then_inc(s_sq, 1)
            act.wait_ge(s_sq_used, KD)
            act.activation(rstd[:, :], bank[7][:, :], ACT.Sqrt, scale=1.0 / D, bias=EPS).then_inc(s_std, 1)

            act.wait_ge(s_ls, 32)
            act.activation(small[:, 0:DP], a_raw[:, 2 * DP:3 * DP], ACT.Exp).then_inc(s_trig, 1)
            act.wait_ge(s_trig_in, 1)
            act.activation(small[:, 2 * DP:3 * DP], small[:, DP:2 * DP], ACT.Exp).then_inc(s_trig, 1)
            act.wait_ge(s_trig_in, 2)
            act.activation(small[:, 5 * DP:6 * DP], small[:, 4 * DP:5 * DP], ACT.Sin).then_inc(s_trig, 1)
            act.activation(small[:, 6 * DP:7 * DP], small[:, 4 * DP:5 * DP], ACT.Sin, scale=0.5).then_inc(s_trig, 1)

            act.wait_ge(s_pk, 16)
            act.wait_ge(s_cpad, 1)
            act.activation(c_silu.rearrange("p k v -> p v k"), pk_sb[:, 0:2 * KD].rearrange("p (v k) -> p v k", v=2),
                           ACT.Silu).then_inc(s_csilu, 1)

            def first_rows(k):
                act.wait_ge(s_ada_ps, k + 1)
                act.activation(rows1[:, k % 2, :], bank[4 + k % 4][:, 0:2 * P], ACT.Copy).then_inc(s_rows, 1)

            first_rows(0)
            first_rows(1)
            for k in range(KD):
                act.wait_ge(s_scale1, k + 1)
                for v in (1, 0):
                    act.wait_ge(s_norm, 2 * k + 2 - v)
                    part = h_all[:, k, (1 - v) * TOK:(2 - v) * TOK]
                    act.activation(part, part, ACT.Identity, scale=scale1[:, k, v:v + 1], bias=mod1[:, k, 0, v:v + 1]).then_inc(s_h, 1)
                if k + 2 < KD:
                    first_rows(k + 2)

            for m in range(KS):
                act.wait_ge(s_unit, m + 1)
                act.activation(u_feat[:, m, :, :], bank[m][:, :].rearrange("p (c t) -> p t c", t=T), ACT.Copy).then_inc(s_uf, 1)
                act.wait_ge(s_uf, m + 1)
                act.dma_start(u_dram[m].rearrange("p t c -> p (t c)"), u_feat[:, m, :, :].rearrange("p t c -> p (t c)")).then_inc(s_u_out, 16)

            act.wait_ge(s_ada_ps, KD)
            job = 0
            for d in range(2):
                for r in range(2):
                    for q0 in range(0, PAIRS, 4):
                        act.wait_ge(s_tr, job + 1)
                        act.activation(w_in_s5[:, d, r, q0:q0 + 4, :].rearrange("p q m -> p (q m)"), bank[4 + job % 2][:, :],
                                       ACT.Copy).then_inc(s_win, 1)
                        job += 1
                        if job == 4:
                            act.wait_ge(s_u_out, 16 * KS)
                            for tau in range(T):
                                act.dma_start(u_chunk[tau * H:(tau + 1) * H, :, :],
                                              u_dram[:, :, tau, :].rearrange("m (g h) c -> h (m g) c", h=H)).then_inc(s_uchunk, 16)

            for c in range(2):
                act.wait_ge(*((s_unit, U_V + 2) if c else (s_v_ps, 1)))
                act.activation(v_tok[:, c, :], bank[6 + c][:, :], ACT.Gelu_apprx_tanh).then_inc(s_v, 1)
            for i in range(2):
                act.wait_ge(s_unit, U_ZU + i + 1)
                act.activation(z_u[:, 2 * i:2 * i + 2, :].rearrange("p m t -> p (m t)"), bank[4 + i][:, :], ACT.Gelu_apprx_tanh).then_inc(s_z, 1)

            for c in range(2):
                act.wait_ge(s_lnvar, c + 1)
                act.activation(bn[:, 18 + c:19 + c], bn[:, 16 + c:17 + c], ACT.Sqrt).then_inc(s_lnstd, 1)
            for b in range(2):
                act.wait_ge(s_k_ps, b + 1)
                act.activation(k_sb[:, 2 * b * LAGS * H:(2 * b + 2) * LAGS * H], bank[6 + b][:, 0:2 * LAGS * H], ACT.Copy).then_inc(s_k, 1)
            act.wait_ge(s_k, 2)
            act.dma_start(k_dram[:].rearrange("m p n -> p m n"), k_sb[:, :].rearrange("p (m n) -> p m n", m=KS)).then_inc(s_k_out, 16)
            for job in range(8):
                d, r, q0 = job // 4, (job // 2) % 2, 8 * (job % 2)
                act.wait_ge(s_e_ps, job + 1)
                col = (r * 2 + d) * PAIRS + q0
                act.activation(e_chunk[:, :, col:col + 8].rearrange("p s c -> p c s"), bank[job % 4][:, :].rearrange("p (c s) -> p c s", c=8),
                               ACT.Copy).then_inc(s_e, 1)
            act.wait_ge(s_k_out, 16)
            for tau in range(T):
                act.dma_start(m_toep[tau * H:(tau + 1) * H, :, :],
                              k_dram[:, :, (T - 1 - tau) * H:(2 * T - 1 - tau) * H].rearrange("m (g h) n -> h (m g) n", h=H)).then_inc(s_m, 16)

            act.wait_ge(s_ux, 1)

            def gate_sigmoids(i):
                for b in range(2):
                    act.wait_ge(s_unit, i * 4 + (U_LOOP + 2 * b + 1))
                    act.activation(rows2[:, b, :], bank[3][:, 2 * P:4 * P], ACT.Copy).then_inc(s_rows, 1)
                    act.wait_ge(s_unit, i * 4 + (U_LOOP + 2 * b + 2))
                    for mm in range(2):
                        m = i * 4 + (2 * b + mm)
                        act.activation(gates[:, bass.ds(m, 1), :].rearrange("p a t -> p (a t)"), bank[4 + b][:, mm * TOK:(mm + 1) * TOK],
                                       ACT.Sigmoid, bias=par("b_gate")[:, bass.ds(m, 1)]).then_inc(s_gate, 1)

            with act.Fori(0, PART1) as i:
                gate_sigmoids(i)

            act.wait_ge(s_y8_ps, 2)
            for b in range(2):
                act.activation(y_tok.rearrange("p (t g b h) -> p b g t h", t=T, b=2, h=H)[:, b],
                               bank[b][:, :].rearrange("p (g t h) -> p g t h", g=4, t=T), ACT.Copy).then_inc(s_y8, 1)

            with act.Fori(PART1, PART1 + PART2) as i:
                gate_sigmoids(i)

            act.wait_ge(s_y, 2 * KS)
            act.activation(y_gelu.rearrange("p m (c t) -> p m t c", t=T), y_feat, ACT.Gelu_apprx_tanh).then_inc(s_ygelu, 1)

            with act.Fori(PART1 + PART2, LOOPS) as i:
                gate_sigmoids(i)

            for m in range(KS):
                act.wait_ge(*((s_unit, U_GLU + 1) if m // 2 else (s_glu_ps, 1)))
                act.activation(glu_gate[:, m, :], bank[(2, 6)[m // 2]][:, (m % 2) * TOK:(m % 2 + 1) * TOK], ACT.Sigmoid,
                               bias=par("b_glu")[:, m:m + 1]).then_inc(s_glu, 1)

            for n in range(2 * LOOPS, 2 * LOOPS + 8):
                m = n - 2 * LOOPS
                u = U_PROJ + 4 * (m // 2) + m % 2 if m < 4 else U_OUT + 2 * (m - 4)
                act.wait_ge(s_unit, u + 1)
                act.activation(rows2[:, n % 2, :], bank[3][:, 2 * P:4 * P], ACT.Copy).then_inc(s_rows, 1)

            for k in range(KD):
                act.wait_ge(s_x1, k + 1)
                if k >= 2:
                    act.wait_ge(s_sq_used, KD + k - 1)
                act.activation(squares[:, k % 2, 0:TOK], x_sb[:, k, :], ACT.Square).then_inc(s_sq, 1)
            act.wait_ge(s_sq_used, 2 * KD)
            act.activation(rstd[:, 0:TOK], bank[6][:, 0:TOK], ACT.Sqrt, scale=1.0 / D, bias=EPS).then_inc(s_std, 1)
            act.wait_ge(s_scale2, 1)
            for k in range(KD):
                act.wait_ge(s_norm2, k + 1)
                act.activation(h2[:, k, :], h2[:, k, :], ACT.Identity, scale=scale2[:, k:k + 1],
                               bias=mod2[:, KD + k:KD + k + 1]).then_inc(s_h2, 1)

            for j in range(KF + 1):
                if j < KF:
                    if j >= 2:
                        act.wait_ge(s_conv, CONV_OPS * (j - 1))
                    act.wait_ge(s_up_used, j + 1)
                    act.activation(up_sb[:, j % 2, :], bank[(j % USLOTS) % 3][:, :], ACT.Copy).then_inc(s_upsb, 1)
                if j >= 1:
                    act.wait_ge(s_conv, CONV_OPS * j)
                    if j >= 3:
                        act.wait_ge(s_act, j)
                    act.activation(silu_sb[:, (j - 1) % 2, :], conv[:, (j - 1) % 2, 0:TOK], ACT.Silu).then_inc(s_silu, 1)

            for k in range(KD):
                act.wait_ge(s_x2, k + 1)
                if k >= 2:
                    act.wait_ge(s_sq_used, 2 * KD + k - 1)
                act.activation(squares[:, k % 2, 0:TOK], x_sb[:, k, :], ACT.Square).then_inc(s_sq, 1)
            act.wait_ge(s_sq_used, 3 * KD)
            act.activation(rstd[:, 0:TOK], bank[3][:, 0:TOK], ACT.Sqrt, scale=1.0 / D, bias=EPS).then_inc(s_std, 1)

        @block.vector
        def _(dve):
            count = [0]

            def mark(ins):
                count[0] += 1
                ins.then_inc(s_dve, 1)

            def settle():
                dve.wait_ge(s_dve, count[0])

            def tt(o, a, b, op):
                mark(dve.tensor_tensor(o, a, b, op))

            def ts(o, a, s1, s2, op0, op1=None):
                mark(dve.tensor_scalar(o, a, s1, s2, op0, op1) if op1 is not None else dve.tensor_scalar(o, a, s1, None, op0))

            def col(i):
                return small[:, i * DP:(i + 1) * DP]

            are, aim = a_raw[:, 0:DP], a_raw[:, DP:2 * DP]
            dt, re_dt, mag, phase, red, sin, sinh = (col(i) for i in range(7))
            t0, t1, t2, t3, k_re, k_im, den, turns = (col(i) for i in range(7, 15))

            dve.wait_ge(s_x, 16)
            for k in range(KD):
                if k >= 2:
                    dve.wait_ge(s_sq_used, k - 1)
                dve.tensor_tensor(squares[:, k % 2, TOK:2 * TOK], x_sb[:, k, :], x_sb[:, k, :], ALU.mult).then_inc(s_sqx, 1)

            dve.wait_ge(s_raw, 48)
            dve.wait_ge(s_trig, 1)
            dve.tensor_tensor(re_dt, are, dt, ALU.mult).then_inc(s_trig_in, 1)
            tt(phase, aim, dt, ALU.mult)
            settle()
            ts(turns, phase, 1.0 / TWO_PI, None, ALU.mult)
            settle()
            ts(t0, turns, ROUND_MAGIC, ROUND_MAGIC, ALU.add, ALU.subtract)
            rest, parts = TWO_PI, []
            for _ in range(3):
                e = np.floor(np.log2(rest))
                part = np.floor(rest / 2.0 ** (e - 7)) * 2.0 ** (e - 7)
                parts.append(float(part))
                rest -= part
            parts.append(float(rest))
            cur = phase
            for i, part in enumerate(parts):
                settle()
                nxt = (t1, t2, t1, t2)[i]
                mark(dve.scalar_tensor_tensor(out=nxt, in0=t0, scalar=-part, in1=cur, op0=ALU.mult, op1=ALU.add))
                cur = nxt
            settle()
            dve.tensor_scalar(red, cur, float(np.float32(3.1415925)), float(np.float32(-3.1415925)), ALU.min, ALU.max).then_inc(s_trig_in, 1)
            dve.wait_ge(s_trig, 4)
            tt(t0, sinh, sinh, ALU.mult)
            settle()
            ts(t1, t0, -2.0, 1.0, ALU.mult, ALU.add)
            mark(dve.memset(power[:, 0, 0, :], 1.0))
            mark(dve.memset(power[:, 1, 0, :], 0.0))
            settle()
            p_re, p_im = power[:, 0], power[:, 1]
            tt(p_re[:, 1, :], mag, t1, ALU.mult)
            tt(p_im[:, 1, :], mag, sin, ALU.mult)
            tt(t2, are, are, ALU.mult)
            tt(t3, aim, aim, ALU.mult)
            settle()
            tt(den, t2, t3, ALU.add)
            ts(t0, p_re[:, 1, :], -1.0, None, ALU.add)
            settle()
            mark(dve.reciprocal(turns, den))
            tt(t1, t0, are, ALU.mult)
            tt(t2, p_im[:, 1, :], aim, ALU.mult)
            tt(t3, p_im[:, 1, :], are, ALU.mult)
            tt(phase, t0, aim, ALU.mult)
            settle()
            tt(t1, t1, t2, ALU.add)
            tt(t3, t3, phase, ALU.subtract)
            settle()
            tt(k_re, t1, turns, ALU.mult)
            tt(k_im, t3, turns, ALU.mult)
            settle()

            def cmul(o_re, o_im, a_re, a_im, b_re, b_im, s_a, s_b):
                tt(s_a, a_re, b_re, ALU.mult)
                tt(s_b, a_im, b_im, ALU.mult)
                settle()
                tt(o_re, s_a, s_b, ALU.subtract)
                settle()
                tt(s_a, a_re, b_im, ALU.mult)
                tt(s_b, a_im, b_re, ALU.mult)
                settle()
                tt(o_im, s_a, s_b, ALU.add)
                settle()

            sa = scratch[:, 0:DP * H].rearrange("p (c h) -> p c h", h=H)
            sb_ = scratch[:, DP * H:2 * DP * H].rearrange("p (c h) -> p c h", h=H)

            def over_h(a):
                return a.unsqueeze(2).broadcast_to([P, DP, H])

            cmul(b_bar[:, 0], b_bar[:, 1], over_h(k_re), over_h(k_im), b_raw[:, 0], b_raw[:, 1], sa, sb_)
            for lo, n in ((1, 1), (2, 2), (4, 4)):
                def lead(r):
                    return power[:, r, lo, :].unsqueeze(1).broadcast_to([P, n, DP])
                def rest_(r):
                    return power[:, r, 1:1 + n, :]
                q_a = scratch[:, 0:n * DP].rearrange("p (e c) -> p e c", e=n)
                q_b = scratch[:, 512:512 + n * DP].rearrange("p (e c) -> p e c", e=n)
                cmul(power[:, 0, lo + 1:lo + 1 + n, :], power[:, 1, lo + 1:lo + 1 + n, :], lead(0), lead(1), rest_(0), rest_(1), q_a, q_b)
            def over_q_h(r, d):
                pw = power[:, r, 0:T, d * PAIRS:(d + 1) * PAIRS]
                if d == 0:
                    pw = pw[:, ::-1, :]
                return pw.rearrange("p e c -> p c e").unsqueeze(3)

            s_big = scratch[:, 0:PAIRS * T * H].rearrange("p (q t h) -> p q t h", q=PAIRS, t=T)

            def w_source(d, r):
                def pw(x):
                    return over_q_h(x, d).broadcast_to([P, PAIRS, T, H])

                def bb(x):
                    return b_bar[:, x, d * PAIRS:(d + 1) * PAIRS, :].unsqueeze(2).broadcast_to([P, PAIRS, T, H])

                tt(w_src[:, d, r], bb(0), pw(r), ALU.mult)
                tt(s_big, bb(1), pw(1 - r), ALU.mult)
                settle()
                dve.tensor_tensor(w_src[:, d, r], w_src[:, d, r], s_big, ALU.add if r else ALU.subtract).then_inc(s_wsrc, 1)
                dve.wait_ge(s_wsrc, 2 * d + r + 1)

            dve.wait_ge(s_pad, 1)
            for g2 in range(2):
                rows = slice(g2 * N, (g2 + 1) * N)
                for r in range(2):
                    ins = dve.tensor_copy(b_pad[rows, r, :, g2, :], b_bar[rows, r])
                    if (g2, r) == (1, 1):
                        ins.then_inc(s_bpad, 1)
                    else:
                        mark(ins)

            dve.wait_ge(s_pk, 16)
            dve.wait_ge(s_std, 1)
            mark(dve.reciprocal(rstd[:, :], rstd[:, :]))
            settle()
            for k in range(KD):
                for src, off in ((ctx_sb, 0), (x_sb, TOK)):
                    dve.tensor_tensor(h_all[:, k, off:off + TOK], src[:, k, :], rstd[:, off:off + TOK], ALU.mult).then_inc(s_norm, 1)
                dve.wait_ge(s_pick, k + 1)
                dve.tensor_tensor(mod1[:, k], bank[4 + k % 4][:, 2 * P:2 * P + 4].rearrange("p (a v) -> p a v", v=2),
                                  par("b_ada")[:, k:k + KD + 1:KD].unsqueeze(2).broadcast_to([P, 2, 2]), ALU.add).then_inc(s_mod1, 1)
                dve.wait_ge(s_mod1, k + 1)
                dve.tensor_scalar(scale1[:, k, :], mod1[:, k, 1, :], 1.0, par("g_mix")[:, k:k + 1], ALU.add, ALU.mult).then_inc(s_scale1, 1)
                if k % 2 == 1:
                    w_source(k // 4, (k // 2) % 2)

            dve.wait_ge(s_tr, 16)
            E1 = T + 1
            c_big = scratch[:, 0:PAIRS * E1 * H].rearrange("p (q t h) -> p q t h", q=PAIRS, t=E1)
            for d in range(2):
                def pe_(r):
                    pw_ = power[:, r, :, d * PAIRS:(d + 1) * PAIRS]
                    if d == 1:
                        pw_ = pw_[:, ::-1, :]
                    return pw_.rearrange("p e c -> p c e").unsqueeze(3).broadcast_to([P, PAIRS, E1, H])

                def cc(r):
                    return c_raw[:, r, d * PAIRS:(d + 1) * PAIRS, :].unsqueeze(2).broadcast_to([P, PAIRS, E1, H])

                o_re, o_im = (ca[:, r, d * PAIRS:(d + 1) * PAIRS] for r in range(2))
                tt(o_re, cc(0), pe_(0), ALU.mult)
                tt(c_big, cc(1), pe_(1), ALU.mult)
                settle()
                tt(o_re, o_re, c_big, ALU.subtract)
                settle()
                tt(o_im, cc(0), pe_(1), ALU.mult)
                tt(c_big, cc(1), pe_(0), ALU.mult)
                settle()
                dve.scalar_tensor_tensor(out=o_im.rearrange("p q e h -> p (q e h)"), in0=o_im.rearrange("p q e h -> p (q e h)"), scalar=-1.0,
                                         in1=c_big.rearrange("p q e h -> p (q e h)"), op0=ALU.mult, op1=ALU.subtract).then_inc(s_ca, 1)
                dve.wait_ge(s_ca, d + 1)

            for c in range(2):
                dve.wait_ge(s_v, c + 1)
                stats, mean_var = bn[:, 6 * c:6 * c + 6], bn[:, 12 + 2 * c:14 + 2 * c]
                mark(dve.bn_stats(stats, v_tok[:, c, :]))
                settle()
                mark(dve.bn_aggr(mean_var, stats))
                settle()
                dve.tensor_scalar(bn[:, 16 + c:17 + c], mean_var[:, 1:2], EPS, None, ALU.add).then_inc(s_lnvar, 1)
            dve.wait_ge(s_lnstd, 2)
            mark(dve.reciprocal(bn[:, 18:20], bn[:, 18:20]))
            dve.wait_ge(s_ln, 64)
            for c in range(2):
                v = v_tok[:, c, :]
                settle()
                ts(v, v, bn[:, 12 + 2 * c:13 + 2 * c], bn[:, 18 + c:19 + c], ALU.subtract, ALU.mult)
                settle()
                v2 = v.rearrange("p (a n) -> p a n", a=2)
                tt(v2, v2, ln_sb[:, 0:2, :], ALU.mult)
                settle()
                dve.tensor_tensor(v2, v2, ln_sb[:, 2:4, :], ALU.add).then_inc(s_vn, 1)

            dve.wait_ge(s_uf, KS)
            dve.tensor_copy(u_x[:, :].rearrange("p (m c) -> p m c", c=CH), u_feat.rearrange("p m t c -> p (m t) c")[:, :, CH:2 * CH]).then_inc(s_ux, 1)

            for r in range(2):
                mark(dve.tensor_copy(power[:, r, 0, :], power[:, r, T, :]))
            settle()
            for lo, n in ((1, 1), (2, 2), (4, 4)):
                q_a = merge_tmp[:, 0, 0:n * DP].rearrange("p (e c) -> p e c", e=n)
                q_b = merge_tmp[:, 1, 0:n * DP].rearrange("p (e c) -> p e c", e=n)
                lead = [power[:, r, lo - 1, :].unsqueeze(1).broadcast_to([P, n, DP]) for r in range(2)]
                rest8 = [power[:, r, 0:n, :] for r in range(2)]
                cmul(power[:, 0, lo:lo + n, :], power[:, 1, lo:lo + n, :], lead[0], lead[1], rest8[0], rest8[1], q_a, q_b)
            mark(dve.tensor_copy(cross[:, :, 0, :], power[:, 1, 0:BLK, :]))
            ts(cross[:, :, 1, :], power[:, 1, 0:BLK, :], -1.0, None, ALU.mult)

            dve.wait_ge(s_e, 8)
            dve.wait_ge(s_sgu_ps, 2)
            blocks = e_chunk.rearrange("p (b j) (r c) -> p j b r c", j=BLK, r=2)
            wide = [P, BLK, 2, DP]
            t_s = wide_same.rearrange("p (b r c) -> p b r c", b=BLK, r=2)
            t_c = wide_cross.rearrange("p (b r c) -> p b r c", b=BLK, r=2)
            q1 = power[:, 0, 0, :].unsqueeze(1).unsqueeze(1).broadcast_to(wide)
            x1 = cross[:, 0].unsqueeze(1).broadcast_to(wide)
            settle()
            for j in range(1, BLK):
                h = blocks[:, j - 1]
                tt(t_s, q1, h, ALU.mult)
                tt(t_c[:, :, ::-1, :], x1, h, ALU.mult)
                dve.wait_ge(s_dve, count[0] - 1)
                tt(blocks[:, j], blocks[:, j], t_s, ALU.add)
                settle()
                tt(blocks[:, j], blocks[:, j], t_c, ALU.add)
                settle()
            ends = blocks[:, BLK - 1]
            enter = entering.rearrange("p b (r c) -> p b r c", r=2)
            q8 = power[:, 0, BLK - 1, :].unsqueeze(1).broadcast_to([P, 2, DP])
            n_s, n_c = t_s[:, 0], t_c[:, 0]
            mark(dve.tensor_copy(enter[:, 0], ends[:, 0]))
            settle()
            for b in range(1, BLK - 1):
                tt(n_s, q8, enter[:, b - 1], ALU.mult)
                tt(n_c[:, ::-1, :], cross[:, BLK - 1], enter[:, b - 1], ALU.mult)
                dve.wait_ge(s_dve, count[0] - 1)
                tt(enter[:, b], ends[:, b], n_s, ALU.add)
                settle()
                tt(enter[:, b], enter[:, b], n_c, ALU.add)
                settle()
            NJ = BLK - 1
            first = 2 * CH // BLK // 2
            carry4 = carry.rearrange("p (r c) s -> p r c s", r=2)
            qj = power[:, 0, 0:NJ, :].rearrange("p j c -> p c j").unsqueeze(1).broadcast_to([P, 2, DP, NJ])
            xj = cross[:, 0:NJ].rearrange("p j r c -> p r c j")
            for b in range(CH // BLK):
                h_in = enter[:, first + b - 1].unsqueeze(3).broadcast_to([P, 2, DP, NJ])
                t_sj = wide_same[:, 0:NJ * 2 * DP].rearrange("p (r c j) -> p r c j", r=2, j=NJ)
                t_cj = wide_cross[:, 0:NJ * 2 * DP].rearrange("p (r c j) -> p r c j", r=2, j=NJ)
                local = e_chunk[:, (first + b) * BLK:(first + b) * BLK + NJ, :].rearrange("p j (r c) -> p r c j", r=2)
                by_dir = [(slice(0, PAIRS), carry4[:, :, 0:PAIRS, :]), (slice(PAIRS, DP), carry4[:, :, PAIRS:DP, ::-1])]
                for cols, c4 in by_dir:
                    mark(dve.tensor_copy(c4[:, :, :, b * BLK], enter[:, first + b - 1][:, :, cols]))
                settle()
                tt(t_sj, qj, h_in, ALU.mult)
                tt(t_cj[:, ::-1], xj, h_in, ALU.mult)
                settle()
                for cols, c4 in by_dir:
                    tt(c4[:, :, :, b * BLK + 1:(b + 1) * BLK], local[:, :, cols], t_sj[:, :, cols], ALU.add)
                settle()
                for cols, c4 in by_dir:
                    dst = c4[:, :, :, b * BLK + 1:(b + 1) * BLK]
                    ins = dve.tensor_tensor(dst, dst, t_cj[:, :, cols], ALU.add)
                    if b == CH // BLK - 1 and cols.stop == DP:
                        ins.then_inc(s_scan, 1)
                    else:
                        mark(ins)

            for j in range(4):
                dve.wait_ge(s_sgu_ps, j // 2 + 1)
                if j == 0:
                    dve.wait_ge(s_z, 2)
                t = merge_tmp[:, j % 2, :]
                tt(t.rearrange("p (c q) -> p c q", c=2), bank[6 + j // 2][:, (j % 2) * TOK:(j % 2 + 1) * TOK].rearrange("p (c q) -> p c q", c=2),
                   sgu_b_sb[:, j, :].unsqueeze(1).broadcast_to([P, 2, P]), ALU.add)
                settle()
                dve.tensor_tensor(y_b[:, j, :], z_u[:, j, :], t, ALU.mult).then_inc(s_yb, 1)
            dve.wait_ge(s_yb, 4)

            for b in range(2):
                dve.wait_ge(s_y_tr, b + 1)
                y_ps = bank[b][:, :].rearrange("p (t m c) -> p m t c", t=4, m=KS)
                for m in range(KS):
                    dve.scalar_tensor_tensor(out=y_feat[:, m, 4 * b:4 * b + 4], in0=u_x[:, m * TOK:(m + 1) * TOK].rearrange("p (t c) -> p t c", t=T)[:, 4 * b:4 * b + 4],
                                             scalar=par("s5_d")[:, m:m + 1], in1=y_ps[:, m], op0=ALU.mult, op1=ALU.add).then_inc(s_y, 1)

            dve.wait_ge(s_pick, KD + 2 * LOOPS)
            dve.tensor_tensor(mod2[:, 0:2 * KD], bank[3][:, 0:2 * KD], par("b_ada")[:, 2 * KD:4 * KD], ALU.add).then_inc(s_mod2, 1)

            for m in range(KS):
                dve.wait_ge(s_glu, m + 1)
                dve.tensor_tensor(y_a[:, m, :], y_gelu[:, m, :], glu_gate[:, m, :], ALU.mult).then_inc(s_ya, 1)

            dve.wait_ge(s_gate, 4 * LOOPS + 1)
            for m in range(KD):
                dve.wait_ge(*((s_unit, U_PROJ + 4 * (m // 4) + 4) if m % 4 == 3 else (s_pr_ps, m - m // 4 + 1)))
                src = bank[PROJ_BANK[m % 4]]
                t = merge_tmp[:, 0, :], merge_tmp[:, 1, :]
                tt(t[0], src[:, 0:TOK], gates[:, m, :], ALU.mult)
                tt(t[1], src[:, TOK:2 * TOK], gates[:, KD + m, :], ALU.mult)
                settle()
                dve.tensor_tensor(merged[:, m, :], t[0], t[1], ALU.add).then_inc(s_mg, 1)
                dve.wait_ge(s_mg, m + 1)

            dve.wait_ge(s_xr, 16)
            dve.wait_ge(s_mod2, 1)
            for m in range(KD):
                if m == KD - 2:
                    dve.wait_ge(s_pick, KD + 2 * LOOPS + 8)
                    dve.tensor_tensor(mod2[:, 2 * KD:4 * KD], bank[3][:, 2 * KD:4 * KD], par("b_ada")[:, 4 * KD:6 * KD],
                                      ALU.add).then_inc(s_mod2, 1)
                    dve.wait_ge(s_mod2, 2)
                    dve.scalar_tensor_tensor(out=scale2[:, :], in0=mod2[:, 2 * KD:3 * KD], scalar=1.0, in1=par("g_ffn"), op0=ALU.add,
                                             op1=ALU.mult).then_inc(s_scale2, 1)
                dve.wait_ge(s_unit, U_OUT + 2 * (m // 2) + 2)
                dve.scalar_tensor_tensor(out=x_sb[:, m, :], in0=bank[OUT_BANK[m // 2]][:, (m % 2) * TOK:(m % 2 + 1) * TOK], scalar=mod2[:, m:m + 1],
                                         in1=x_sb[:, m, :], op0=ALU.mult, op1=ALU.add).then_inc(s_x1, 1)
            dve.wait_ge(s_x1, KD)
            dve.wait_ge(s_std, 2)
            mark(dve.reciprocal(rstd[:, 0:TOK], rstd[:, 0:TOK]))
            settle()
            for k in range(KD):
                dve.tensor_tensor(h2[:, k, :], x_sb[:, k, :], rstd[:, 0:TOK], ALU.mult).then_inc(s_norm2, 1)

            taps = [(dy, dx) for dy in (-1, 0, 1) for dx in (-1, 0, 1) if (dy, dx) != (0, 0)]
            cw = par("conv_w").rearrange("p (m k) -> p m k", k=9)
            with dve.Fori(0, KF // 2) as i:
                for b in range(2):
                    base = i * (2 * CONV_OPS) + b * CONV_OPS
                    dve.wait_ge(s_upsb, i * 2 + (b + 2))
                    dve.wait_ge(s_act, i * 2 + (b + 1))
                    src = [up_sb[:, b, half * TOK:(half + 1) * TOK] for half in range(2)]
                    dst = [conv[:, b, half * TOK:(half + 1) * TOK] for half in range(2)]
                    tile = [bass.ds(i * 2 + (b + KF * half), 1) for half in range(2)]
                    for half in range(2):
                        dve.tensor_scalar(dst[half], src[half], cw[:, tile[half], 4], par("conv_b")[:, tile[half]],
                                          ALU.mult, ALU.add).then_inc(s_conv, 1)
                    done = 2
                    for dy, dx in taps:
                        r0, r1 = max(0, -dy), GRID_H - max(0, dy)
                        c0, c1 = max(0, -dx), GRID_W - max(0, dx)
                        for half in range(2):
                            o = dst[half].rearrange("p (r c) -> p r c", c=GRID_W)[:, r0:r1, c0:c1]
                            a = src[half].rearrange("p (r c) -> p r c", c=GRID_W)[:, r0 + dy:r1 + dy, c0 + dx:c1 + dx]
                            dve.wait_ge(s_conv, base + (done - 1))
                            dve.scalar_tensor_tensor(out=o, in0=a, scalar=cw[:, tile[half], (dy + 1) * 3 + dx + 1], in1=o, op0=ALU.mult,
                                                     op1=ALU.add).then_inc(s_conv, 1)
                            done += 1

            for m in range(KD):
                dve.wait_ge(s_dn_ps, m // 2 + 1)
                dve.scalar_tensor_tensor(out=x_sb[:, m, :], in0=bank[4 + m // 2][:, (m % 2) * TOK:(m % 2 + 1) * TOK],
                                         scalar=mod2[:, 3 * KD + m:3 * KD + m + 1], in1=x_sb[:, m, :], op0=ALU.mult, op1=ALU.add).then_inc(s_x2, 1)
            dve.wait_ge(s_x2, KD)
            dve.wait_ge(s_std, 3)
            mark(dve.reciprocal(rstd[:, 0:TOK], rstd[:, 0:TOK]))
            settle()
            for k in range(KD):
                dve.scalar_tensor_tensor(out=x_sb[:, k, :], in0=x_sb[:, k, :], scalar=par("g_final")[:, k:k + 1], in1=rstd[:, 0:TOK],
                                         op0=ALU.mult, op1=ALU.mult).then_inc(s_fin, 1)


_INS = [("x_t", [P, KD * TOK]), ("ctx_t", [P, KD * TOK]), ("pk", [P, PKW]), ("s5raw", [P, S5RAW]), ("log_step", [2, DP]),
        ("early_w", [6, P, UNIT]), ("ring_w", [UNITS, P, UNIT]), ("up_w", [3 * USLOTS, P, UNIT]), ("ln", [1, 4, TOK]), ("sgu_w", [P, 4, 2 * P]), ("sgu_b", [2, 4, P])]


def _tiles(w, m_per_unit):
    k, m = w.shape
    w = w.reshape(k // P, P, m // P // m_per_unit, m_per_unit, P)
    return w.transpose(2, 1, 3, 0, 4).reshape(m // P // m_per_unit, P, -1)


def _features(*vs):
    return [np.asarray(v).reshape(-1, P).T for v in vs]


def kernel(**inputs):
    import concourse.bacc as bacc
    from concourse.bass_utils import run_bass_kernel_spmd

    a = {k: np.asarray(v) for k, v in inputs.items()}
    w_in, w_ada, w_up = a["w_in"][0], a["w_ada"][0], a["w_up"][0]
    ada1 = _tiles(w_ada[:, :2 * D].reshape(D, 2, KD, P).transpose(0, 2, 1, 3).reshape(D, 2 * D), 2)
    ada = _tiles(w_ada[:, 2 * D:], 2)
    w_u, w_zu, w_v, w_gate = w_in[:, :512], w_in[:, 512:1024], w_in[:, 1024:1536], w_in[:, 1536:]
    gate = _tiles(w_gate, 2)
    v_units = w_v.reshape(2, 4, P, 512).transpose(0, 2, 1, 3).reshape(2, P, UNIT)
    loop = np.stack([ada[:8], gate], axis=1).reshape(4 * LOOPS, P, UNIT)
    pa, pb = _tiles(a["w_proj_a"][0], 4), _tiles(a["w_proj_b"][0], 4)
    last = np.stack([ada[12:16], _tiles(a["w_out"][0], 2)], axis=1).reshape(8, P, UNIT)
    ring_w = np.concatenate([_tiles(w_u, 2), ada1[6:8], v_units, _tiles(w_zu, 2), loop, _tiles(a["s5_w_glu"][0], 4),
                             ada[8:10], pb[0:1], pa[0:1], ada[10:12], pb[1:2], pa[1:2], last], axis=0)
    up = w_up.reshape(KD, P, 2, KF, P).transpose(3, 1, 2, 0, 4).reshape(KF, P, UNIT)
    down = a["w_down"][0].reshape(KF // 2, 2, P, D).transpose(0, 2, 1, 3).reshape(KF // 2, P, UNIT)
    conv_w = a["conv_w"][0].reshape(9, 2 * KF, P).transpose(2, 1, 0).reshape(P, -1)
    pick = np.tile(np.eye(CT, 2, dtype=np.float32), (NCT, 1))
    pk = np.concatenate(_features(a["c"][0], a["c_ctx"], a["b_ada"][0], a["g_mix"][0], a["g_ffn"][0], a["g_final"], a["b_gate"][0],
                                  a["s5_b_glu"][0], a["s5_d"][0], a["conv_b"][0]) + [pick, conv_w], axis=1)

    def per_state(v):
        v = v.reshape(2, PAIRS, 2, N, -1)
        return v.transpose(2, 3, 0, 1, 4).reshape(P, -1)

    c_re, c_im = (a[n][0].transpose(0, 1, 3, 2) for n in ("s5_c_re", "s5_c_im"))
    s5raw = np.concatenate([per_state(v) for v in (a["s5_a_re"][0], a["s5_a_im"][0], a["s5_b_re"][0], a["s5_b_im"][0], c_re, c_im)], axis=1)
    log_step = a["s5_log_step"][0].reshape(2, PAIRS, 2).transpose(2, 0, 1).reshape(2, DP)

    def tokens_t(v):
        return v.reshape(TOK, KD, P).transpose(2, 1, 0).reshape(P, -1)

    arrays = {
        "x_t": tokens_t(a["x"][0]), "ctx_t": tokens_t(a["ctx"][0]), "pk": pk, "s5raw": s5raw, "log_step": log_step,
        "early_w": ada1[:6], "ring_w": ring_w, "up_w": np.concatenate([up, down], axis=0),
        "ln": np.stack([a["sgu_ln_g"][0], a["sgu_ln_b"][0]]).reshape(1, 4, TOK), "sgu_w": a["sgu_w"][0].transpose(2, 0, 1).reshape(P, 4, 2 * P),
        "sgu_b": a["sgu_b"][0].reshape(4, 2, P).transpose(1, 0, 2),
    }
    arrays = {k: np.ascontiguousarray(v) for k, v in arrays.items()}
    nc = bacc.Bacc("TRN2", target_bir_lowering=False, num_devices=1)
    aps = [nc.dram_tensor(name, shape, F32, kind="ExternalInput").ap() for name, shape in _INS]
    out = nc.dram_tensor("out", [P, KD, TOK], F32, kind="ExternalOutput").ap()
    build(nc, *aps, out)
    r = run_bass_kernel_spmd(nc, [arrays], core_ids=[0])
    y = np.asarray(r.results[0]["out"])
    return np.ascontiguousarray(y.transpose(2, 1, 0).reshape(1, TOK, D))
```

```python
from contextlib import ExitStack

import numpy as np

import concourse.bass as bass
from concourse import mybir

F32 = mybir.dt.float32
ALU = mybir.AluOpType
ACT = mybir.ActivationFunctionType

P = 128
D = 1024
KD = D // P
TOK = 256
GRID_W = 64
GRID_H = TOK // GRID_W
S5W = 512
KS = S5W // P
G, H, N = 32, 16, 64
PAIRS = G // 2
CT = 32
NCT = P // CT
T = 8
CH = TOK // T
LAGS = 2 * T - 1
FFN = 2816
KF = FFN // P
NMOD = 6
EPS = 1e-6
TWO_PI = 2.0 * np.pi
ROUND_MAGIC = 12582912.0

RING = 4
UNIT = 2048
U_ADA1, U_INU, U_V, U_ZU, U_LOOP = 0, 2, 4, 6, 8
LOOPS = 4
PART1, PART2 = 2, 1
U_GLU = U_LOOP + 4 * LOOPS
U_PROJ = U_GLU + 1
U_OUT = U_PROJ + 8
UNITS = U_OUT + 8
LATER = (NMOD - 2) * KD // 2
BLK = 8
USLOTS = 11
UP_ROUNDS = KF // USLOTS
DOWN_LAST = 6

_PK = {}
_at = 0
for _name, _w in [("c", KD), ("c_ctx", KD), ("b_ada", NMOD * KD), ("g_mix", KD), ("g_ffn", KD), ("g_final", KD),
                  ("b_gate", 2 * KD), ("b_glu", KS), ("s5_d", KS), ("conv_b", 2 * KF), ("pick", 2), ("conv_w", 2 * KF * 9)]:
    _PK[_name] = (_at, _at + _w)
    _at += _w
PKW = _at
DP = 2 * PAIRS
S5RAW = DP * 2 + DP * H * 4


def build(nc, x_t, ctx_t, pk, s5raw, log_step, early_w, ring_w, up_w, ln, sgu_w, sgu_b, out):
    with ExitStack() as ctx:
        def sb(name, n):
            return ctx.enter_context(nc.sbuf_tensor(name, [P, n], F32))

        def sem(name):
            return ctx.enter_context(nc.semaphore(name))

        bank = [ctx.enter_context(nc.psum_tensor(f"bank{i}", [P, 512], F32)) for i in range(8)]

        s5_region = sb("s5_region", 8192 + 9216 + 4096 + 4096)
        w_in_s5 = s5_region[:, 0:8192].rearrange("p (d r q m) -> p d r q m", d=2, r=2, q=PAIRS)
        ca_region = s5_region[:, 8192:8192 + 9216]
        w_src = ca_region[:, 0:8192].rearrange("p (d r q t h) -> p d r q t h", d=2, r=2, q=PAIRS, t=T)
        ca = ca_region.rearrange("p (r c e h) -> p r c e h", r=2, c=DP, e=T + 1)
        m_region = s5_region[:, 17408:17408 + 4096]
        scratch = m_region[:, 0:2304]
        b_raw = m_region[:, 2304:2304 + 1024].rearrange("p (r c h) -> p r c h", r=2, c=DP)
        m_toep = m_region.rearrange("p (g m) -> p g m", g=G)
        e_region = s5_region[:, 21504:21504 + 4096]
        c_raw = e_region[:, 0:1024].rearrange("p (r c h) -> p r c h", r=2, c=DP)
        b_bar = e_region[:, 1024:2048].rearrange("p (r c h) -> p r c h", r=2, c=DP)
        b_pad = e_region[:, 2048:4096].rearrange("p (r c g h) -> p r c g h", r=2, c=DP, g=2)
        e_chunk = e_region.rearrange("p (s c) -> p s c", s=2 * CH)
        up_ring = s5_region[:, 0:USLOTS * UNIT].rearrange("p (s n) -> p s n", s=USLOTS)

        x_region = sb("x_region", KD * TOK)
        x_sb = x_region[:, :].rearrange("p (k t) -> p k t", k=KD)
        carry = x_region[:, :].rearrange("p (c s) -> p c s", c=2 * DP)
        ctx_region = sb("ctx_region", KD * TOK)
        ctx_sb = ctx_region[:, :].rearrange("p (k t) -> p k t", k=KD)
        u_chunk = ctx_region[:, :].rearrange("p (g c) -> p g c", g=G)
        y_tok = ctx_region[:, 0:1024]
        y_feat = ctx_region[:, 1024:2048].rearrange("p (m t c) -> p m t c", m=KS, t=T)
        glu_gate = ctx_region[:, 0:1024].rearrange("p (m t) -> p m t", m=KS)
        up_sb = ctx_region[:, 0:1024].rearrange("p (b n) -> p b n", b=2)
        conv = ctx_region[:, 1024:2048].rearrange("p (b n) -> p b n", b=2)
        h_all = sb("h_all", KD * 2 * TOK)[:, :].rearrange("p (k t) -> p k t", k=KD)
        h_x = h_all[:, :, TOK:2 * TOK]
        merged = h_x
        h2 = h_all[:, :, 0:TOK]
        ln_sb = h_all[:, 0:4, 0:TOK]
        sgu_w_sb = h_all[:, 4:8, 0:TOK]
        u_x = sb("u_x", 1024)
        y_gelu = u_x[:, :].rearrange("p (m t) -> p m t", m=KS)
        ring_region = sb("ring_region", RING * UNIT)
        ring = ring_region[:, :].rearrange("p (s n) -> p s n", s=RING)
        ffn_act = ring_region[:, 0:KF * TOK].rearrange("p (j t) -> p j t", j=KF)
        gate_region = sb("gates", 2 * KD * TOK)
        gates = gate_region[:, :].rearrange("p (m t) -> p m t", m=2 * KD)
        u_feat = gate_region[:, 0:2048].rearrange("p (m t c) -> p m t c", m=KS, t=T)
        power8 = gate_region[:, 2048:2048 + 2 * BLK * DP].rearrange("p (r e c) -> p r e c", r=2, e=BLK)
        silu_sb = gates[:, 0:2, :]
        merge_tmp = sb("merge_tmp", 2 * TOK)[:, :].rearrange("p (b t) -> p b t", b=2)
        z_region = sb("z_region", 2048)
        z_u = z_region[:, 0:1024].rearrange("p (m t) -> p m t", m=KS)
        v_tok = z_region[:, 1024:2048].rearrange("p (c n) -> p c n", c=2)
        squares = z_region[:, 1024:2048].rearrange("p (b n) -> p b n", b=2)
        y_b = z_u
        wide_same, wide_cross = z_region[:, 1024:1536], z_region[:, 1536:2048]
        y_a = z_region[:, 1024:2048].rearrange("p (m t) -> p m t", m=KS)
        entering = merge_tmp.rearrange("p b t -> p (b t)")[:, 0:(BLK - 1) * 2 * DP].rearrange("p (b c) -> p b c", c=2 * DP)
        sgu_b_sb = sb("sgu_b_sb", 512)[:, :].rearrange("p (j q) -> p j q", j=4)
        rstd = sb("rstd", 512)
        pk_sb = sb("pk_sb", PKW)
        c_pad = sb("c_pad", KD * CT)[:, :].rearrange("p (k v) -> p k v", k=KD)
        c_silu = c_pad[:, :, 0:2]
        rows1 = merge_tmp
        rows2 = rstd[:, :].rearrange("p (b t) -> p b t", b=2)
        mod1 = sb("mod1", 4 * KD)[:, :].rearrange("p (k a v) -> p k a v", a=2, v=2)
        scale1 = sb("scale1", 2 * KD)[:, :].rearrange("p (k v) -> p k v", v=2)
        mod2 = sb("mod2", 4 * KD)
        scale2 = sb("scale2", KD)
        ones = sb("ones", P)
        ident = sb("ident", P)
        power = sb("power", 2 * (T + 1) * DP)[:, :].rearrange("p (r e c) -> p r e c", r=2, e=T + 1)
        a_raw = sb("a_raw", 3 * DP)
        small = sb("small", 16 * DP)
        cross = small[:, :].rearrange("p (j r c) -> p j r c", j=BLK, r=2)
        bn = sb("bn", 2 * 6 + 2 * 2 + 4 + 1)
        k_sb = m_region[:, 0:KS * LAGS * H]

        def par(name):
            a, b = _PK[name]
            return pk_sb[:, a:b]

        early = [gate_region[:, k * UNIT:(k + 1) * UNIT] for k in range(2)] + \
                [s5_region[:, k * UNIT:(k + 1) * UNIT] for k in range(4)] + [ring[:, 0, :], ring[:, 1, :]]

        u_dram = nc.dram_tensor("u_scratch", [KS, P, T, 2 * CH], F32)
        k_dram = nc.dram_tensor("k_scratch", [KS, P, LAGS * H], F32)

        s_pk, s_raw, s_x, s_ctx = sem("pk_loaded"), sem("s5_raw_loaded"), sem("x_loaded"), sem("ctx_loaded")
        s_ls, s_braw, s_craw = sem("log_step_loaded"), sem("s5_b_loaded"), sem("s5_c_loaded")
        s_ring = [sem(f"ring_loaded{i}") for i in range(RING)]
        s_unit = sem("unit_multiplied")
        s_up = [sem(f"up_loaded{i}") for i in range(USLOTS)]
        s_up_used = sem("up_used")
        s_const, s_pad = sem("constants_set"), sem("pad_zeroed")
        s_sq, s_sq_used = sem("squares_ready"), sem("squares_used")
        s_std = sem("std_ready")
        s_csilu = sem("c_silu_ready")
        s_early = [sem(f"early_unit_loaded{k}") for k in range(6)]
        s_cpad = sem("c_pad_zeroed")
        s_rows, s_pick = sem("modulation_rows_ready"), sem("modulation_in_psum")
        s_ada_ps, s_mod1, s_scale1 = sem("ada_in_psum"), sem("mod1_ready"), sem("scale1_ready")
        s_norm, s_h = sem("normed_ready"), sem("h_ready")
        s_trig_in, s_trig = sem("trig_args_ready"), sem("act_exp_sin_done")
        s_wsrc, s_tr, s_win = sem("w_src_ready"), sem("transposed"), sem("w_in_evacuated")
        s_ux = sem("u_x_copied")
        s_bpad, s_ca = sem("b_pad_ready"), sem("ca_ready")
        s_uf, s_u_out, s_uchunk = sem("u_feat_ready"), sem("u_stored"), sem("u_chunk_loaded")
        s_z = sem("z_ready")
        s_v_ps, s_v, s_vn = sem("v_in_psum"), sem("v_gelu_ready"), sem("v_normed")
        s_ln = sem("gating_params_loaded")
        s_sgu_ps, s_yb = sem("sgu_in_psum"), sem("y_b_ready")
        s_k_ps, s_k, s_k_out, s_m = sem("k_in_psum"), sem("k_evacuated"), sem("k_stored"), sem("m_loaded")
        s_e_ps, s_e, s_ev, s_scan = sem("e_in_psum"), sem("e_evacuated_by_act"), sem("e_evacuated_by_dve"), sem("carry_ready")
        s_gate = sem("gate_ready")
        s_mod2, s_scale2 = sem("mod2_ready"), sem("scale2_ready")
        s_y8_ps, s_y8, s_y_tr = sem("y_by_chunk_in_psum"), sem("y_by_chunk_ready"), sem("y_transposed")
        s_y, s_ygelu = sem("y_with_skip_ready"), sem("y_gelu_ready")
        s_glu_ps, s_glu, s_ya = sem("glu_in_psum"), sem("glu_gate_ready"), sem("y_a_ready")
        s_pr_ps, s_mg = sem("proj_in_psum"), sem("merged_ready")
        s_xr = sem("x_reloaded")
        s_x1 = sem("x1_ready")
        s_norm2, s_h2 = sem("normed2_ready"), sem("h2_ready")
        s_upsb, s_conv = sem("up_evacuated"), sem("conv_tap")
        s_silu, s_act = sem("silu_ready"), sem("ffn_act_ready")
        s_dn_ps, s_x2, s_fin, s_stored = sem("down_in_psum"), sem("x2_ready"), sem("final_ready"), sem("out_stored")
        s_dve = sem("dve_chain")
        s_pool = sem("pool_chain")
        s_lnvar, s_lnstd = sem("ln_variance_ready"), sem("ln_deviation_ready")

        PROJ_BANK = (4, 5, 7, 0)
        OUT_BANK = (1, 2, 4, 5)
        E_BANKS = 6
        CONV_OPS = 18
        block = ctx.enter_context(nc.Block())

        def out_unit(i):
            return U_OUT + (1, 3, 4, 5)[i]

        def ring_ready(pe, u):
            pe.wait_ge(s_ring[u % RING], 16 * (u // RING + 1))

        @block.sync
        def _(sp):
            sp.dma_start(x_region[:, :], x_t).then_inc(s_x, 16)
            sp.dma_start(ctx_region[:, :], ctx_t).then_inc(s_ctx, 16)
            sp.dma_start(early[0], early_w[0]).then_inc(s_early[0], 16)
            sp.dma_start(early[1], early_w[1]).then_inc(s_early[1], 16)
            for u in (U_INU, U_INU + 1):
                sp.dma_start(ring[:, u, :], ring_w[u]).then_inc(s_ring[u], 16)
            sp.dma_start(m_region[:, 2304:2304 + 1024], s5raw[:, 2 * DP:2 * DP + 1024]).then_inc(s_braw, 16)
            for k in range(2, 6):
                sp.dma_start(early[k], early_w[k]).then_inc(s_early[k], 16)
            for u in (U_ADA1, U_ADA1 + 1):
                sp.dma_start(ring[:, u, :], ring_w[u]).then_inc(s_ring[u], 16)
            sp.dma_start(e_region[:, 0:1024], s5raw[:, 2 * DP + 1024:2 * DP + 2048]).then_inc(s_craw, 16)
            for u in (U_V, U_V + 1):
                sp.wait_ge(s_ada_ps, u - U_V + 7)
                sp.dma_start(ring[:, u % RING, :], ring_w[u]).then_inc(s_ring[u % RING], 16)
            sp.wait_ge(s_unit, RING)
            for u in (U_ZU, U_ZU + 1):
                sp.dma_start(ring[:, u % RING, :], ring_w[u]).then_inc(s_ring[u % RING], 16)
            sp.wait_ge(s_u_out, 16 * KS)
            for tau in range(T):
                sp.dma_start(u_chunk[tau * H:(tau + 1) * H, :, :],
                             u_dram[:, :, tau, :].rearrange("m (g h) c -> h (m g) c", h=H)).then_inc(s_uchunk, 16)
            full = UNITS // RING
            with sp.Fori(2, full) as i:
                for s in range(RING):
                    sp.wait_ge(s_unit, i * RING + (s - RING + 1))
                    sp.dma_start(ring[:, s, :], ring_w[bass.ds(i * RING + s, 1)].rearrange("a p n -> p (a n)")).then_inc(s_ring[s], 16)
            for u in range(full * RING, UNITS):
                sp.wait_ge(s_unit, u - RING + 1)
                sp.dma_start(ring[:, u % RING, :], ring_w[u]).then_inc(s_ring[u % RING], 16)
            sp.wait_ge(s_y8_ps, 2)
            for s in range(USLOTS):
                sp.dma_start(up_ring[:, s, :], up_w[s]).then_inc(s_up[s], 16)
            with sp.Fori(1, UP_ROUNDS + 1) as r:
                for s in range(USLOTS):
                    sp.wait_ge(s_up_used, r * USLOTS + (s - USLOTS + 1))
                    sp.dma_start(up_ring[:, s, :], up_w[bass.ds(r * USLOTS + s, 1)].rearrange("a p n -> p (a n)")).then_inc(s_up[s], 16)
            for m in range(KD):
                sp.wait_ge(s_fin, m + 1)
                sp.dma_start(out[:, m, :], x_sb[:, m, :]).then_inc(s_stored, 16)
            sp.wait_ge(s_stored, 16 * KD)

        @block.gpsimd
        def _(pool):
            pool.memset(ones[:, :], 1.0).then_inc(s_const, 1)
            pool.memset(c_pad, 0.0).then_inc(s_cpad, 1)
            pool.memset(ident[:, :], 0.0).then_inc(s_pool, 1)
            pool.wait_ge(s_pool, 1)
            pool.affine_select(out=ident[:, :], in_=ident[:, :], compare_op=ALU.not_equal, fill=1.0, base=0,
                               pattern=[[-1, P]], channel_multiplier=1).then_inc(s_const, 1)
            pool.memset(b_pad, 0.0).then_inc(s_pad, 1)
            pool.dma_start(sgu_b_sb[0:64, :, :], sgu_b[0:1].partition_broadcast(64)).then_inc(s_ln, 16)
            pool.dma_start(sgu_b_sb[64:128, :, :], sgu_b[1:2].partition_broadcast(64)).then_inc(s_ln, 16)
            pool.wait_ge(s_unit, U_V)
            pool.dma_start(ln_sb, ln.partition_broadcast(P)).then_inc(s_ln, 16)
            pool.dma_start(sgu_w_sb, sgu_w).then_inc(s_ln, 16)
            pool.wait_ge(s_y8_ps, 2)
            pool.dma_start(x_region[:, :], x_t).then_inc(s_xr, 16)
            pool.sem_inc(s_act, 2)
            with pool.Fori(0, KF // 2) as i:
                for b in range(2):
                    pool.wait_ge(s_silu, i * 2 + (b + 1))
                    pool.tensor_tensor(ffn_act[:, bass.ds(i * 2 + b, 1), :].rearrange("p a t -> p (a t)"), silu_sb[:, b, :],
                                       conv[:, b, TOK:2 * TOK], ALU.mult).then_inc(s_act, 1)

        @block.tensor
        def _(pe):
            pe.wait_ge(s_const, 1)
            for k in range(KD):
                pe.wait_ge(s_sq, 2 * (k + 1))
                pe.matmul(bank[7][:, :], ones[:, :], squares[:, k % 2, :], start=(k == 0),
                          stop=(k == KD - 1)).then_inc(s_sq_used, 1)

            pe.wait_ge(s_csilu, 1)

            def modulation_rows(dst, unit, count):
                u3 = unit.rearrange("p (a k n) -> p k a n", a=2, k=KD)
                for k in range(KD):
                    c = k % NCT
                    mx = pe.matmul(dst[c * CT:(c + 1) * CT, :].rearrange("p (a n) -> p a n", a=2), c_pad[:, k, :], u3[:, k],
                                   start=(k < NCT), stop=(k >= KD - NCT), skip_group_check=True)
                mx.then_inc(count, 1)

            def first_rows(k):
                if k < 6:
                    pe.wait_ge(s_early[k], 16)
                else:
                    ring_ready(pe, U_ADA1 + k - 6)
                if k == 3:
                    pe.wait_ge(s_std, 1)
                elif k >= 4:
                    pe.wait_ge(s_mod1, k - 3)
                modulation_rows(bank[4 + k % 4][:, 0:2 * P], early[k], s_ada_ps)

            def first_pick(k):
                pe.wait_ge(s_rows, k + 1)
                for a in range(2):
                    mx = pe.matmul(bank[4 + k % 4][:, 2 * P + 2 * a:2 * P + 2 * a + 2], rows1[:, k % 2, a * P:(a + 1) * P], par("pick"),
                                   start=True, stop=True)
                mx.then_inc(s_pick, 1)

            def u_of_tile(k):
                pe.wait_ge(s_h, 2 * (k + 1))
                for m in range(KS):
                    if m == KS // 2 and k + 2 < KD:
                        first_rows(k + 2)
                    if k == 0 and m % 2 == 0:
                        ring_ready(pe, U_INU + m // 2)
                    mx = pe.matmul(bank[m][:, :], ring[:, U_INU + m // 2, ((m % 2) * KD + k) * P:((m % 2) * KD + k + 1) * P],
                                   h_all[:, k, :], start=(k == 0), stop=(k == KD - 1))
                    if k == KD - 1:
                        mx.then_inc(s_unit, 1)

            first_rows(0)
            first_rows(1)
            first_pick(0)
            for k in range(KD):
                if k + 1 < KD:
                    first_pick(k + 1)
                u_of_tile(k)

            pe.wait_ge(s_const, 2)
            job = 0
            for d in range(2):
                for r in range(2):
                    pe.wait_ge(s_wsrc, 2 * d + r + 1)
                    for q0 in range(0, PAIRS, 4):
                        if job >= 2:
                            pe.wait_ge(s_win, job - 1)
                        for q in range(4):
                            mx = pe.transpose(bank[4 + job % 2][:, q * P:(q + 1) * P],
                                              w_src[:, d, r, q0 + q].rearrange("p t h -> p (t h)"), ident[:, :])
                        mx.then_inc(s_tr, 1)
                        job += 1

            pe.wait_ge(s_mod1, KD)
            for half in range(2):
                u = U_V + half
                ring_ready(pe, u)
                for c in range(2):
                    for kk in range(KD // 2):
                        k = half * (KD // 2) + kk
                        mx = pe.matmul(bank[6 + c][:, :], h_x[:, k, c * P:(c + 1) * P], ring[:, u % RING, kk * 512:(kk + 1) * 512],
                                       start=(k == 0), stop=(k == KD - 1))
                    if half == 1 and c == 0:
                        mx.then_inc(s_v_ps, 1)
                mx.then_inc(s_unit, 1)

            pe.wait_ge(s_win, PAIRS)
            for i in range(2):
                u = U_ZU + i
                ring_ready(pe, u)
                for mm in range(2):
                    for k in range(KD):
                        mx = pe.matmul(bank[4 + i][:, mm * TOK:(mm + 1) * TOK], ring[:, u % RING, (mm * KD + k) * P:(mm * KD + k + 1) * P],
                                       h_x[:, k, :], start=(k == 0), stop=(k == KD - 1))
                mx.then_inc(s_unit, 1)

            def chunk_inputs(job):
                d, r, q0 = job // 4, (job // 2) % 2, 8 * (job % 2)
                if job >= E_BANKS:
                    n = job - E_BANKS
                    pe.wait_ge(s_ev if n % 2 else s_e, n // 2 + 1)
                for q in range(q0, q0 + 8):
                    for g2 in range(2):
                        rhs = u_chunk[:, 2 * q + g2, :].rearrange("p (a c) -> p a c", a=2)
                        if d == 1:
                            rhs = rhs[:, :, ::-1]
                        mx = pe.matmul(bank[job % E_BANKS][g2 * N:(g2 + 1) * N, (q - q0) * 2 * CH:(q - q0 + 1) * 2 * CH],
                                       w_in_s5[:, d, r, q, g2 * N:(g2 + 1) * N], rhs, start=True, stop=True)
                mx.then_inc(s_e_ps, 1)

            pe.wait_ge(s_uchunk, 16 * T)
            pe.wait_ge(s_uf, KS)
            pe.wait_ge(s_z, 2)
            for job in range(E_BANKS):
                chunk_inputs(job)

            pe.wait_ge(s_bpad, 1)
            pe.wait_ge(s_ca, 2)
            pe.wait_ge(s_v, 2)
            for q in range(PAIRS):
                m, row = q // 4, 32 * (q % 4)
                base = (m % 2) * LAGS * H
                for d, e0, j0 in ((1, 1, 0), (0, 0, T - 1)):
                    for r in range(2):
                        mx = pe.matmul(bank[6 + m // 2][row:row + 32, base + j0 * H:base + (j0 + T) * H],
                                       b_pad[:, r, d * PAIRS + q].rearrange("p g h -> p (g h)"),
                                       ca[:, r, d * PAIRS + q, e0:e0 + T, :].rearrange("p e h -> p (e h)"),
                                       start=(d == 1 and r == 0), stop=(d == 0 and r == 1), skip_group_check=True)
                if q % 8 == 7:
                    mx.then_inc(s_k_ps, 1)

            pe.wait_ge(s_vn, 2)
            pe.wait_ge(s_ln, 64)
            pe.wait_ge(s_k, 2)
            for j in range(4):
                for g2 in range(2):
                    for c in range(2):
                        mx = pe.matmul(bank[6 + j // 2][g2 * 64:(g2 + 1) * 64, (j % 2) * TOK + c * P:(j % 2) * TOK + (c + 1) * P],
                                       v_tok[:, c, (2 * j + g2) * 64:(2 * j + g2 + 1) * 64], sgu_w_sb[:, j, g2 * P:(g2 + 1) * P],
                                       start=True, stop=True)
                if j % 2 == 1:
                    mx.then_inc(s_sgu_ps, 1)

            for job in range(E_BANKS, 8):
                chunk_inputs(job)

            mod_rows = bank[3][:, 2 * P:4 * P]

            def gates_and_modulation(i):
                for b in range(2):
                    slot = (U_LOOP + 2 * b) % RING
                    pe.wait_ge(s_ring[slot], (i + (U_LOOP // RING + 1)) * 16)
                    modulation_rows(mod_rows, ring[:, slot, :], s_unit)
                    slot = (U_LOOP + 2 * b + 1) % RING
                    pe.wait_ge(s_ring[slot], (i + (U_LOOP // RING + 1)) * 16)
                    pe.wait_ge(s_gate, i * 4 + (2 * b + 1))
                    for mm in range(2):
                        for k in range(KD):
                            mx = pe.matmul(bank[4 + b][:, mm * TOK:(mm + 1) * TOK], ring[:, slot, (mm * KD + k) * P:(mm * KD + k + 1) * P],
                                           h_x[:, k, :], start=(k == 0), stop=(k == KD - 1))
                    mx.then_inc(s_unit, 1)
                    pe.wait_ge(s_rows, i * 2 + (KD + b + 1))
                    for mm in range(2):
                        mx = pe.matmul(bank[3][:, bass.ds(i * 4 + (2 * b + mm), 1)], rows2[:, b, mm * P:(mm + 1) * P], par("pick")[:, 0:1],
                                       start=True, stop=True)
                    mx.then_inc(s_pick, 1)

            def later_rows(u):
                ring_ready(pe, u)
                modulation_rows(mod_rows, ring[:, u % RING, :], s_unit)

            def later_pick(n):
                pe.wait_ge(s_rows, KD + n + 1)
                for mm in range(2):
                    rows = rows1 if n >= LATER - 2 else rows2
                    mx = pe.matmul(bank[3][:, 2 * n + mm:2 * n + mm + 1], rows[:, n % 2, mm * P:(mm + 1) * P], par("pick")[:, 0:1],
                                   start=True, stop=True)
                mx.then_inc(s_pick, 1)

            pe.wait_ge(s_z, 2)
            pe.wait_ge(s_e, 4)
            pe.wait_ge(s_ev, 4)
            with pe.Fori(0, PART1 - 1) as i:
                gates_and_modulation(i)

            pe.wait_ge(s_m, 16 * T)
            for g2 in range(2):
                for j in range(P // H // 2):
                    for m in range(KS):
                        g = m * (P // H) + 2 * j + g2
                        pe.matmul(bank[g2][m * CH:(m + 1) * CH, j * P:(j + 1) * P], u_chunk[:, g, CH:2 * CH], m_toep[:, g, :],
                                  start=(j == 0), stop=False, skip_group_check=True)

            with pe.Fori(PART1 - 1, PART1) as i:
                gates_and_modulation(i)

            pe.wait_ge(s_scan, 1)
            for g2 in range(2):
                half = slice(g2 * N, (g2 + 1) * N)
                for d, r, e0 in ((0, 0, 1), (0, 1, 1), (1, 0, 0), (1, 1, 0)):
                    for j in range(P // H // 2):
                        for m in range(KS):
                            q = m * (P // H // 2) + j
                            mx = pe.matmul(bank[g2][m * CH:(m + 1) * CH, j * P:(j + 1) * P], carry[half, (r * 2 + d) * PAIRS + q, :],
                                           ca[half, r, d * PAIRS + q, e0:e0 + T, :].rearrange("p e h -> p (e h)"),
                                           start=False, stop=(d == 1 and r == 1), skip_group_check=True)
                mx.then_inc(s_y8_ps, 1)

            with pe.Fori(PART1, PART1 + PART2) as i:
                gates_and_modulation(i)

            pe.wait_ge(s_y8, 2)
            for tau in range(T):
                mx = pe.transpose(bank[tau // 4][:, (tau % 4) * P:(tau % 4 + 1) * P], y_tok[:, tau * P:(tau + 1) * P], ident[:, :])
                if tau % 4 == 3:
                    mx.then_inc(s_y_tr, 1)

            with pe.Fori(PART1 + PART2, LOOPS) as i:
                gates_and_modulation(i)

            ring_ready(pe, U_GLU)
            pe.wait_ge(s_ygelu, 1)
            pe.wait_ge(s_yb, 4)
            for m in range(KS):
                for k in range(KS):
                    mx = pe.matmul(bank[(2, 6)[m // 2]][:, (m % 2) * TOK:(m % 2 + 1) * TOK],
                                   ring[:, U_GLU % RING, (m * KS + k) * P:(m * KS + k + 1) * P], y_gelu[:, k, :],
                                   start=(k == 0), stop=(k == KS - 1))
                if m == 1:
                    mx.then_inc(s_glu_ps, 1)
            mx.then_inc(s_unit, 1)

            pe.wait_ge(s_mod2, 1)
            for i in range(4):
                later_rows(U_PROJ + 2 * i)
                u = U_PROJ + 2 * i + 1
                ring_ready(pe, u)
                for mm in range(2):
                    m = 2 * i + mm
                    dst = bank[PROJ_BANK[m % 4]]
                    if m >= 4:
                        pe.wait_ge(s_mg, m - 3)
                    elif m == 0:
                        pe.wait_ge(s_gate, 4 * LOOPS + 1)
                    elif m == 3:
                        pe.wait_ge(s_y, 2 * KS)
                    for half, src in enumerate((y_b, y_a)):
                        if m == 0 and half == 1:
                            pe.wait_ge(s_ya, KS)
                        for k in range(KS):
                            t = (half * 2 + mm) * KS + k
                            mx = pe.matmul(dst[:, (1 - half) * TOK:(2 - half) * TOK], ring[:, u % RING, t * P:(t + 1) * P],
                                           src[:, k, :], start=(k == 0), stop=(k == KS - 1))
                    mx.then_inc(s_unit if mm else s_pr_ps, 1)
                later_pick(2 * LOOPS + i)

            def sum_squares(dst, before, k):
                pe.wait_ge(s_sq, before + k + 1)
                pe.matmul(dst[:, 0:TOK], ones[:, :], squares[:, k % 2, 0:TOK], start=(k == 0), stop=(k == KD - 1)).then_inc(s_sq_used, 1)

            for i in range(4):
                if i < 2:
                    later_rows(U_OUT + 2 * i)
                u = out_unit(i)
                ring_ready(pe, u)
                if i == 0:
                    pe.wait_ge(s_mg, KD)
                for mm in range(2):
                    for k in range(KD):
                        mx = pe.matmul(bank[OUT_BANK[i]][:, mm * TOK:(mm + 1) * TOK], ring[:, u % RING, (mm * KD + k) * P:(mm * KD + k + 1) * P],
                                       merged[:, k, :], start=(k == 0), stop=(k == KD - 1))
                mx.then_inc(s_unit, 1)
                if i < 2:
                    later_pick(2 * LOOPS + 4 + i)
                if i >= 1:
                    sum_squares(bank[6], 2 * KD, 2 * i - 2)
                    sum_squares(bank[6], 2 * KD, 2 * i - 1)
            sum_squares(bank[6], 2 * KD, KD - 2)
            sum_squares(bank[6], 2 * KD, KD - 1)
            pe.wait_ge(s_mod2, 2)
            for n in range(2):
                later_rows(U_OUT + 6 + n)
                later_pick(LATER - 2 + n)

            with pe.Fori(0, UP_ROUNDS) as r:
                for s in range(USLOTS):
                    pe.wait_ge(s_up[s], r * 16 + 16)
                    pe.wait_ge(s_upsb, r * USLOTS + max(1, s - 1))
                    for half in range(2):
                        for k in range(KD):
                            if s == 0 and half == 0:
                                pe.wait_ge(s_h2, k + 1)
                            mx = pe.matmul(bank[s % 3][:, half * TOK:(half + 1) * TOK], up_ring[:, s, (half * KD + k) * P:(half * KD + k + 1) * P],
                                           h2[:, k, :], start=(k == 0), stop=(k == KD - 1))
                    mx.then_inc(s_up_used, 1)

            def down(k, m):
                mx = pe.matmul(bank[4 + m // 2][:, (m % 2) * TOK:(m % 2 + 1) * TOK],
                               up_ring[:, k // 2, (k % 2) * D + m * P:(k % 2) * D + (m + 1) * P], ffn_act[:, k, :],
                               start=(k == 0 and m % 2 == 0), stop=(k == KF - 1), skip_group_check=True)
                if k == KF - 1 and m % 2 == 1:
                    mx.then_inc(s_dn_ps, 1)

            for k in range(KF - DOWN_LAST):
                if k % 2 == 0:
                    pe.wait_ge(s_up[k // 2], 16 * (UP_ROUNDS + 1))
                pe.wait_ge(s_act, k + 3)
                for m in range(KD):
                    down(k, m)
            for m in range(KD):
                for k in range(KF - DOWN_LAST, KF):
                    if m == 0:
                        if k % 2 == 0:
                            pe.wait_ge(s_up[k // 2], 16 * (UP_ROUNDS + 1))
                        pe.wait_ge(s_act, k + 3)
                    down(k, m)
                if m % 2 == 1 and m >= 3:
                    sum_squares(bank[3], 3 * KD, m - 3)
                    sum_squares(bank[3], 3 * KD, m - 2)
            sum_squares(bank[3], 3 * KD, KD - 2)
            sum_squares(bank[3], 3 * KD, KD - 1)

        @block.scalar
        def _(act):
            act.sem_inc(s_gate, 1)
            act.sem_inc(s_upsb, 1)
            act.dma_start(a_raw[:, 0:2 * DP], s5raw[:, 0:2 * DP]).then_inc(s_raw, 16)
            for g2 in range(2):
                act.dma_start(a_raw[g2 * N:(g2 + 1) * N, 2 * DP:3 * DP], log_step[g2:g2 + 1].partition_broadcast(N)).then_inc(s_ls, 16)
            act.dma_start(pk_sb[:, :], pk).then_inc(s_pk, 16)

            def preload_sqrt():
                act.activation(bn[:, 20:21], ones[:, 0:1], ACT.Sqrt)

            act.wait_ge(s_ls, 32)
            act.activation(small[:, 0:DP], a_raw[:, 2 * DP:3 * DP], ACT.Exp).then_inc(s_trig, 1)
            act.wait_ge(s_trig_in, 1)
            act.activation(small[:, 2 * DP:3 * DP], small[:, DP:2 * DP], ACT.Exp).then_inc(s_trig, 1)
            act.wait_ge(s_trig_in, 2)
            act.activation(small[:, 5 * DP:6 * DP], small[:, 4 * DP:5 * DP], ACT.Sin).then_inc(s_trig, 1)
            act.activation(small[:, 6 * DP:7 * DP], small[:, 4 * DP:5 * DP], ACT.Sin, scale=0.5).then_inc(s_trig, 1)

            act.wait_ge(s_pk, 16)
            act.wait_ge(s_cpad, 1)
            act.activation(c_silu.rearrange("p k v -> p v k"), pk_sb[:, 0:2 * KD].rearrange("p (v k) -> p v k", v=2),
                           ACT.Silu).then_inc(s_csilu, 1)

            preload_sqrt()
            act.wait_ge(s_sq_used, KD)
            act.activation(rstd[:, :], bank[7][:, :], ACT.Sqrt, scale=1.0 / D, bias=EPS).then_inc(s_std, 1)

            def first_rows(k):
                act.wait_ge(s_ada_ps, k + 1)
                act.activation(rows1[:, k % 2, :], bank[4 + k % 4][:, 0:2 * P], ACT.Copy).then_inc(s_rows, 1)

            first_rows(0)
            first_rows(1)
            for k in range(KD):
                act.wait_ge(s_scale1, k + 1)
                for v in (1, 0):
                    act.wait_ge(s_norm, 2 * k + 2 - v)
                    part = h_all[:, k, (1 - v) * TOK:(2 - v) * TOK]
                    act.activation(part, part, ACT.Identity, scale=scale1[:, k, v:v + 1], bias=mod1[:, k, 0, v:v + 1]).then_inc(s_h, 1)
                if k + 2 < KD:
                    first_rows(k + 2)

            for m in range(KS):
                act.wait_ge(s_unit, m + 1)
                act.activation(u_feat[:, m, :, :], bank[m][:, :].rearrange("p (c t) -> p t c", t=T), ACT.Copy).then_inc(s_uf, 1)
                act.wait_ge(s_uf, m + 1)
                act.dma_start(u_dram[m].rearrange("p t c -> p (t c)"), u_feat[:, m, :, :].rearrange("p t c -> p (t c)")).then_inc(s_u_out, 16)

            act.wait_ge(s_ada_ps, KD)
            job = 0
            for d in range(2):
                for r in range(2):
                    for q0 in range(0, PAIRS, 4):
                        act.wait_ge(s_tr, job + 1)
                        act.activation(w_in_s5[:, d, r, q0:q0 + 4, :].rearrange("p q m -> p (q m)"), bank[4 + job % 2][:, :],
                                       ACT.Copy).then_inc(s_win, 1)
                        job += 1

            for c in range(2):
                act.wait_ge(*((s_unit, U_V + 2) if c else (s_v_ps, 1)))
                act.activation(v_tok[:, c, :], bank[6 + c][:, :], ACT.Gelu_apprx_tanh).then_inc(s_v, 1)
            for i in range(2):
                act.wait_ge(s_unit, U_ZU + i + 1)
                act.activation(z_u[:, 2 * i:2 * i + 2, :].rearrange("p m t -> p (m t)"), bank[4 + i][:, :], ACT.Gelu_apprx_tanh).then_inc(s_z, 1)

            for c in range(2):
                act.wait_ge(s_lnvar, c + 1)
                act.activation(bn[:, 18 + c:19 + c], bn[:, 16 + c:17 + c], ACT.Sqrt).then_inc(s_lnstd, 1)
            for b in range(2):
                act.wait_ge(s_k_ps, b + 1)
                act.activation(k_sb[:, 2 * b * LAGS * H:(2 * b + 2) * LAGS * H], bank[6 + b][:, 0:2 * LAGS * H], ACT.Copy).then_inc(s_k, 1)
            act.wait_ge(s_k, 2)
            act.dma_start(k_dram[:].rearrange("m p n -> p m n"), k_sb[:, :].rearrange("p (m n) -> p m n", m=KS)).then_inc(s_k_out, 16)
            for job in range(0, 8, 2):
                d, r, q0 = job // 4, (job // 2) % 2, 8 * (job % 2)
                act.wait_ge(s_e_ps, job + 1)
                col = (r * 2 + d) * PAIRS + q0
                act.activation(e_chunk[:, :, col:col + 8].rearrange("p s c -> p c s"), bank[job % E_BANKS][:, :].rearrange("p (c s) -> p c s", c=8),
                               ACT.Copy).then_inc(s_e, 1)
            act.wait_ge(s_k_out, 16)
            for tau in range(T):
                act.dma_start(m_toep[tau * H:(tau + 1) * H, :, :],
                              k_dram[:, :, (T - 1 - tau) * H:(2 * T - 1 - tau) * H].rearrange("m (g h) n -> h (m g) n", h=H)).then_inc(s_m, 16)

            act.wait_ge(s_ux, 1)

            def gate_sigmoids(i):
                for b in range(2):
                    act.wait_ge(s_unit, i * 4 + (U_LOOP + 2 * b + 1))
                    act.activation(rows2[:, b, :], bank[3][:, 2 * P:4 * P], ACT.Copy).then_inc(s_rows, 1)
                    act.wait_ge(s_unit, i * 4 + (U_LOOP + 2 * b + 2))
                    for mm in range(2):
                        m = i * 4 + (2 * b + mm)
                        act.activation(gates[:, bass.ds(m, 1), :].rearrange("p a t -> p (a t)"), bank[4 + b][:, mm * TOK:(mm + 1) * TOK],
                                       ACT.Sigmoid, bias=par("b_gate")[:, bass.ds(m, 1)]).then_inc(s_gate, 1)

            with act.Fori(0, PART1) as i:
                gate_sigmoids(i)

            act.wait_ge(s_y8_ps, 2)
            for b in range(2):
                act.activation(y_tok.rearrange("p (t g b h) -> p b g t h", t=T, b=2, h=H)[:, b],
                               bank[b][:, :].rearrange("p (g t h) -> p g t h", g=4, t=T), ACT.Copy).then_inc(s_y8, 1)

            with act.Fori(PART1, PART1 + PART2) as i:
                gate_sigmoids(i)

            act.wait_ge(s_y, 2 * KS)
            act.activation(y_gelu.rearrange("p m (c t) -> p m t c", t=T), y_feat, ACT.Gelu_apprx_tanh).then_inc(s_ygelu, 1)

            with act.Fori(PART1 + PART2, LOOPS) as i:
                gate_sigmoids(i)

            for m in range(KS):
                act.wait_ge(*((s_unit, U_GLU + 1) if m // 2 else (s_glu_ps, 1)))
                act.activation(glu_gate[:, m, :], bank[(2, 6)[m // 2]][:, (m % 2) * TOK:(m % 2 + 1) * TOK], ACT.Sigmoid,
                               bias=par("b_glu")[:, m:m + 1]).then_inc(s_glu, 1)

            def last_rows(u, n, rows):
                act.wait_ge(s_unit, u + 1)
                act.activation(rows[:, n % 2, :], bank[3][:, 2 * P:4 * P], ACT.Copy).then_inc(s_rows, 1)

            preload_sqrt()
            for n in range(6):
                last_rows(U_PROJ + 2 * n, n, rows2)
            for k in range(KD):
                act.wait_ge(s_x1, k + 1)
                if k >= 2:
                    act.wait_ge(s_sq_used, KD + k - 1)
                act.activation(squares[:, k % 2, 0:TOK], x_sb[:, k, :], ACT.Square).then_inc(s_sq, 1)

            act.wait_ge(s_sq_used, 2 * KD)
            act.activation(rstd[:, 0:TOK], bank[6][:, 0:TOK], ACT.Sqrt, scale=1.0 / D, bias=EPS).then_inc(s_std, 1)
            for n in range(2):
                last_rows(U_OUT + 6 + n, n, rows1)
            act.wait_ge(s_scale2, 1)
            for k in range(KD):
                act.wait_ge(s_norm2, k + 1)
                act.activation(h2[:, k, :], h2[:, k, :], ACT.Identity, scale=scale2[:, k:k + 1],
                               bias=mod2[:, KD + k:KD + k + 1]).then_inc(s_h2, 1)

            for j in range(KF + 1):
                if j < KF:
                    if j >= 2:
                        act.wait_ge(s_conv, CONV_OPS * (j - 1))
                    act.wait_ge(s_up_used, j + 1)
                    act.activation(up_sb[:, j % 2, :], bank[(j % USLOTS) % 3][:, :], ACT.Copy).then_inc(s_upsb, 1)
                if j >= 1:
                    act.wait_ge(s_conv, CONV_OPS * j)
                    if j >= 3:
                        act.wait_ge(s_act, j)
                    act.activation(silu_sb[:, (j - 1) % 2, :], conv[:, (j - 1) % 2, 0:TOK], ACT.Silu).then_inc(s_silu, 1)

            preload_sqrt()
            for k in range(KD):
                act.wait_ge(s_x2, k + 1)
                if k >= 2:
                    act.wait_ge(s_sq_used, 2 * KD + k - 1)
                act.activation(squares[:, k % 2, 0:TOK], x_sb[:, k, :], ACT.Square).then_inc(s_sq, 1)
            act.wait_ge(s_sq_used, 3 * KD)
            act.activation(rstd[:, 0:TOK], bank[3][:, 0:TOK], ACT.Sqrt, scale=1.0 / D, bias=EPS).then_inc(s_std, 1)

        @block.vector
        def _(dve):
            count = [0]

            def mark(ins):
                count[0] += 1
                ins.then_inc(s_dve, 1)

            def settle():
                dve.wait_ge(s_dve, count[0])

            def tt(o, a, b, op):
                mark(dve.tensor_tensor(o, a, b, op))

            def ts(o, a, s1, s2, op0, op1=None):
                mark(dve.tensor_scalar(o, a, s1, s2, op0, op1) if op1 is not None else dve.tensor_scalar(o, a, s1, None, op0))

            def col(i):
                return small[:, i * DP:(i + 1) * DP]

            are, aim = a_raw[:, 0:DP], a_raw[:, DP:2 * DP]
            dt, re_dt, mag, phase, red, sin, sinh = (col(i) for i in range(7))
            t0, t1, t2, t3, k_re, k_im, den, turns = (col(i) for i in range(7, 15))

            def squares_of_both(k):
                if k >= 2:
                    dve.wait_ge(s_sq_used, k - 1)
                for src, off in ((ctx_sb, 0), (x_sb, TOK)):
                    dve.tensor_tensor(squares[:, k % 2, off:off + TOK], src[:, k, :], src[:, k, :], ALU.mult).then_inc(s_sq, 1)

            dve.wait_ge(s_ctx, 16)
            dve.wait_ge(s_x, 16)
            for k in range(3):
                squares_of_both(k)

            dve.wait_ge(s_raw, 16)
            dve.wait_ge(s_trig, 1)
            dve.tensor_tensor(re_dt, are, dt, ALU.mult).then_inc(s_trig_in, 1)
            tt(phase, aim, dt, ALU.mult)
            settle()
            ts(turns, phase, 1.0 / TWO_PI, None, ALU.mult)
            settle()
            ts(t0, turns, ROUND_MAGIC, ROUND_MAGIC, ALU.add, ALU.subtract)
            rest, parts = TWO_PI, []
            for _ in range(3):
                e = np.floor(np.log2(rest))
                part = np.floor(rest / 2.0 ** (e - 7)) * 2.0 ** (e - 7)
                parts.append(float(part))
                rest -= part
            parts.append(float(rest))
            cur = phase
            for i, part in enumerate(parts):
                settle()
                nxt = (t1, t2, t1, t2)[i]
                mark(dve.scalar_tensor_tensor(out=nxt, in0=t0, scalar=-part, in1=cur, op0=ALU.mult, op1=ALU.add))
                cur = nxt
            settle()
            dve.tensor_scalar(red, cur, float(np.float32(3.1415925)), float(np.float32(-3.1415925)), ALU.min, ALU.max).then_inc(s_trig_in, 1)
            for k in range(3, KD):
                squares_of_both(k)

            def cmul(o_re, o_im, a_re, a_im, b_re, b_im, s_a, s_b):
                tt(s_a, a_re, b_re, ALU.mult)
                tt(s_b, a_im, b_im, ALU.mult)
                settle()
                tt(o_re, s_a, s_b, ALU.subtract)
                settle()
                tt(s_a, a_re, b_im, ALU.mult)
                tt(s_b, a_im, b_re, ALU.mult)
                settle()
                tt(o_im, s_a, s_b, ALU.add)
                settle()

            p_re, p_im = power[:, 0], power[:, 1]
            sa = scratch[:, 0:DP * H].rearrange("p (c h) -> p c h", h=H)
            sb_ = scratch[:, DP * H:2 * DP * H].rearrange("p (c h) -> p c h", h=H)

            def over_h(a):
                return a.unsqueeze(2).broadcast_to([P, DP, H])

            def over_q_h(r, d):
                pw = power[:, r, 0:T, d * PAIRS:(d + 1) * PAIRS]
                if d == 0:
                    pw = pw[:, ::-1, :]
                return pw.rearrange("p e c -> p c e").unsqueeze(3)

            s_big = scratch[:, 0:PAIRS * T * H].rearrange("p (q t h) -> p q t h", q=PAIRS, t=T)

            def w_products(d, r):
                def pw(x):
                    return over_q_h(x, d).broadcast_to([P, PAIRS, T, H])

                def bb(x):
                    return b_bar[:, x, d * PAIRS:(d + 1) * PAIRS, :].unsqueeze(2).broadcast_to([P, PAIRS, T, H])

                tt(w_src[:, d, r], bb(0), pw(r), ALU.mult)
                tt(s_big, bb(1), pw(1 - r), ALU.mult)
                settle()

            def w_sum(d, r):
                dve.tensor_tensor(w_src[:, d, r], w_src[:, d, r], s_big, ALU.add if r else ALU.subtract).then_inc(s_wsrc, 1)
                dve.wait_ge(s_wsrc, 2 * d + r + 1)

            def discretise():
                dve.wait_ge(s_trig, 4)
                tt(t0, sinh, sinh, ALU.mult)
                settle()
                ts(t1, t0, -2.0, 1.0, ALU.mult, ALU.add)
                mark(dve.memset(power[:, 0, 0, :], 1.0))
                mark(dve.memset(power[:, 1, 0, :], 0.0))
                settle()
                p_re, p_im = power[:, 0], power[:, 1]
                tt(p_re[:, 1, :], mag, t1, ALU.mult)
                tt(p_im[:, 1, :], mag, sin, ALU.mult)
                tt(t2, are, are, ALU.mult)
                tt(t3, aim, aim, ALU.mult)
                settle()
                tt(den, t2, t3, ALU.add)
                ts(t0, p_re[:, 1, :], -1.0, None, ALU.add)
                settle()
                mark(dve.reciprocal(turns, den))
                tt(t1, t0, are, ALU.mult)
                tt(t2, p_im[:, 1, :], aim, ALU.mult)
                tt(t3, p_im[:, 1, :], are, ALU.mult)
                tt(phase, t0, aim, ALU.mult)
                settle()
                tt(t1, t1, t2, ALU.add)
                tt(t3, t3, phase, ALU.subtract)
                settle()
                tt(k_re, t1, turns, ALU.mult)
                tt(k_im, t3, turns, ALU.mult)
                settle()

                dve.wait_ge(s_braw, 16)
                cmul(b_bar[:, 0], b_bar[:, 1], over_h(k_re), over_h(k_im), b_raw[:, 0], b_raw[:, 1], sa, sb_)
                for lo, n in ((1, 1), (2, 2), (4, 4)):
                    def lead(r):
                        return power[:, r, lo, :].unsqueeze(1).broadcast_to([P, n, DP])
                    def rest_(r):
                        return power[:, r, 1:1 + n, :]
                    q_a = scratch[:, 0:n * DP].rearrange("p (e c) -> p e c", e=n)
                    q_b = scratch[:, 512:512 + n * DP].rearrange("p (e c) -> p e c", e=n)
                    cmul(power[:, 0, lo + 1:lo + 1 + n, :], power[:, 1, lo + 1:lo + 1 + n, :], lead(0), lead(1), rest_(0), rest_(1), q_a, q_b)

            dve.wait_ge(s_pk, 16)
            dve.wait_ge(s_std, 1)
            mark(dve.reciprocal(rstd[:, :], rstd[:, :]))
            settle()
            for k in range(KD):
                for src, off in ((ctx_sb, 0), (x_sb, TOK)):
                    dve.tensor_tensor(h_all[:, k, off:off + TOK], src[:, k, :], rstd[:, off:off + TOK], ALU.mult).then_inc(s_norm, 1)
                dve.wait_ge(s_pick, k + 1)
                dve.tensor_tensor(mod1[:, k], bank[4 + k % 4][:, 2 * P:2 * P + 4].rearrange("p (a v) -> p a v", v=2),
                                  par("b_ada")[:, k:k + KD + 1:KD].unsqueeze(2).broadcast_to([P, 2, 2]), ALU.add).then_inc(s_mod1, 1)
                dve.wait_ge(s_mod1, k + 1)
                dve.tensor_scalar(scale1[:, k, :], mod1[:, k, 1, :], 1.0, par("g_mix")[:, k:k + 1], ALU.add, ALU.mult).then_inc(s_scale1, 1)
                if k == 1:
                    discretise()
                elif k >= 2:
                    src = (k - 2) // 2
                    if k % 2 == 0:
                        w_products(src // 2, src % 2)
                    else:
                        w_sum(src // 2, src % 2)
            w_products(1, 1)
            w_sum(1, 1)
            dve.wait_ge(s_pad, 1)
            for g2 in range(2):
                rows = slice(g2 * N, (g2 + 1) * N)
                for r in range(2):
                    ins = dve.tensor_copy(b_pad[rows, r, :, g2, :], b_bar[rows, r])
                    if (g2, r) == (1, 1):
                        ins.then_inc(s_bpad, 1)
                    else:
                        mark(ins)


            for r in range(2):
                mark(dve.tensor_copy(power8[:, r, 0, :], power[:, r, T, :]))
            settle()
            for lo, n in ((1, 1), (2, 2), (4, 4)):
                q_a = merge_tmp[:, 0, 0:n * DP].rearrange("p (e c) -> p e c", e=n)
                q_b = merge_tmp[:, 1, 0:n * DP].rearrange("p (e c) -> p e c", e=n)
                lead = [power8[:, r, lo - 1, :].unsqueeze(1).broadcast_to([P, n, DP]) for r in range(2)]
                rest8 = [power8[:, r, 0:n, :] for r in range(2)]
                cmul(power8[:, 0, lo:lo + n, :], power8[:, 1, lo:lo + n, :], lead[0], lead[1], rest8[0], rest8[1], q_a, q_b)
            mark(dve.tensor_copy(cross[:, :, 0, :], power8[:, 1, 0:BLK, :]))
            ts(cross[:, :, 1, :], power8[:, 1, 0:BLK, :], -1.0, None, ALU.mult)

            dve.wait_ge(s_craw, 16)
            dve.wait_ge(s_tr, 16)
            E1 = T + 1
            c_big = scratch[:, 0:PAIRS * E1 * H].rearrange("p (q t h) -> p q t h", q=PAIRS, t=E1)
            for d in range(2):
                def pe_(r):
                    pw_ = power[:, r, :, d * PAIRS:(d + 1) * PAIRS]
                    if d == 1:
                        pw_ = pw_[:, ::-1, :]
                    return pw_.rearrange("p e c -> p c e").unsqueeze(3).broadcast_to([P, PAIRS, E1, H])

                def cc(r):
                    return c_raw[:, r, d * PAIRS:(d + 1) * PAIRS, :].unsqueeze(2).broadcast_to([P, PAIRS, E1, H])

                o_re, o_im = (ca[:, r, d * PAIRS:(d + 1) * PAIRS] for r in range(2))
                tt(o_re, cc(0), pe_(0), ALU.mult)
                tt(c_big, cc(1), pe_(1), ALU.mult)
                settle()
                tt(o_re, o_re, c_big, ALU.subtract)
                settle()
                tt(o_im, cc(0), pe_(1), ALU.mult)
                tt(c_big, cc(1), pe_(0), ALU.mult)
                settle()
                dve.scalar_tensor_tensor(out=o_im.rearrange("p q e h -> p (q e h)"), in0=o_im.rearrange("p q e h -> p (q e h)"), scalar=-1.0,
                                         in1=c_big.rearrange("p q e h -> p (q e h)"), op0=ALU.mult, op1=ALU.subtract).then_inc(s_ca, 1)
                dve.wait_ge(s_ca, d + 1)

            for c in range(2):
                dve.wait_ge(s_v, c + 1)
                stats, mean_var = bn[:, 6 * c:6 * c + 6], bn[:, 12 + 2 * c:14 + 2 * c]
                mark(dve.bn_stats(stats, v_tok[:, c, :]))
                settle()
                mark(dve.bn_aggr(mean_var, stats))
                settle()
                dve.tensor_scalar(bn[:, 16 + c:17 + c], mean_var[:, 1:2], EPS, None, ALU.add).then_inc(s_lnvar, 1)
            dve.wait_ge(s_lnstd, 2)
            mark(dve.reciprocal(bn[:, 18:20], bn[:, 18:20]))
            dve.wait_ge(s_ln, 64)
            for c in range(2):
                v = v_tok[:, c, :]
                settle()
                ts(v, v, bn[:, 12 + 2 * c:13 + 2 * c], bn[:, 18 + c:19 + c], ALU.subtract, ALU.mult)
                settle()
                v2 = v.rearrange("p (a n) -> p a n", a=2)
                tt(v2, v2, ln_sb[:, 0:2, :], ALU.mult)
                settle()
                dve.tensor_tensor(v2, v2, ln_sb[:, 2:4, :], ALU.add).then_inc(s_vn, 1)

            dve.wait_ge(s_uf, KS)
            dve.tensor_copy(u_x[:, :].rearrange("p (m c) -> p m c", c=CH), u_feat.rearrange("p m t c -> p (m t) c")[:, :, CH:2 * CH]).then_inc(s_ux, 1)

            dve.wait_ge(s_k_ps, 2)
            for job in range(1, 8, 2):
                dve.wait_ge(s_e_ps, job + 1)
                c0 = ((job // 2) % 2 * 2 + job // 4) * PAIRS + 8
                dve.tensor_copy(e_chunk[:, :, c0:c0 + 8].rearrange("p s c -> p c s"), bank[job % E_BANKS][:, :].rearrange("p (c s) -> p c s", c=8)).then_inc(s_ev, 1)
            dve.wait_ge(s_e, 4)
            dve.wait_ge(s_ev, 4)
            dve.wait_ge(s_sgu_ps, 2)
            blocks = e_chunk.rearrange("p (b j) (r c) -> p j b r c", j=BLK, r=2)
            wide = [P, BLK, 2, DP]
            t_s = wide_same.rearrange("p (b r c) -> p b r c", b=BLK, r=2)
            t_c = wide_cross.rearrange("p (b r c) -> p b r c", b=BLK, r=2)
            q1 = power8[:, 0, 0, :].unsqueeze(1).unsqueeze(1).broadcast_to(wide)
            x1 = cross[:, 0].unsqueeze(1).broadcast_to(wide)
            settle()
            for j in range(1, BLK):
                h = blocks[:, j - 1]
                tt(t_s, q1, h, ALU.mult)
                tt(t_c[:, :, ::-1, :], x1, h, ALU.mult)
                dve.wait_ge(s_dve, count[0] - 1)
                tt(blocks[:, j], blocks[:, j], t_s, ALU.add)
                settle()
                tt(blocks[:, j], blocks[:, j], t_c, ALU.add)
                settle()
            ends = blocks[:, BLK - 1]
            enter = entering.rearrange("p b (r c) -> p b r c", r=2)
            q8 = power8[:, 0, BLK - 1, :].unsqueeze(1).broadcast_to([P, 2, DP])
            n_s, n_c = t_s[:, 0], t_c[:, 0]
            mark(dve.tensor_copy(enter[:, 0], ends[:, 0]))
            settle()
            for b in range(1, BLK - 1):
                tt(n_s, q8, enter[:, b - 1], ALU.mult)
                tt(n_c[:, ::-1, :], cross[:, BLK - 1], enter[:, b - 1], ALU.mult)
                dve.wait_ge(s_dve, count[0] - 1)
                tt(enter[:, b], ends[:, b], n_s, ALU.add)
                settle()
                tt(enter[:, b], enter[:, b], n_c, ALU.add)
                settle()
            NJ = BLK - 1
            first = 2 * CH // BLK // 2
            carry4 = carry.rearrange("p (r c) s -> p r c s", r=2)
            qj = power8[:, 0, 0:NJ, :].rearrange("p j c -> p c j").unsqueeze(1).broadcast_to([P, 2, DP, NJ])
            xj = cross[:, 0:NJ].rearrange("p j r c -> p r c j")
            for b in range(CH // BLK):
                h_in = enter[:, first + b - 1].unsqueeze(3).broadcast_to([P, 2, DP, NJ])
                t_sj = wide_same[:, 0:NJ * 2 * DP].rearrange("p (r c j) -> p r c j", r=2, j=NJ)
                t_cj = wide_cross[:, 0:NJ * 2 * DP].rearrange("p (r c j) -> p r c j", r=2, j=NJ)
                local = e_chunk[:, (first + b) * BLK:(first + b) * BLK + NJ, :].rearrange("p j (r c) -> p r c j", r=2)
                by_dir = [(slice(0, PAIRS), carry4[:, :, 0:PAIRS, :]), (slice(PAIRS, DP), carry4[:, :, PAIRS:DP, ::-1])]
                for cols, c4 in by_dir:
                    mark(dve.tensor_copy(c4[:, :, :, b * BLK], enter[:, first + b - 1][:, :, cols]))
                settle()
                tt(t_sj, qj, h_in, ALU.mult)
                tt(t_cj[:, ::-1], xj, h_in, ALU.mult)
                settle()
                for cols, c4 in by_dir:
                    tt(c4[:, :, :, b * BLK + 1:(b + 1) * BLK], local[:, :, cols], t_sj[:, :, cols], ALU.add)
                settle()
                for cols, c4 in by_dir:
                    dst = c4[:, :, :, b * BLK + 1:(b + 1) * BLK]
                    ins = dve.tensor_tensor(dst, dst, t_cj[:, :, cols], ALU.add)
                    if b == CH // BLK - 1 and cols.stop == DP:
                        ins.then_inc(s_scan, 1)
                    else:
                        mark(ins)

            for j in range(4):
                dve.wait_ge(s_sgu_ps, j // 2 + 1)
                if j == 0:
                    dve.wait_ge(s_z, 2)
                t = merge_tmp[:, j % 2, :]
                tt(t.rearrange("p (c q) -> p c q", c=2), bank[6 + j // 2][:, (j % 2) * TOK:(j % 2 + 1) * TOK].rearrange("p (c q) -> p c q", c=2),
                   sgu_b_sb[:, j, :].unsqueeze(1).broadcast_to([P, 2, P]), ALU.add)
                settle()
                dve.tensor_tensor(y_b[:, j, :], z_u[:, j, :], t, ALU.mult).then_inc(s_yb, 1)
            dve.wait_ge(s_yb, 4)

            for b in range(2):
                dve.wait_ge(s_y_tr, b + 1)
                y_ps = bank[b][:, :].rearrange("p (t m c) -> p m t c", t=4, m=KS)
                for m in range(KS):
                    dve.scalar_tensor_tensor(out=y_feat[:, m, 4 * b:4 * b + 4], in0=u_x[:, m * TOK:(m + 1) * TOK].rearrange("p (t c) -> p t c", t=T)[:, 4 * b:4 * b + 4],
                                             scalar=par("s5_d")[:, m:m + 1], in1=y_ps[:, m], op0=ALU.mult, op1=ALU.add).then_inc(s_y, 1)

            dve.wait_ge(s_pick, KD + 2 * LOOPS)
            dve.tensor_tensor(mod2[:, 0:2 * KD], bank[3][:, 0:2 * KD], par("b_ada")[:, 2 * KD:4 * KD], ALU.add).then_inc(s_mod2, 1)

            for m in range(KS):
                dve.wait_ge(s_glu, m + 1)
                dve.tensor_tensor(y_a[:, m, :], y_gelu[:, m, :], glu_gate[:, m, :], ALU.mult).then_inc(s_ya, 1)

            dve.wait_ge(s_gate, 4 * LOOPS + 1)
            for m in range(KD):
                dve.wait_ge(*((s_unit, U_PROJ + m + 1) if m % 2 else (s_pr_ps, m // 2 + 1)))
                src = bank[PROJ_BANK[m % 4]]
                t = merge_tmp[:, 0, :], merge_tmp[:, 1, :]
                tt(t[0], src[:, 0:TOK], gates[:, m, :], ALU.mult)
                tt(t[1], src[:, TOK:2 * TOK], gates[:, KD + m, :], ALU.mult)
                settle()
                dve.tensor_tensor(merged[:, m, :], t[0], t[1], ALU.add).then_inc(s_mg, 1)
                dve.wait_ge(s_mg, m + 1)

            dve.wait_ge(s_xr, 16)
            dve.wait_ge(s_mod2, 1)
            for m in range(KD):
                if m == 4:
                    dve.wait_ge(s_pick, KD + LATER - 2)
                    dve.tensor_tensor(mod2[:, 2 * KD:3 * KD], bank[3][:, 2 * KD:3 * KD], par("b_ada")[:, 4 * KD:5 * KD],
                                      ALU.add).then_inc(s_mod2, 1)
                    dve.wait_ge(s_mod2, 2)
                    dve.scalar_tensor_tensor(out=scale2[:, :], in0=mod2[:, 2 * KD:3 * KD], scalar=1.0, in1=par("g_ffn"), op0=ALU.add,
                                             op1=ALU.mult).then_inc(s_scale2, 1)
                dve.wait_ge(s_unit, out_unit(m // 2) + 1)
                dve.scalar_tensor_tensor(out=x_sb[:, m, :], in0=bank[OUT_BANK[m // 2]][:, (m % 2) * TOK:(m % 2 + 1) * TOK], scalar=mod2[:, m:m + 1],
                                         in1=x_sb[:, m, :], op0=ALU.mult, op1=ALU.add).then_inc(s_x1, 1)
            dve.wait_ge(s_x1, KD)
            dve.wait_ge(s_std, 2)
            mark(dve.reciprocal(rstd[:, 0:TOK], rstd[:, 0:TOK]))
            settle()
            for k in range(KD):
                dve.tensor_tensor(h2[:, k, :], x_sb[:, k, :], rstd[:, 0:TOK], ALU.mult).then_inc(s_norm2, 1)

            dve.wait_ge(s_pick, KD + LATER)
            dve.tensor_tensor(mod2[:, 3 * KD:4 * KD], bank[3][:, 3 * KD:4 * KD], par("b_ada")[:, 5 * KD:6 * KD], ALU.add).then_inc(s_mod2, 1)
            dve.wait_ge(s_mod2, 3)

            taps = [(dy, dx) for dy in (-1, 0, 1) for dx in (-1, 0, 1) if (dy, dx) != (0, 0)]
            cw = par("conv_w").rearrange("p (m k) -> p m k", k=9)
            with dve.Fori(0, KF // 2) as i:
                for b in range(2):
                    base = i * (2 * CONV_OPS) + b * CONV_OPS
                    dve.wait_ge(s_upsb, i * 2 + (b + 2))
                    dve.wait_ge(s_act, i * 2 + (b + 1))
                    src = [up_sb[:, b, half * TOK:(half + 1) * TOK] for half in range(2)]
                    dst = [conv[:, b, half * TOK:(half + 1) * TOK] for half in range(2)]
                    tile = [bass.ds(i * 2 + (b + KF * half), 1) for half in range(2)]
                    for half in range(2):
                        dve.tensor_scalar(dst[half], src[half], cw[:, tile[half], 4], par("conv_b")[:, tile[half]],
                                          ALU.mult, ALU.add).then_inc(s_conv, 1)
                    done = 2
                    for dy, dx in taps:
                        r0, r1 = max(0, -dy), GRID_H - max(0, dy)
                        c0, c1 = max(0, -dx), GRID_W - max(0, dx)
                        for half in range(2):
                            o = dst[half].rearrange("p (r c) -> p r c", c=GRID_W)[:, r0:r1, c0:c1]
                            a = src[half].rearrange("p (r c) -> p r c", c=GRID_W)[:, r0 + dy:r1 + dy, c0 + dx:c1 + dx]
                            dve.wait_ge(s_conv, base + (done - 1))
                            dve.scalar_tensor_tensor(out=o, in0=a, scalar=cw[:, tile[half], (dy + 1) * 3 + dx + 1], in1=o, op0=ALU.mult,
                                                     op1=ALU.add).then_inc(s_conv, 1)
                            done += 1

            for m in range(KD):
                dve.wait_ge(s_dn_ps, m // 2 + 1)
                dve.scalar_tensor_tensor(out=x_sb[:, m, :], in0=bank[4 + m // 2][:, (m % 2) * TOK:(m % 2 + 1) * TOK],
                                         scalar=mod2[:, 3 * KD + m:3 * KD + m + 1], in1=x_sb[:, m, :], op0=ALU.mult, op1=ALU.add).then_inc(s_x2, 1)
            dve.wait_ge(s_x2, KD)
            dve.wait_ge(s_std, 3)
            mark(dve.reciprocal(rstd[:, 0:TOK], rstd[:, 0:TOK]))
            settle()
            for k in range(KD):
                dve.scalar_tensor_tensor(out=x_sb[:, k, :], in0=x_sb[:, k, :], scalar=par("g_final")[:, k:k + 1], in1=rstd[:, 0:TOK],
                                         op0=ALU.mult, op1=ALU.mult).then_inc(s_fin, 1)


_INS = [("x_t", [P, KD * TOK]), ("ctx_t", [P, KD * TOK]), ("pk", [P, PKW]), ("s5raw", [P, S5RAW]), ("log_step", [2, DP]),
        ("early_w", [6, P, UNIT]), ("ring_w", [UNITS, P, UNIT]), ("up_w", [3 * USLOTS, P, UNIT]), ("ln", [1, 4, TOK]), ("sgu_w", [P, 4, 2 * P]), ("sgu_b", [2, 4, P])]


def _tiles(w, m_per_unit):
    k, m = w.shape
    w = w.reshape(k // P, P, m // P // m_per_unit, m_per_unit, P)
    return w.transpose(2, 1, 3, 0, 4).reshape(m // P // m_per_unit, P, -1)


def _features(*vs):
    return [np.asarray(v).reshape(-1, P).T for v in vs]


def kernel(**inputs):
    import concourse.bacc as bacc
    from concourse.bass_utils import run_bass_kernel_spmd

    a = {k: np.asarray(v) for k, v in inputs.items()}
    w_in, w_ada, w_up = a["w_in"][0], a["w_ada"][0], a["w_up"][0]
    ada1 = _tiles(w_ada[:, :2 * D].reshape(D, 2, KD, P).transpose(0, 2, 1, 3).reshape(D, 2 * D), 2)
    ada = _tiles(w_ada[:, 2 * D:], 2)
    w_u, w_zu, w_v, w_gate = w_in[:, :512], w_in[:, 512:1024], w_in[:, 1024:1536], w_in[:, 1536:]
    gate = _tiles(w_gate, 2)
    v_units = w_v.reshape(2, 4, P, 512).transpose(0, 2, 1, 3).reshape(2, P, UNIT)
    loop = np.stack([ada[:8], gate], axis=1).reshape(4 * LOOPS, P, UNIT)
    pa, pb = _tiles(a["w_proj_a"][0], 2), _tiles(a["w_proj_b"][0], 2)
    proj = np.stack([ada[8:12], np.concatenate([pb, pa], axis=2)], axis=1).reshape(8, P, UNIT)
    w_out = _tiles(a["w_out"][0], 2)
    last = np.concatenate([ada[12:13], w_out[0:1], ada[13:14], w_out[1:4], ada[14:16]], axis=0)
    ring_w = np.concatenate([ada1[6:8], _tiles(w_u, 2), v_units, _tiles(w_zu, 2), loop, _tiles(a["s5_w_glu"][0], 4),
                             proj, last], axis=0)
    up = w_up.reshape(KD, P, 2, KF, P).transpose(3, 1, 2, 0, 4).reshape(KF, P, UNIT)
    down = a["w_down"][0].reshape(KF // 2, 2, P, D).transpose(0, 2, 1, 3).reshape(KF // 2, P, UNIT)
    conv_w = a["conv_w"][0].reshape(9, 2 * KF, P).transpose(2, 1, 0).reshape(P, -1)
    pick = np.tile(np.eye(CT, 2, dtype=np.float32), (NCT, 1))
    pk = np.concatenate(_features(a["c"][0], a["c_ctx"], a["b_ada"][0], a["g_mix"][0], a["g_ffn"][0], a["g_final"], a["b_gate"][0],
                                  a["s5_b_glu"][0], a["s5_d"][0], a["conv_b"][0]) + [pick, conv_w], axis=1)

    def per_state(v):
        v = v.reshape(2, PAIRS, 2, N, -1)
        return v.transpose(2, 3, 0, 1, 4).reshape(P, -1)

    c_re, c_im = (a[n][0].transpose(0, 1, 3, 2) for n in ("s5_c_re", "s5_c_im"))
    s5raw = np.concatenate([per_state(v) for v in (a["s5_a_re"][0], a["s5_a_im"][0], a["s5_b_re"][0], a["s5_b_im"][0], c_re, c_im)], axis=1)
    log_step = a["s5_log_step"][0].reshape(2, PAIRS, 2).transpose(2, 0, 1).reshape(2, DP)

    def tokens_t(v):
        return v.reshape(TOK, KD, P).transpose(2, 1, 0).reshape(P, -1)

    arrays = {
        "x_t": tokens_t(a["x"][0]), "ctx_t": tokens_t(a["ctx"][0]), "pk": pk, "s5raw": s5raw, "log_step": log_step,
        "early_w": ada1[:6], "ring_w": ring_w, "up_w": np.concatenate([up, down], axis=0),
        "ln": np.stack([a["sgu_ln_g"][0], a["sgu_ln_b"][0]]).reshape(1, 4, TOK), "sgu_w": a["sgu_w"][0].transpose(2, 0, 1).reshape(P, 4, 2 * P),
        "sgu_b": a["sgu_b"][0].reshape(4, 2, P).transpose(1, 0, 2),
    }
    arrays = {k: np.ascontiguousarray(v) for k, v in arrays.items()}
    nc = bacc.Bacc("TRN2", target_bir_lowering=False, num_devices=1)
    aps = [nc.dram_tensor(name, shape, F32, kind="ExternalInput").ap() for name, shape in _INS]
    out = nc.dram_tensor("out", [P, KD, TOK], F32, kind="ExternalOutput").ap()
    build(nc, *aps, out)
    r = run_bass_kernel_spmd(nc, [arrays], core_ids=[0])
    y = np.asarray(r.results[0]["out"])
    return np.ascontiguousarray(y.transpose(2, 1, 0).reshape(1, TOK, D))
```
